# Optimizing a Trainium2 kernel written in Bass

```python
import jax
import jax.numpy as jnp
from jax import lax
import numpy as np
import jax, jax.numpy as jnp

D_MODEL = 1024
BATCH = 1
SEQ = 512
DEPTH = 2

GRID_W = 64
CTX_LEN = 256
N_EVEN = (DEPTH + 1) // 2
N_ODD = DEPTH // 2

HEAD_DIM = 64
ATTN_HEADS = (D_MODEL // 2) // HEAD_DIM
ATTN_KV_HEADS = ATTN_HEADS // 4
ATTN_GROUP = ATTN_HEADS // ATTN_KV_HEADS
WINDOW = 128
ATTN_BLOCK = 128
ROPE_BASE = 10000.0

HGRN_EXPAND = 128
HGRN_WIDTH = D_MODEL // 2
HGRN_HEADS = HGRN_WIDTH // HGRN_EXPAND
HGRN_DK = HGRN_EXPAND
HGRN_DV = HGRN_EXPAND
CHUNK = 64

RET_HEADS = 4
RET_DK = D_MODEL // RET_HEADS
RET_DV = 2 * RET_DK
RET_BASE = 10000.0

FFN_HIDDEN = -(-8 * D_MODEL // (3 * 256)) * 256

A_Q = ATTN_HEADS * HEAD_DIM
A_KV = ATTN_KV_HEADS * HEAD_DIM
EVEN_PARTS = (('a_q', A_Q), ('a_k', A_KV), ('a_v', A_KV), ('b_q', HGRN_WIDTH), ('b_ff', HGRN_WIDTH),
              ('b_fb', HGRN_WIDTH), ('b_i', HGRN_WIDTH), ('b_g', HGRN_WIDTH))
EVEN_IN = A_Q + 2 * A_KV + 5 * HGRN_WIDTH
EVEN_OUT = A_Q + HGRN_HEADS * HGRN_DV
ODD_PARTS = (('q', RET_HEADS * RET_DK), ('k', RET_HEADS * RET_DK), ('v', RET_HEADS * RET_DV),
             ('g', RET_HEADS * RET_DV))
ODD_IN = 2 * RET_HEADS * RET_DK + 2 * RET_HEADS * RET_DV
ODD_OUT = RET_HEADS * RET_DV
EPS = 1e-6
F32 = jnp.float32


def _offsets(parts):
    out, start = {}, 0
    for name, width in parts:
        out[name] = (start, start + width)
        start += width
    return out

def split_parts(u, parts):
    return {n: u[..., s:e] for n, (s, e) in _offsets(parts).items()}

def project_parts(h, w, parts, names):
    off = _offsets(parts)
    return {n: h @ w[:, off[n][0]:off[n][1]] for n in names}

def rms_norm(x, g=None):
    xf = x.astype(F32)
    y = xf * lax.rsqrt(jnp.mean(xf * xf, axis=-1, keepdims=True) + EPS)
    if g is not None:
        y = y * g.astype(F32)
    return y.astype(x.dtype)

def modulate(h, shift, scale):
    return h * (1.0 + scale) + shift

def to_heads(u, n_heads):
    b, l, _ = u.shape
    return u.reshape(b, l, n_heads, -1).transpose(0, 2, 1, 3)

def from_heads(o):
    return o.transpose(0, 2, 1, 3)

def flip(a):
    return jnp.flip(a, axis=2)

def axial_rope_tables(n_tok):
    t = jnp.arange(n_tok)
    row = (t // GRID_W).astype(F32)
    col = (t % GRID_W).astype(F32)
    n_freq = HEAD_DIM // 4
    inv = ROPE_BASE ** (-jnp.arange(n_freq, dtype=F32) / n_freq)
    ang = jnp.concatenate([row[:, None] * inv, col[:, None] * inv], axis=-1)
    return jnp.cos(ang), jnp.sin(ang)

def retention_rope_tables(n_tok):
    theta = 1.0 / (RET_BASE ** jnp.linspace(0.0, 1.0, RET_DK // 2, dtype=F32))
    ang = jnp.arange(n_tok, dtype=F32)[:, None] * theta
    return jnp.cos(ang), jnp.sin(ang)

def apply_rope(x, cos, sin):
    half = x.shape[-1] // 2
    xf = x.astype(F32)
    x1, x2 = xf[..., :half], xf[..., half:]
    return jnp.concatenate([x1 * cos - x2 * sin, x2 * cos + x1 * sin], axis=-1).astype(x.dtype)

def attn_q_heads(u, g):
    b, l, _ = u.shape
    q = rms_norm(u.reshape(b, l, ATTN_KV_HEADS, ATTN_GROUP, HEAD_DIM), g)
    return q.transpose(0, 2, 3, 1, 4)

def kv_heads(u, g=None):
    b, l, _ = u.shape
    h = u.reshape(b, l, ATTN_KV_HEADS, HEAD_DIM)
    if g is not None:
        h = rms_norm(h, g)
    return h.transpose(0, 2, 1, 3)

def window_attention(q, k, v, k_ctx, v_ctx, sink):
    b, kv, g, l, d = q.shape
    n_blocks = l // ATTN_BLOCK
    span = ATTN_BLOCK + 2 * WINDOW
    pad = ((0, 0), (0, 0), (WINDOW, WINDOW), (0, 0))
    kp, vp = jnp.pad(k, pad), jnp.pad(v, pad)
    scale = d ** -0.5
    sink_col = jnp.broadcast_to(sink[None, :, :, None, None], (b, kv, g, ATTN_BLOCK, 1))

    def block(i):
        start = i * ATTN_BLOCK
        qb = lax.dynamic_slice_in_dim(q, start, ATTN_BLOCK, axis=3)
        kb = lax.dynamic_slice_in_dim(kp, start, span, axis=2)
        vb = lax.dynamic_slice_in_dim(vp, start, span, axis=2)
        q_pos = start + jnp.arange(ATTN_BLOCK)
        k_pos = start - WINDOW + jnp.arange(span)
        valid = ((jnp.abs(k_pos[None, :] - q_pos[:, None]) <= WINDOW)
                 & (k_pos >= 0)[None, :] & (k_pos < l)[None, :])
        s_lat = jnp.einsum('bkgqd,bksd->bkgqs', qb, kb, preferred_element_type=F32) * scale
        s_lat = jnp.where(valid, s_lat, -jnp.inf)
        s_ctx = jnp.einsum('bkgqd,bkcd->bkgqc', qb, k_ctx, preferred_element_type=F32) * scale
        p = jax.nn.softmax(jnp.concatenate([sink_col, s_lat, s_ctx], axis=-1), axis=-1)
        p_lat = p[..., 1:1 + span].astype(v.dtype)
        p_ctx = p[..., 1 + span:].astype(v.dtype)
        return (jnp.einsum('bkgqs,bksd->bkgqd', p_lat, vb)
                + jnp.einsum('bkgqc,bkcd->bkgqd', p_ctx, v_ctx))

    o = lax.map(block, jnp.arange(n_blocks))
    return o.transpose(1, 0, 4, 2, 3, 5).reshape(b, l, kv * g * d)

def context_attention(q, k, v, sink):
    b, kv, g, lc, d = q.shape
    s = jnp.einsum('bkgqd,bkcd->bkgqc', q, k, preferred_element_type=F32) * d ** -0.5
    sink_col = jnp.broadcast_to(sink[None, :, :, None, None], (b, kv, g, lc, 1))
    p = jax.nn.softmax(jnp.concatenate([sink_col, s], axis=-1), axis=-1)[..., 1:].astype(v.dtype)
    o = jnp.einsum('bkgqc,bkcd->bkgqd', p, v)
    return o.transpose(0, 3, 1, 2, 4).reshape(b, lc, kv * g * d)

def chunk_scan(q_in, k_in, v, decay, s0):
    xs = (jnp.moveaxis(q_in, 2, 0), jnp.moveaxis(k_in, 2, 0), jnp.moveaxis(v, 2, 0), decay)

    def step(s, inp):
        q_n, k_n, v_n, a_n = inp
        o_n = jnp.einsum('bhcd,bhde->bhce', q_n, s)
        s = a_n * s + jnp.einsum('bhcd,bhce->bhde', k_n, v_n)
        return s, o_n

    s, o = lax.scan(step, s0, xs)
    return jnp.moveaxis(o, 0, 2), s

def gla_chunked(q, k, v, log_f, s0):
    b, h, l, dk = q.shape
    dv = v.shape[-1]
    n = l // CHUNK
    qc, kc, lc = (a.reshape(b, h, n, CHUNK, dk) for a in (q, k, log_f))
    vc = v.reshape(b, h, n, CHUNK, dv)
    cum = jnp.cumsum(lc, axis=3)
    ref = cum[:, :, :, CHUNK // 2:CHUNK // 2 + 1]
    scores = jnp.einsum('bhntd,bhnsd->bhnts', qc * jnp.exp(cum - ref), kc * jnp.exp(ref - cum))
    lower = jnp.tril(jnp.ones((CHUNK, CHUNK), dtype=bool))
    o_intra = jnp.einsum('bhnts,bhnse->bhnte', jnp.where(lower, scores, 0.0), vc)
    cum_last = cum[:, :, :, -1:]
    decay = jnp.moveaxis(jnp.exp(cum_last[:, :, :, 0]), 2, 0)[..., None]
    o_inter, s = chunk_scan(qc * jnp.exp(cum), kc * jnp.exp(cum_last - cum), vc, decay, s0)
    return (o_intra + o_inter).reshape(b, h, l, dv), s

def gla_final_state(k, v, log_f):
    cum = jnp.cumsum(log_f, axis=2)
    return jnp.einsum('bhld,bhle->bhde', k * jnp.exp(cum[:, :, -1:] - cum), v)

def retention_chunked(q, k, v, log_gamma, s0):
    b, h, l, dk = q.shape
    dv = v.shape[-1]
    n = l // CHUNK
    qc = q.reshape(b, h, n, CHUNK, dk)
    kc = k.reshape(b, h, n, CHUNK, dk)
    vc = v.reshape(b, h, n, CHUNK, dv)
    pos = jnp.arange(CHUNK, dtype=F32)
    rel = pos[:, None] - pos[None, :]
    dmat = jnp.where(rel >= 0, jnp.exp(log_gamma[:, None, None] * jnp.maximum(rel, 0.0)), 0.0)
    scores = jnp.einsum('bhntd,bhnsd->bhnts', qc, kc) * dmat[None, :, None]
    o_intra = jnp.einsum('bhnts,bhnse->bhnte', scores, vc)
    lg = log_gamma[:, None]
    q_in = qc * jnp.exp(lg * (pos + 1.0))[None, :, None, :, None]
    k_in = kc * jnp.exp(lg * (CHUNK - 1.0 - pos))[None, :, None, :, None]
    decay = jnp.broadcast_to(jnp.exp(log_gamma * CHUNK)[None, None, :, None, None], (n, 1, h, 1, 1))
    o_inter, s = chunk_scan(q_in, k_in, vc, decay, s0)
    return (o_intra + o_inter).reshape(b, h, l, dv), s

def retention_final_state(k, v, log_gamma):
    lc = k.shape[2]
    w = jnp.exp(log_gamma[:, None] * (lc - 1.0 - jnp.arange(lc, dtype=F32)))
    return jnp.einsum('bhld,bhle->bhde', k * w[None, :, :, None], v)

def gated_head_norm(o, g_raw, gain=None):
    b, h, l, dv = o.shape
    y = rms_norm(from_heads(o), gain) * jax.nn.silu(g_raw.reshape(b, l, h, dv).astype(F32))
    return y.reshape(b, l, h * dv)

def even_mixer(h_ctx, h_lat, w_in, w_out, qk_g, sink, out_g, lb, cos, sin, need_ctx):
    dt = h_lat.dtype
    n_b = h_ctx.shape[0]
    sink = sink.astype(F32).reshape(ATTN_KV_HEADS, ATTN_GROUP)
    lb = lb.reshape(HGRN_HEADS, 1, HGRN_DK)
    p = split_parts(h_lat @ w_in, EVEN_PARTS)
    names = [n for n, _ in EVEN_PARTS] if need_ctx else ['a_k', 'a_v', 'b_ff', 'b_fb', 'b_i']
    pc = project_parts(h_ctx, w_in, EVEN_PARTS, names)

    def gates(f_raw):
        f = lb + (1.0 - lb) * jax.nn.sigmoid(to_heads(f_raw, HGRN_HEADS).astype(F32))
        return 1.0 - f, jnp.log(f)

    k_ctx = kv_heads(pc['a_k'], qk_g[1])
    v_ctx = kv_heads(pc['a_v'])
    q_lat = apply_rope(attn_q_heads(p['a_q'], qk_g[0]), cos, sin)
    k_lat = apply_rope(kv_heads(p['a_k'], qk_g[1]), cos, sin)
    a_lat = window_attention(q_lat, k_lat, kv_heads(p['a_v']), k_ctx, v_ctx, sink)

    k_fw_c, lf_fw_c = gates(pc['b_ff'])
    k_bw_c, lf_bw_c = gates(pc['b_fb'])
    i_c = to_heads(pc['b_i'], HGRN_HEADS).astype(F32)
    if need_ctx:
        zeros = jnp.zeros((n_b, HGRN_HEADS, HGRN_DK, HGRN_DV), F32)
        q_c = jax.nn.silu(to_heads(pc['b_q'], HGRN_HEADS).astype(F32))
        o_fw_c, s_fw = gla_chunked(q_c, k_fw_c, i_c, lf_fw_c, zeros)
        o_bw_c, s_bw = gla_chunked(flip(q_c), flip(k_bw_c), flip(i_c), flip(lf_bw_c), zeros)
    else:
        s_fw = gla_final_state(k_fw_c, i_c, lf_fw_c)
        s_bw = gla_final_state(flip(k_bw_c), flip(i_c), flip(lf_bw_c))
    k_fw, lf_fw = gates(p['b_ff'])
    k_bw, lf_bw = gates(p['b_fb'])
    q_l = jax.nn.silu(to_heads(p['b_q'], HGRN_HEADS).astype(F32))
    i_l = to_heads(p['b_i'], HGRN_HEADS).astype(F32)
    o_fw, _ = gla_chunked(q_l, k_fw, i_l, lf_fw, s_fw)
    o_bw, _ = gla_chunked(flip(q_l), flip(k_bw), flip(i_l), flip(lf_bw), s_bw)
    b_lat = gated_head_norm(o_fw + flip(o_bw), p['b_g'], out_g)

    y_lat = jnp.concatenate([a_lat.astype(dt), b_lat.astype(dt)], axis=-1) @ w_out
    if not need_ctx:
        return None, y_lat
    a_ctx = context_attention(attn_q_heads(pc['a_q'], qk_g[0]), k_ctx, v_ctx, sink)
    b_ctx = gated_head_norm(o_fw_c + flip(o_bw_c), pc['b_g'], out_g)
    y_ctx = jnp.concatenate([a_ctx.astype(dt), b_ctx.astype(dt)], axis=-1) @ w_out
    return y_ctx, y_lat

def odd_mixer(h_ctx, h_lat, w_in, w_out, cos, sin, need_ctx):
    dt = h_lat.dtype
    n_b = h_ctx.shape[0]
    log_g_fw = jnp.log(1.0 - 2.0 ** (-5.0 - jnp.arange(RET_HEADS, dtype=F32)))
    log_g_bw = log_g_fw[::-1]
    k_scale = RET_DK ** -0.5
    p = split_parts(h_lat @ w_in, ODD_PARTS)
    names = [n for n, _ in ODD_PARTS] if need_ctx else ['k', 'v']
    pc = project_parts(h_ctx, w_in, ODD_PARTS, names)

    k_c = to_heads(pc['k'], RET_HEADS).astype(F32) * k_scale
    v_c = to_heads(pc['v'], RET_HEADS).astype(F32)
    if need_ctx:
        zeros = jnp.zeros((n_b, RET_HEADS, RET_DK, RET_DV), F32)
        q_c = to_heads(pc['q'], RET_HEADS).astype(F32)
        o_fw_c, s_fw = retention_chunked(q_c, k_c, v_c, log_g_fw, zeros)
        o_bw_c, s_bw = retention_chunked(flip(q_c), flip(k_c), flip(v_c), log_g_bw, zeros)
    else:
        s_fw = retention_final_state(k_c, v_c, log_g_fw)
        s_bw = retention_final_state(flip(k_c), flip(v_c), log_g_bw)

    q_l = apply_rope(to_heads(p['q'], RET_HEADS).astype(F32), cos, sin)
    k_l = apply_rope(to_heads(p['k'], RET_HEADS).astype(F32), cos, sin) * k_scale
    v_l = to_heads(p['v'], RET_HEADS).astype(F32)
    o_fw, _ = retention_chunked(q_l, k_l, v_l, log_g_fw, s_fw)
    o_bw, _ = retention_chunked(flip(q_l), flip(k_l), flip(v_l), log_g_bw, s_bw)
    y_lat = gated_head_norm(o_fw + flip(o_bw), p['g']).astype(dt) @ w_out
    if not need_ctx:
        return None, y_lat
    y_ctx = gated_head_norm(o_fw_c + flip(o_bw_c), pc['g']).astype(dt) @ w_out
    return y_ctx, y_lat

def swiglu(h, w_in, w_out):
    gate, up = jnp.split(h @ w_in, 2, axis=-1)
    return (jax.nn.silu(gate) * up) @ w_out

def first_inputs(seed: int = 0) -> dict:
    key = jax.random.key(seed)
    ks = jax.random.split(key, 17)
    d = D_MODEL

    def nrm(k, shape, scale):
        return jax.random.normal(k, shape, F32) * scale

    return {
        'x': nrm(ks[0], (BATCH, SEQ, d), 1.0),
        'c': nrm(ks[1], (BATCH, d), 1.0),
        'ctx': nrm(ks[2], (BATCH, CTX_LEN, d), 1.0),
        'c_ctx': nrm(ks[3], (d,), 1.0),
        'mod_w': nrm(ks[4], (DEPTH, d, 6 * d), 0.5 * d ** -0.5),
        'mod_b': nrm(ks[5], (DEPTH, 6 * d), 0.02),
        'norm_g': 1.0 + nrm(ks[6], (DEPTH, 2, d), 0.02),
        'ffn_w_in': nrm(ks[7], (DEPTH, d, 2 * FFN_HIDDEN), d ** -0.5),
        'ffn_w_out': nrm(ks[8], (DEPTH, FFN_HIDDEN, d), FFN_HIDDEN ** -0.5),
        'even_w_in': nrm(ks[9], (N_EVEN, d, EVEN_IN), d ** -0.5),
        'even_w_out': nrm(ks[10], (N_EVEN, EVEN_OUT, d), EVEN_OUT ** -0.5),
        'attn_qk_norm_g': 1.0 + nrm(ks[11], (N_EVEN, 2, HEAD_DIM), 0.02),
        'attn_sink': nrm(ks[12], (N_EVEN, ATTN_HEADS), 0.5),
        'hgrn_out_norm_g': 1.0 + nrm(ks[13], (N_EVEN, HGRN_DV), 0.02),
        'hgrn_lb': nrm(ks[14], (N_EVEN + 1, HGRN_WIDTH), 0.1),
        'odd_w_in': nrm(ks[15], (N_ODD, d, ODD_IN), d ** -0.5),
        'odd_w_out': nrm(ks[16], (N_ODD, ODD_OUT, d), ODD_OUT ** -0.5),
    }

def first_block(x, c, ctx, c_ctx, mod_w, mod_b, norm_g, ffn_w_in, ffn_w_out, even_w_in, even_w_out,
              attn_qk_norm_g, attn_sink, hgrn_out_norm_g, hgrn_lb, odd_w_in, odd_w_out):
    n_tok = x.shape[1]
    rope_cos, rope_sin = axial_rope_tables(n_tok)
    ret_cos, ret_sin = retention_rope_tables(n_tok)
    lower_bounds = jnp.cumsum(jax.nn.softmax(hgrn_lb.astype(F32), axis=0), axis=0)
    cond_lat = jax.nn.silu(c)
    cond_ctx = jax.nn.silu(c_ctx)
    for layer in range(DEPTH):
        last = layer == DEPTH - 1
        j = layer // 2
        m_lat = jnp.split((cond_lat @ mod_w[layer] + mod_b[layer])[:, None, :], 6, axis=-1)
        m_ctx = jnp.split((cond_ctx @ mod_w[layer] + mod_b[layer])[None, None, :], 6, axis=-1)
        h_lat = modulate(rms_norm(x, norm_g[layer, 0]), m_lat[0], m_lat[1])
        h_ctx = modulate(rms_norm(ctx, norm_g[layer, 0]), m_ctx[0], m_ctx[1])
        if layer % 2 == 0:
            y_ctx, y_lat = even_mixer(h_ctx, h_lat, even_w_in[j], even_w_out[j], attn_qk_norm_g[j],
                                      attn_sink[j], hgrn_out_norm_g[j], lower_bounds[j],
                                      rope_cos, rope_sin, not last)
        else:
            y_ctx, y_lat = odd_mixer(h_ctx, h_lat, odd_w_in[j], odd_w_out[j], ret_cos, ret_sin, not last)
        x = x + m_lat[2] * y_lat
        x = x + m_lat[5] * swiglu(modulate(rms_norm(x, norm_g[layer, 1]), m_lat[3], m_lat[4]),
                                  ffn_w_in[layer], ffn_w_out[layer])
        if not last:
            ctx = ctx + m_ctx[2] * y_ctx
            ctx = ctx + m_ctx[5] * swiglu(modulate(rms_norm(ctx, norm_g[layer, 1]), m_ctx[3], m_ctx[4]),
                                          ffn_w_in[layer], ffn_w_out[layer])
    return x


DEPTH_2 = 1

DN_HEADS = 8
DN_DK = 128
DN_DV = 128
DN_QK_WIDTH = DN_HEADS * DN_DK
DN_WIDTH = DN_HEADS * DN_DV
CONV_K = 4
DIL_CONFIGS = ((128, 1), (512, 4), (2048, 16))
HEADS_PER_GROUP = 4
ATTN_HEADS_2 = HEADS_PER_GROUP * len(DIL_CONFIGS)
ATTN_HEAD_DIM = 64
ATTN_WIDTH = ATTN_HEADS_2 * ATTN_HEAD_DIM
IN_SPLITS = (DN_QK_WIDTH, DN_QK_WIDTH, DN_WIDTH, DN_WIDTH, DN_HEADS, DN_HEADS,
             ATTN_WIDTH, ATTN_WIDTH, ATTN_WIDTH, ATTN_WIDTH, D_MODEL, D_MODEL)
N_IN = sum(IN_SPLITS)


def rms_norm_2(x, w):
    xf = x.astype(jnp.float32)
    y = xf * lax.rsqrt(jnp.mean(xf * xf, axis=-1, keepdims=True) + EPS)
    return (y * w.astype(jnp.float32)).astype(x.dtype)

def l2_normalize(x):
    xf = x.astype(jnp.float32)
    return xf * lax.rsqrt(jnp.sum(xf * xf, axis=-1, keepdims=True) + EPS)

def causal_dwconv_silu(x, w):
    k_w = w.shape[0]
    s = x.shape[1]
    xp = jnp.pad(x, ((0, 0), (k_w - 1, 0), (0, 0)))
    y = sum(xp[:, j:j + s] * w[j] for j in range(k_w))
    return jax.nn.silu(y)

def gated_delta_rule(q, k, v, g, beta):
    b, s, h, dk = q.shape
    n = s // CHUNK

    def to_chunks(t):
        return jnp.moveaxis(t.reshape((b, n, CHUNK) + t.shape[2:]), 3, 2)

    q, k, v, g, beta = map(to_chunks, (q * dk ** -0.5, k, v, g, beta))
    gc = jnp.cumsum(g, axis=-1)
    causal = jnp.tril(jnp.ones((CHUNK, CHUNK), dtype=bool))
    strict = jnp.tril(jnp.ones((CHUNK, CHUNK), dtype=bool), -1)
    decay = jnp.exp(jnp.where(causal, gc[..., :, None] - gc[..., None, :], -jnp.inf))
    k_beta = k * beta[..., None]
    v_beta = v * beta[..., None]
    lmat = jnp.where(strict, jnp.einsum('bnhcd,bnhed->bnhce', k_beta, k) * decay, 0.0)
    eye = jnp.eye(CHUNK, dtype=jnp.float32)
    t_inv = lax.linalg.triangular_solve(eye + lmat, jnp.broadcast_to(eye, lmat.shape),
                                        left_side=True, lower=True, unit_diagonal=True)
    u = jnp.einsum('bnhce,bnhed->bnhcd', t_inv, v_beta)
    w = jnp.einsum('bnhce,bnhed->bnhcd', t_inv, k_beta * jnp.exp(gc)[..., None])
    a_qk = jnp.einsum('bnhcd,bnhed->bnhce', q, k) * decay
    q_dec = q * jnp.exp(gc)[..., None]
    k_dec = k * jnp.exp(gc[..., -1:] - gc)[..., None]
    g_last = jnp.exp(gc[..., -1])

    def step(state, xs):
        q_c, k_c, u_c, w_c, a_c, gl = xs
        v_new = u_c - jnp.einsum('bhcd,bhde->bhce', w_c, state)
        o_c = jnp.einsum('bhcd,bhde->bhce', q_c, state) + jnp.einsum('bhce,bhed->bhcd', a_c, v_new)
        state = state * gl[..., None, None] + jnp.einsum('bhcd,bhce->bhde', k_c, v_new)
        return state, o_c

    xs = tuple(jnp.moveaxis(t, 1, 0) for t in (q_dec, k_dec, u, w, a_qk, g_last))
    state0 = jnp.zeros((b, h, dk, v.shape[-1]), jnp.float32)
    _, o = lax.scan(step, state0, xs)
    o = jnp.moveaxis(jnp.moveaxis(o, 0, 1), 2, 3)
    return o.reshape(b, s, h, -1)

def dilated_window_attention(q, k, v, window, dilation):
    b, s, h, dh = q.shape
    n_back = window // dilation
    sub_len = s // dilation
    nb = -(-sub_len // ATTN_BLOCK)
    lp = nb * ATTN_BLOCK
    bb = b * dilation

    def to_sub(t):
        t = t.reshape(b, sub_len, dilation, h, dh).transpose(0, 2, 1, 3, 4).reshape(bb, sub_len, h, dh)
        return jnp.pad(t, ((0, 0), (0, lp - sub_len), (0, 0), (0, 0)))

    def band(t):
        tp = jnp.pad(t, ((0, 0), (ATTN_BLOCK, 0), (0, 0), (0, 0))).reshape(bb, nb + 1, ATTN_BLOCK, h, dh)
        return jnp.concatenate([tp[:, :-1], tp[:, 1:]], axis=2)

    qb = to_sub(q).reshape(bb, nb, ATTN_BLOCK, h, dh)
    kb = band(to_sub(k))
    vb = band(to_sub(v))
    scores = jnp.einsum('bnqhd,bnkhd->bnhqk', qb, kb,
                        preferred_element_type=jnp.float32) * (dh ** -0.5)
    blk = jnp.arange(nb)[:, None, None]
    qpos = blk * ATTN_BLOCK + jnp.arange(ATTN_BLOCK)[None, :, None]
    kpos = (blk - 1) * ATTN_BLOCK + jnp.arange(2 * ATTN_BLOCK)[None, None, :]
    dist = qpos - kpos
    mask = (dist >= 0) & (dist <= n_back) & (kpos >= 0)
    scores = jnp.where(mask[None, :, None], scores, -jnp.inf)
    m = jnp.max(scores, axis=-1, keepdims=True)
    p = jnp.exp(scores - m)
    denom = jnp.sum(p, axis=-1, keepdims=True)
    o = jnp.einsum('bnhqk,bnkhd->bnqhd', (p / denom).astype(v.dtype), vb)
    lse = (m + jnp.log(denom))[..., 0]
    o = o.reshape(bb, lp, h, dh)[:, :sub_len]
    o = o.reshape(b, dilation, sub_len, h, dh).transpose(0, 2, 1, 3, 4).reshape(b, s, h, dh)
    lse = lse.transpose(0, 1, 3, 2).reshape(bb, lp, h)[:, :sub_len]
    lse = lse.reshape(b, dilation, sub_len, h).transpose(0, 2, 1, 3).reshape(b, s, h)
    return o, lse

def second_inputs(seed: int = 0) -> dict:
    key = jax.random.key(seed)
    ks = jax.random.split(key, 16)
    f32 = jnp.float32
    d = D_MODEL
    x = jax.random.normal(ks[0], (BATCH, SEQ, d), f32)
    c = jax.random.normal(ks[1], (BATCH, d), f32)
    norm_w = 1.0 + 0.02 * jax.random.normal(ks[2], (DEPTH_2, d), f32)
    ada_w = jax.random.normal(ks[3], (DEPTH_2, d, 3 * d), f32) * d ** -0.5
    ada_b = 0.01 * jax.random.normal(ks[4], (DEPTH_2, 3 * d), f32)
    w_in = jax.random.normal(ks[5], (DEPTH_2, d, N_IN), f32) * d ** -0.5
    conv_w = jax.random.normal(ks[6], (DEPTH_2, CONV_K, 2 * DN_QK_WIDTH + DN_WIDTH), f32) * CONV_K ** -0.5
    a_log = jnp.log(jax.random.uniform(ks[7], (DEPTH_2, DN_HEADS), f32, 1.0, 16.0))
    dt = jnp.exp(jax.random.uniform(ks[8], (DEPTH_2, DN_HEADS), f32, np.log(1e-3), np.log(1e-1)))
    dt_bias = dt + jnp.log(-jnp.expm1(-dt))
    dn_norm_w = 1.0 + 0.02 * jax.random.normal(ks[9], (DEPTH_2, DN_DV), f32)
    w_proj_a = jax.random.normal(ks[10], (DEPTH_2, DN_WIDTH, d), f32) * DN_WIDTH ** -0.5
    w_proj_b = jax.random.normal(ks[11], (DEPTH_2, ATTN_WIDTH, d), f32) * ATTN_WIDTH ** -0.5
    w_out = jax.random.normal(ks[12], (DEPTH_2, d, d), f32) * d ** -0.5
    final_norm_w = 1.0 + 0.02 * jax.random.normal(ks[13], (d,), f32)
    return {"x": x, "c": c, "norm_w": norm_w, "ada_w": ada_w, "ada_b": ada_b, "w_in": w_in,
            "conv_w": conv_w, "a_log": a_log, "dt_bias": dt_bias, "dn_norm_w": dn_norm_w,
            "w_proj_a": w_proj_a, "w_proj_b": w_proj_b, "w_out": w_out, "final_norm_w": final_norm_w}

def second_block(x, c, norm_w, ada_w, ada_b, w_in, conv_w, a_log, dt_bias, dn_norm_w,
              w_proj_a, w_proj_b, w_out, final_norm_w):
    b, s, _ = x.shape
    split_points = [int(p) for p in np.cumsum(IN_SPLITS)[:-1]]
    for l in range(DEPTH_2):
        mod = jax.nn.silu(c) @ ada_w[l] + ada_b[l]
        shift, scale, gate = jnp.split(mod, 3, axis=-1)
        h = rms_norm_2(x, norm_w[l]) * (1.0 + scale[:, None]) + shift[:, None]
        proj = h @ w_in[l]
        (qa, ka, va, za, beta_in, a_in, qb, kb, vb, zb, ga, gb) = jnp.split(proj, split_points, axis=-1)

        qkv = causal_dwconv_silu(jnp.concatenate([qa, ka, va], axis=-1), conv_w[l])
        qa, ka, va = jnp.split(qkv, [DN_QK_WIDTH, 2 * DN_QK_WIDTH], axis=-1)
        q_dn = l2_normalize(qa.reshape(b, s, DN_HEADS, DN_DK))
        k_dn = l2_normalize(ka.reshape(b, s, DN_HEADS, DN_DK))
        v_dn = va.reshape(b, s, DN_HEADS, DN_DV).astype(jnp.float32)
        beta = jax.nn.sigmoid(beta_in.astype(jnp.float32))
        g = -jnp.exp(a_log[l].astype(jnp.float32)) * jax.nn.softplus(
            a_in.astype(jnp.float32) + dt_bias[l].astype(jnp.float32))
        o_a = gated_delta_rule(q_dn, k_dn, v_dn, g, beta).astype(x.dtype)
        y_a = rms_norm_2(o_a, dn_norm_w[l]).reshape(b, s, DN_WIDTH) * jax.nn.silu(za)
        y_a = y_a @ w_proj_a[l]

        qb = qb.reshape(b, s, ATTN_HEADS_2, ATTN_HEAD_DIM)
        kb = kb.reshape(b, s, ATTN_HEADS_2, ATTN_HEAD_DIM)
        vb = vb.reshape(b, s, ATTN_HEADS_2, ATTN_HEAD_DIM)
        outs, lses = [], []
        for gi, (win, dil) in enumerate(DIL_CONFIGS):
            hs = slice(gi * HEADS_PER_GROUP, (gi + 1) * HEADS_PER_GROUP)
            o_g, lse_g = dilated_window_attention(qb[:, :, hs], kb[:, :, hs], vb[:, :, hs], win, dil)
            outs.append(o_g)
            lses.append(lse_g)
        o_b = jnp.stack(outs, axis=2)
        w_g = jax.nn.softmax(jnp.stack(lses, axis=2), axis=2)
        y_b = (o_b * w_g[..., None].astype(o_b.dtype)).reshape(b, s, ATTN_WIDTH) * jax.nn.silu(zb)
        y_b = y_b @ w_proj_b[l]

        merged = jax.nn.sigmoid(ga) * y_a + jax.nn.sigmoid(gb) * y_b
        x = x + gate[:, None] * (merged @ w_out[l])
    return rms_norm_2(x, final_norm_w)


def setup_inputs(seed=0):
    out = dict(first_inputs(seed))
    for name, value in second_inputs(seed + 1).items():
        if name != "x":
            out[name + "_2"] = value
    return out


def reference(
    x, c, ctx, c_ctx, mod_w, mod_b, norm_g, ffn_w_in, ffn_w_out, even_w_in, even_w_out,
    attn_qk_norm_g, attn_sink, hgrn_out_norm_g, hgrn_lb, odd_w_in, odd_w_out, c_2, norm_w_2,
    ada_w_2, ada_b_2, w_in_2, conv_w_2, a_log_2, dt_bias_2, dn_norm_w_2, w_proj_a_2, w_proj_b_2,
    w_out_2, final_norm_w_2,
):
    x = first_block(
        x, c, ctx, c_ctx, mod_w, mod_b, norm_g, ffn_w_in, ffn_w_out, even_w_in, even_w_out,
        attn_qk_norm_g, attn_sink, hgrn_out_norm_g, hgrn_lb, odd_w_in, odd_w_out,
    )
    return second_block(
        x, c_2, norm_w_2, ada_w_2, ada_b_2, w_in_2, conv_w_2, a_log_2, dt_bias_2, dn_norm_w_2,
        w_proj_a_2, w_proj_b_2, w_out_2, final_norm_w_2,
    )


_drawn_inputs = setup_inputs


def setup_inputs(seed=0):
    import zlib

    import numpy as np

    out = dict(_drawn_inputs(seed))
    spreads = {}
    factors = {'norm_g': 4.55,
     'attn_qk_norm_g': 8.0,
     'attn_sink': 8.0,
     'hgrn_out_norm_g': 8.0,
     'hgrn_lb': 8.0,
     'norm_w_2': 7.304,
     'ada_b_2': 8.0,
     'a_log_2': 2.966,
     'dn_norm_w_2': 8.0,
     'final_norm_w_2': 2.786}
    for name, (base, spread) in spreads.items():
        noise = np.random.default_rng([zlib.crc32(name.encode()), seed]).standard_normal(out[name].shape)
        drawn = base * np.exp(spread * noise) if base else spread * noise
        out[name] = jnp.asarray(drawn.astype(out[name].dtype))
    for name, factor in factors.items():
        out[name] = (out[name] * factor).astype(out[name].dtype)
    return out
```

```python
from contextlib import ExitStack

import numpy as np

import concourse.bass as bass
from concourse import mybir

F32 = mybir.dt.float32
F32R = mybir.dt.float32r
U32 = mybir.dt.uint32
ALU = mybir.AluOpType
ACT = mybir.ActivationFunctionType
AX_X = mybir.AxisListType.X

P = 128
D = 1024
DC = D // P
LAT, CTX = 512, 256
TOK = LAT + CTX
EPS = 1e-6
FFN = 2816
HALF = FFN // P // 2
SLOT = 2048
RET_H = 4
GLA_H = 4
DN_H = 8
NEG = -1e30


def constants():
    f = np.float32
    p = np.arange(P)
    out = {}
    out["ident"] = np.eye(P, dtype=f)
    out["ones"] = np.ones((P, P), f)
    out["ones64"] = np.kron(np.eye(2), np.ones((64, 64))).astype(f)
    rot = np.zeros((P, P), f)
    for b in (0, 64):
        for i in range(32):
            rot[b + i, b + 32 + i] = -1.0
            rot[b + 32 + i, b + i] = 1.0
    out["rotT"] = np.ascontiguousarray(rot.T)
    out["upper"] = (p[:, None] <= p[None, :]).astype(f)
    tok = np.arange(LAT)
    inv = f(10000.0) ** (-np.arange(16, dtype=f) / f(16))
    ang = np.concatenate([(tok // 64).astype(f)[:, None] * inv, (tok % 64).astype(f)[:, None] * inv], axis=-1)
    out["axial"] = np.stack([np.tile(np.cos(ang).T, (4, 1)), np.tile(np.sin(ang).T, (4, 1))], 1).astype(f)
    theta = f(1.0) / (f(10000.0) ** np.linspace(0.0, 1.0, P, dtype=f))
    ang = tok.astype(f)[:, None] * theta
    out["retrope"] = np.stack([np.cos(ang).T, np.sin(ang).T], 1).astype(f)
    q, k = p[:, None], np.arange(3 * P)[None, :]
    win = np.where((k >= q) & (k <= q + 2 * P), 0.0, NEG)
    four = np.stack([win] * 4, 1)
    four[:, 0, :P] = NEG
    four[:, 3, 2 * P:] = NEG
    out["window"] = four.astype(f)
    s, t = (p % 64)[:, None], np.arange(64)[None, :]
    out["tri64"] = np.stack([s <= t, s >= t], 1).astype(f)
    m = np.ones((2, TOK), f)
    m[0, np.arange(TOK) % 64 == 0] = 0.0
    m[1, np.arange(TOK) % 64 == 63] = 0.0
    out["restart"] = np.broadcast_to(m[None], (P, 2, TOK)).copy()
    g = np.log(1.0 - 2.0 ** (-5.0 - np.arange(RET_H, dtype=np.float64)))
    lat_u = (np.arange(7 * P) - 3 * P)[None, :] - p[:, None]
    ctx_u = (np.arange(5 * P) + P)[None, :] - p[:, None]
    tables = []
    for h in range(RET_H):
        fw, bw = g[h], g[RET_H - 1 - h]
        lat = np.where(lat_u >= 0, np.exp(fw * np.maximum(lat_u, 0)), 0.0)
        lat = lat + np.where(lat_u <= 0, np.exp(bw * np.maximum(-lat_u, 0)), 0.0)
        tables.append(np.concatenate([lat, np.exp(fw * ctx_u) + np.exp(bw * (LAT + CTX - ctx_u))], 1))
    out["decay"] = (np.stack(tables) * 256.0 ** -0.5).astype(f)
    lev = [((p[:, None] // (2 * b) == p[None, :] // (2 * b)) & (p[:, None] // b % 2 == 1)
            & (p[None, :] // b % 2 == 0)) for b in (1, 2, 4, 8, 16, 32, 64)]
    out["levels"] = np.stack(lev, 1).astype(f)
    k = np.arange(2 * P)[None, :]
    near = np.where((k >= q) & (k <= q + P), 0.0, NEG)
    first = np.where((k >= P) & (k <= q + P), 0.0, NEG)
    k = np.arange(P)[None, :]
    dil4 = np.where(k <= q, 0.0, NEG)
    dil16 = np.where((k <= q) & (k % 4 == q % 4), 0.0, NEG)
    out["near"] = np.stack([first, near, near, near], 1).astype(f)
    out["dil"] = np.stack([dil4, dil16], 1).astype(f)
    pair = np.zeros((P, 2, P), f)
    for s in range(4):
        pair[s, s // 2, (s % 2) * 64:(s % 2) * 64 + 64] = 1.0
    out["pair"] = pair
    return out


SMALL = {}
_at = 0
for _name, _width in (("mod_b", 96), ("ada_b", 24), ("norm_g", 32), ("norm_w", 8), ("final_w", 8),
                      ("qk_g", 2), ("sink", 8), ("lb", 8), ("hgrn_g", 1), ("conv", 96), ("a_log", 8),
                      ("dt_bias", 8), ("dn_w", 1), ("cond", 16), ("cond_2", 8), ("eps", 1)):
    SMALL[_name] = (_at, _at + _width)
    _at += _width
SMALLS = _at

STREAM = [("mod", 60, 8, 256), ("aq", 2, 8, 256), ("akv", 1, 8, 256), ("bq", 2, 8, 256), ("bg", 2, 8, 256),
          ("bf", 4, 8, 256), ("bi", 2, 8, 256), ("eo", 4, 8, 256)]
STREAM += [(f"f0{part}{half}", *shape) for half in (0, 1)
           for part, shape in (("i", (HALF, 8, 256)), ("o", (8, HALF, 128)))]
STREAM += [("ckv0", 4, 8, 256), ("ckv1", 8, 8, 256), ("rqk", 8, 8, 256), ("rv", 8, 8, 256),
           ("rg", 8, 8, 256), ("ro", 8, 16, 128)]
STREAM += [(f"f1{part}{half}", *shape) for half in (0, 1)
           for part, shape in (("i", (HALF, 8, 256)), ("o", (8, HALF, 128)))]
STREAM += [("dqkv", 12, 8, 256), ("dba", 1, 8, 16), ("dz", 4, 8, 256), ("pa", 4, 8, 256), ("ga", 4, 8, 256),
           ("tqk", 6, 8, 256), ("tv", 3, 8, 256), ("tz", 3, 8, 256), ("pb", 4, 6, 256), ("gb", 4, 8, 256),
           ("wo", 4, 8, 256)]
SHARED = {"ckv0": ("rqk", 4), "ckv1": ("rv", 0)}


class Ring:

    def __init__(self, plan):
        self.plan = plan
        self.tile = 0
        self.issued = 0
        self.split = 0
        self.unit = 8


class Map:

    def __init__(self, first, end):
        self.free = [(first, end)]

    def take(self, size):
        for n, (a, b) in enumerate(self.free):
            if b - a >= size:
                self.free[n:n + 1] = [(a + size, b)] if b - a > size else []
                return a
        raise ValueError(f"no room for {size} bytes in {self.free}")

    def give(self, at, size):
        joined = []
        for a, b in sorted(self.free + [(at, at + size)]):
            if joined and joined[-1][1] == a:
                joined[-1] = (joined[-1][0], b)
            else:
                joined.append((a, b))
        self.free = joined


def wait(eng, sem, count):
    if not isinstance(count, int) or count > 0:
        eng.wait_ge(sem, count)


def over_tiles(eng, n, body):
    pairs = (n - 1) // 2
    if pairs == 1:
        body(0, 0, False)
        body(1, 1, False)
    elif pairs > 1:
        with eng.Fori(0, pairs) as i:
            body(2 * i, 0, False)
            body(2 * i + 1, 1, False)
    for t in range(2 * pairs, n):
        body(t, t % 2, t == n - 1)


def program(nc, io):
    plan = []
    for name, n, kc, nt in STREAM:
        src, first = SHARED.get(name, (name, 0))
        plan += [(io["w_" + src], first + t, kc * nt) for t in range(n)]
    shapes = {name: (n, kc, nt) for name, n, kc, nt in STREAM}
    ring = Ring(plan)
    room = Map(-(-nc.sbuf_base // 32) * 32, nc.sbuf_top // 32 * 32)

    with ExitStack() as top:
        def sem(name):
            return top.enter_context(nc.semaphore(name))

        def sb(scope, name, shape, dtype=F32):
            size = -(-int(np.prod(shape[1:])) * 4 // 32) * 32
            at = room.take(size)
            scope.callback(room.give, at, size)
            return nc.alloc_sbuf_tensor_at(name, shape, dtype, offset=at)

        def psum(scope, name, shape):
            return scope.enter_context(nc.psum_tensor(name, shape, F32))

        def stage_block():
            return nc.Block(no_gpsimd_drain=True)

        small = sb(top, "small", [P, SMALLS])
        ident = sb(top, "ident", [P, P])
        ones = sb(top, "ones", [P, P])
        stage = sb(top, "stage", [P, 2, SLOT])
        x_lat = sb(top, "x_lat", [P, DC, LAT])
        mods = sb(top, "mods", [P, 2, 48, 2])
        ada = sb(top, "ada", [P, 24])
        scale_of = sb(top, "scale_of", [P, 2, 2, 2, DC])
        scale_2 = sb(top, "scale_2", [P, DC])

        def cols(name):
            a, b = SMALL[name]
            return small[:, a:b]

        eps_col = cols("eps")

        loaded = sem("inputs_loaded")
        w_landed = [sem("weights_landed_0"), sem("weights_landed_1")]
        hi_ready = sem("weights_hi_ready")
        lo_ready = sem("weights_lo_ready")
        unit_done = sem("unit_summed")
        unit_free = sem("unit_read")
        stored = sem("output_stored")

        def issue(sp, parity_of, t_expr, src, index, words):
            wait(sp, lo_ready, t_expr - 1)
            sp.dma_start(stage[:, parity_of, 0:words], src[bass.ds(index, 1)].rearrange("o p n -> p (o n)"))\
                .then_inc(w_landed[parity_of], 16)

        def issue_next(sp, upto_tile):
            while ring.issued < min(upto_tile, len(plan)):
                src, index, words = plan[ring.issued]
                issue(sp, ring.issued % 2, ring.issued, src, index, words)
                ring.issued += 1

        def issue_stage(sp, n):
            if ring.issued == ring.tile + 2 and n > 4:
                src, first, words = plan[ring.issued]
                base = ring.issued
                pairs = (n - 2) // 2
                with sp.Fori(0, pairs) as i:
                    for j in range(2):
                        issue(sp, (base + j) % 2, 2 * i + (base + j), src, 2 * i + (first + j), words)
                ring.issued += 2 * pairs
            issue_next(sp, ring.tile + n + 2)

        def landed(eng, t, parity):
            slot = (ring.tile + parity) % 2
            half = (t - parity) // 2 if isinstance(t, int) else None
            first = (ring.tile + parity) // 2 + 1
            if half is not None:
                eng.wait_ge(w_landed[slot], 16 * (first + half))
            else:
                eng.wait_ge(w_landed[slot], 8 * (t - parity) + 16 * first)
            return slot

        used_before = set()

        def counted_from(sems, first):
            again = id(sems) in used_before
            used_before.add(id(sems))
            if again or first:
                with stage_block() as block:
                    @block.vector
                    def _(dve):
                        for k, s in sems.items():
                            if again:
                                dve.sem_clear(s)
                            if k in first:
                                dve.sem_inc(s, first[k])
            return sems

        def linear(name, x_hi, x_lo, units, evac_act=None, evac_dve=None):
            n, kc, nt = shapes[name]
            assert plan[ring.tile][0] is io["w_" + SHARED.get(name, (name, 0))[0]]
            words = kc * nt
            units_of = units if callable(units) else lambda t: units
            U = len(units_of(0))
            c0 = ring.unit
            with ExitStack() as scope:
                w_hi = sb(scope, f"{name}_w_hi", [P, 2, words], F32R)
                w_lo = sb(scope, f"{name}_w_lo", [P, 2, words], F32R)
                acc = psum(scope, f"{name}_acc", [P, 2, 2, 512])

                def results(j):
                    return [acc[:, (c0 + j * U + u) % 2] for u in range(U)]

                def counts(t):
                    return lambda u: t * U + (c0 + u + 1)

                with stage_block() as block:
                    @block.sync
                    def _(sp):
                        issue_stage(sp, n)

                    @block.scalar
                    def _(act):
                        def round_hi(t, j):
                            slot = landed(act, t, j)
                            if not isinstance(t, int) or t >= 2:
                                act.wait_ge(unit_done, (t - 1) * U + c0)
                            nc.scalar.copy(w_hi[:, j, :], stage[:, slot, 0:words]).then_inc(hi_ready, 1)

                        round_hi(0, 0)

                        def body(t, j, last):
                            if not last:
                                round_hi(t + 1, 1 - j)
                            if evac_act:
                                evac_act(act, t, j, counts(t), results(j))

                        over_tiles(act, n, body)

                    @block.gpsimd
                    def _(pool):
                        def body(t, j, last):
                            pool.wait_ge(hi_ready, t + (ring.split + 1))
                            if not isinstance(t, int) or t >= 2:
                                wait(pool, unit_done, (t - 1) * U + c0)
                            nc.gpsimd.tensor_tensor(w_lo[:, j, :], stage[:, (ring.tile + j) % 2, 0:words],
                                                    w_hi[:, j, :].bitcast(F32), ALU.subtract).then_inc(lo_ready, 1)

                        over_tiles(pool, n, body)

                    @block.tensor
                    def _(pe):
                        def body(t, j, last):
                            hi = w_hi[:, j, :].rearrange("p (k n) -> p k n", k=kc)
                            lo = w_lo[:, j, :].rearrange("p (k n) -> p k n", k=kc)
                            for u, unit in enumerate(units_of(t)):
                                out = acc[:, (c0 + j * U + u) % 2]
                                if not isinstance(t, int) or c0 + t * U + u >= 2:
                                    wait(pe, unit_free, t * U + (c0 + u - 1))
                                if u == 0:
                                    pe.wait_ge(hi_ready, t + (ring.split + 1))
                                for part in ("hi", "lo"):
                                    if part == "lo" and u == 0:
                                        pe.wait_ge(lo_ready, t + (ring.tile + 1))
                                    w = hi if part == "hi" else lo
                                    for k in range(kc):
                                        for xi, x in enumerate((x_hi, x_lo) if part == "hi" else (x_hi,)):
                                            begin = part == "hi" and k == 0 and xi == 0
                                            end = part == "lo" and k == kc - 1
                                            if unit[0] == "F":
                                                for b, (s, m) in enumerate(unit[2]):
                                                    mm = nc.tensor.matmul(out[:, b, 0:m], w[:, k, unit[1]:unit[1] + P],
                                                                          x[:, k, s:s + m], start=begin, stop=end)
                                            else:
                                                mm = nc.tensor.matmul(out[:, 0, 0:unit[3]], x[:, k, unit[1]],
                                                                      w[:, k, unit[2]:unit[2] + unit[3]],
                                                                      start=begin, stop=end)
                                mm.then_inc(unit_done, 1)

                        over_tiles(pe, n, body)

                    @block.vector
                    def _(dve):
                        if evac_dve:
                            over_tiles(dve, n, lambda t, j, last: evac_dve(dve, t, j, counts(t), results(j)))

            ring.tile += n
            ring.split += n
            ring.unit += n * U

        ALL = [(0, LAT), (LAT, CTX)]
        ONLY_LAT = [(0, LAT)]

        def feature_units(segs, nt=256):
            return [("F", c, segs) for c in range(0, nt, P)]

        norm_sem = {k: sem("norm_" + k) for k in ("squares", "summed", "root", "rstd", "scaled", "hi", "lo")}
        norms = [0]

        def norm_split(x_of, groups, hi, lo):
            n = norms[0]
            norms[0] += 1
            T = sum(g[1] for g in groups)
            S = norm_sem
            G = len(groups)
            with ExitStack() as scope:
                squares = sb(scope, f"norm{n}_squares", [P, 2, T])
                rstd = sb(scope, f"norm{n}_rstd", [P, T])
                scaled = sb(scope, f"norm{n}_scaled", [P, 2, T])
                total = psum(scope, f"norm{n}_total", [P, 2, 512])
                done = {k: norm_done.get(k, 0) for k in S}
                with stage_block() as block:
                    @block.scalar
                    def _(act):
                        for c in range(DC):
                            if c >= 2:
                                act.wait_ge(S["summed"], done["summed"] + c - 1)
                            for s, m, _, _ in groups:
                                last = nc.scalar.activation(squares[:, c % 2, s:s + m], x_of(c, s, m), ACT.Square)
                            last.then_inc(S["squares"], 1)
                        act.wait_ge(S["summed"], done["summed"] + DC)
                        for b, (s, m, _, _) in enumerate(groups):
                            last = nc.scalar.activation(rstd[:, s:s + m], total[:, b, 0:m], ACT.Sqrt, bias=eps_col,
                                                        scale=1.0 / D)
                        last.then_inc(S["root"], 1)
                        for c in range(DC):
                            act.wait_ge(S["scaled"], done["scaled"] + c + 1)
                            for s, m, _, b in groups:
                                last = nc.scalar.activation(hi[:, c, s:s + m], scaled[:, c % 2, s:s + m],
                                                            ACT.Identity, bias=b(c))
                            last.then_inc(S["hi"], 1)

                    @block.tensor
                    def _(pe):
                        for c in range(DC):
                            pe.wait_ge(S["squares"], done["squares"] + c + 1)
                            for b, (s, m, _, _) in enumerate(groups):
                                mm = nc.tensor.matmul(total[:, b, 0:m], ones[:], squares[:, c % 2, s:s + m],
                                                      start=c == 0, stop=c == DC - 1)
                            mm.then_inc(S["summed"], 1)

                    @block.vector
                    def _(dve):
                        dve.wait_ge(S["root"], done["root"] + 1)
                        nc.vector.reciprocal(rstd[:], rstd[:]).then_inc(S["rstd"], 1)
                        dve.wait_ge(S["rstd"], done["rstd"] + 1)

                        def low(c):
                            dve.wait_ge(S["hi"], done["hi"] + c + 1)
                            for s, m, _, b in groups:
                                last = nc.vector.scalar_tensor_tensor(
                                    lo[:, c, s:s + m], scaled[:, c % 2, s:s + m], b(c),
                                    hi[:, c, s:s + m].bitcast(F32), ALU.add, ALU.subtract)
                            last.then_inc(S["lo"], 1)

                        for c in range(DC):
                            if c >= 2:
                                dve.wait_ge(S["lo"], done["lo"] + c - 1)
                            for s, m, a, _ in groups:
                                last = nc.vector.scalar_tensor_tensor(
                                    scaled[:, c % 2, s:s + m], x_of(c, s, m), a(c), rstd[:, s:s + m],
                                    ALU.mult, ALU.mult)
                            last.then_inc(S["scaled"], 1)
                            if c >= 1:
                                low(c - 1)
                        low(DC - 1)
            for k, m in (("squares", DC), ("summed", DC), ("root", 1), ("rstd", 1), ("scaled", DC), ("hi", DC),
                         ("lo", DC)):
                norm_done[k] = done[k] + m

        norm_done = {}

        cut_sem = {"hi": sem("cut_hi"), "lo": sem("cut_lo")}
        cut_done = [0]

        def cut(src, hi, lo, chunks):
            base = cut_done[0]
            cut_done[0] += chunks
            with stage_block() as block:
                @block.scalar
                def _(act):
                    with act.Fori(0, chunks) as c:
                        nc.scalar.copy(hi[:, bass.ds(c, 1), :], src[:, bass.ds(c, 1), :]).then_inc(cut_sem["hi"], 1)

                @block.vector
                def _(dve):
                    with dve.Fori(0, chunks) as c:
                        dve.wait_ge(cut_sem["hi"], c + (base + 1))
                        nc.vector.tensor_tensor(lo[:, bass.ds(c, 1), :], src[:, bass.ds(c, 1), :],
                                                hi[:, bass.ds(c, 1), :].bitcast(F32), ALU.subtract)\
                            .then_inc(cut_sem["lo"], 1)

        ffn_sem = {k: sem("ffn_" + k) for k in ("hi", "lo")}
        ffn_done = [1]

        def feed_forward(layer, x_hi, x_lo, segs, residual):
            T = sum(m for _, m in segs)
            for half in (0, 1):
                base = ffn_done[0]
                ffn_done[0] += HALF
                with ExitStack() as scope:
                    h_hi = sb(scope, f"ffn{layer}{half}_hi", [P, HALF, T], F32R)
                    h_lo = sb(scope, f"ffn{layer}{half}_lo", [P, HALF, T], F32R)
                    with ExitStack() as inner:
                        gate = sb(inner, f"ffn{layer}{half}_gate", [P, T])
                        hidden = sb(inner, f"ffn{layer}{half}_hidden", [P, T])

                        def evac_act(act, t, j, count, res):
                            act.wait_ge(unit_done, count(0))
                            for b, (s, m) in enumerate(segs):
                                last = nc.scalar.activation(gate[:, s:s + m], res[0][:, b, 0:m], ACT.Silu)
                            last.then_inc(unit_free, 1)
                            act.wait_ge(unit_free, count(1))
                            nc.scalar.copy(h_hi[:, bass.ds(t, 1), :], hidden[:].rearrange("p (o n) -> p o n", o=1))\
                                .then_inc(ffn_sem["hi"], 1)

                        def evac_dve(dve, t, j, count, res):
                            dve.wait_ge(unit_done, count(1))
                            dve.wait_ge(unit_free, count(0))
                            wait(dve, ffn_sem["lo"], t + base)
                            for b, (s, m) in enumerate(segs):
                                last = nc.vector.tensor_tensor(hidden[:, s:s + m], res[1][:, b, 0:m],
                                                               gate[:, s:s + m], ALU.mult)
                            last.then_inc(unit_free, 1)
                            dve.wait_ge(ffn_sem["hi"], t + (base + 1))
                            nc.vector.tensor_tensor(h_lo[:, bass.ds(t, 1), :],
                                                    hidden[:].rearrange("p (o n) -> p o n", o=1),
                                                    h_hi[:, bass.ds(t, 1), :].bitcast(F32), ALU.subtract)\
                                .then_inc(ffn_sem["lo"], 1)

                        linear(f"f{layer}i{half}", x_hi, x_lo, feature_units(segs), evac_act, evac_dve)
                    linear(f"f{layer}o{half}", h_hi, h_lo, [("F", 0, segs)], None, residual)

        def add_residual(segs, gates, per_tile):
            def evac(dve, t, j, count, res):
                for u in range(per_tile):
                    dve.wait_ge(unit_done, count(u))
                    for b, (s, m) in enumerate(segs):
                        c = t * per_tile + u
                        x = x_lat[:, bass.ds(c, 1), :] if s == 0 else x_ctx[0][:, bass.ds(c, 1), :]
                        x = x.rearrange("p o n -> p (o n)")
                        last = nc.vector.scalar_tensor_tensor(
                            x, res[u][:, b, 0:m], gates[b][:, bass.ds(c, 1)], x, ALU.mult, ALU.add)
                    last.then_inc(unit_free, 1)
            return evac

        x_ctx = [None]

        rope_loaded, rope_turned = sem("ret_rope_loaded"), sem("ret_rope_turned")
        conv_sem, silu_sem = sem("conv_tap"), sem("conv_silu")
        with stage_block() as block:
            @block.sync
            def _(sp):
                for dst, src in ((small, "small"), (ident, "ident"), (ones, "ones")):
                    sp.dma_start(dst[:], io[src]).then_inc(loaded, 16)
                issue_next(sp, 2)
                sp.dma_start(x_lat[:], io["x"]).then_inc(loaded, 16)

            @block.vector
            def _(dve):
                for s in (unit_done, unit_free):
                    dve.sem_inc(s, ring.unit)
                for s in ffn_sem.values():
                    dve.sem_inc(s, ffn_done[0])
                dve.sem_inc(rope_turned, 1)
                dve.sem_inc(silu_sem, 2)

        cond_ready, modded = sem("cond_ready"), sem("modulation_ready")
        with ExitStack() as scope:
            cond = sb(scope, "cond_silu", [P, 24])
            mod_sum = psum(scope, "mod_sum", [P, 512])
            n, kc, nt = shapes["mod"]
            main = 48
            with stage_block() as block:
                @block.sync
                def _(sp):
                    issue_stage(sp, n)

                @block.scalar
                def _(act):
                    act.wait_ge(loaded, 64)
                    a, b = SMALL["cond"][0], SMALL["cond_2"][1]
                    nc.scalar.activation(cond[:], small[:, a:b], ACT.Silu).then_inc(cond_ready, 1)

                @block.tensor
                def _(pe):
                    pe.wait_ge(cond_ready, 1)

                    def tile(t, j, ncols, at):
                        slot = landed(pe, t, j)
                        w = stage[:, slot, :].rearrange("p (k n) -> p k n", k=kc)
                        for u in range(2):
                            for k in range(kc):
                                rhs = cond[:, k:16:8] if ncols == 2 else cond[:, 16 + k:17 + k]
                                mm = nc.tensor.matmul(mod_sum[:, bass.ds(at + u * ncols, ncols)],
                                                      w[:, k, u * P:(u + 1) * P], rhs,
                                                      start=k == 0, stop=k == kc - 1, skip_group_check=True)
                        mm.then_inc(lo_ready, 1)

                    with pe.Fori(0, main // 2) as i:
                        for j in range(2):
                            tile(2 * i + j, j, 2, 8 * i + 4 * j)
                    with pe.Fori(0, (n - main) // 2) as i:
                        for j in range(2):
                            tile(2 * i + (main + j), j, 1, 4 * i + (4 * main + 2 * j))

                @block.vector
                def _(dve):
                    dve.wait_ge(loaded, 64)
                    dve.wait_ge(lo_ready, n)
                    a, b = SMALL["mod_b"]
                    bias = small[:, a:b].rearrange("p (m o) -> p m o", o=1).broadcast_to([P, 96, 2])
                    nc.vector.tensor_tensor(mods[:].rearrange("p l m v -> p (l m) v"),
                                            mod_sum[:, 0:192].rearrange("p (m v) -> p m v", v=2), bias, ALU.add)
                    nc.vector.tensor_tensor(ada[:], mod_sum[:, 192:216], cols("ada_b"), ALU.add).then_inc(modded, 1)
                    dve.wait_ge(modded, 1)
                    gain = cols("norm_g").rearrange("p (l w c) -> p l w c", l=2, w=2)
                    for layer in range(2):
                        for which in range(2):
                            for v in range(2):
                                m = 24 * which + 8
                                nc.vector.scalar_tensor_tensor(
                                    scale_of[:, layer, which, v, :], mods[:, layer, m:m + 8, v], 1.0,
                                    gain[:, layer, which, :], ALU.add, ALU.mult)
                    nc.vector.scalar_tensor_tensor(scale_2[:], ada[:, 8:16], 1.0, cols("norm_w"), ALU.add, ALU.mult)\
                        .then_inc(modded, 1)
            ring.tile += n

        def group(layer, which, v, first, tokens):
            return (first, tokens, lambda c: scale_of[:, layer, which, v, c:c + 1],
                    lambda c: mods[:, layer, 24 * which + c, v:v + 1])

        def gates_of(layer, which, v):
            m = 24 * which + 16
            return mods[:, layer, m:m + 8, v]

        def copy_units(buf, first, per_tile=2, func=ACT.Identity):
            def evac(act, t, j, count, res):
                for u in range(per_tile):
                    act.wait_ge(unit_done, count(u))
                    width = buf.shape[2]
                    for b, s in enumerate(range(0, width, 512)):
                        m = min(512, width - s)
                        last = nc.scalar.activation(
                            buf[:, bass.ds(t * per_tile + (first + u), 1), s:s + m],
                            res[u][:, b:b + 1, 0:m], func)
                    last.then_inc(unit_free, 1)
            return evac

        mix = ExitStack()

        ctx_scope = ExitStack()
        x_ctx[0] = sb(ctx_scope, "x_ctx", [P, DC, CTX])
        ctx_loaded = sem("context_loaded")
        with stage_block() as block:
            @block.sync
            def _(sp):
                sp.dma_start(x_ctx[0][:], io["ctx"]).then_inc(ctx_loaded, 16)
                sp.wait_ge(ctx_loaded, 16)

        def x_all(c, s, m):
            return x_lat[:, c, s:s + m] if s < LAT else x_ctx[0][:, c, s - LAT:s - LAT + m]

        attend_jobs = ("scores", "scores_read", "maximum", "exp", "turned", "turned_read", "mixed")
        attend_sem = {}
        for k in attend_jobs + ("queries", "reciprocal", "normed", "out", "out_read", "log", "lse"):
            attend_sem[k] = sem("attend_" + k)

        def attend(tag, blocks, heads, q_copies, out_copies, width, kb_max, cols_out, scale, lse=None):
            H = len(heads)
            S = counted_from(attend_sem, {k: H if k in attend_jobs else 1 for k in attend_sem})
            chunks = cols_out // P
            with ExitStack() as scope:
                has_sink = heads[0]["sink"] is not None
                row = sb(scope, f"{tag}_row", [P, 2, width + has_sink])
                minus_max = sb(scope, f"{tag}_minus_max", [P, H])
                total = sb(scope, f"{tag}_total", [P, H])
                inverse = sb(scope, f"{tag}_inverse", [P, H])
                log_total = sb(scope, f"{tag}_log_total", [P, H])
                probs = sb(scope, f"{tag}_probs", [P, 2, kb_max * P])
                mixed = sb(scope, f"{tag}_mixed", [P, cols_out])
                sbanks = (width + 511) // 512
                p_scores = psum(scope, f"{tag}_p_scores", [P, 2, sbanks, 512])
                p_turned = psum(scope, f"{tag}_p_turned", [P, (kb_max + 3) // 4 * 512])
                p_mixed = psum(scope, f"{tag}_p_mixed", [P, (cols_out + 511) // 512 * 512])
                p_out = psum(scope, f"{tag}_p_out", [P, (cols_out + 511) // 512 * 512])

                def slot_of(h):
                    n = heads[h]["column"] // 64
                    return slice(n, n + 1)

                def before(i, h, lag):
                    return i * H + (H + max(h + 1 - lag, 0))

                def key_blocks(i, h):
                    return sum(k[1] for k in heads[h]["keys"](i)) // P

                with stage_block() as block:
                    @block.tensor
                    def _(pe):
                        def scores(i, h):
                            if h == 0:
                                pe.wait_ge(S["queries"], i + 2)
                            pe.wait_ge(S["scores_read"], before(i, h, 2))
                            for b, (_, m, rhs, _) in enumerate(heads[h]["keys"](i)):
                                mm = nc.tensor.matmul(p_scores[:, h % 2, b, 0:m], heads[h]["q"], rhs,
                                                      start=True, stop=True)
                            mm.then_inc(S["scores"], 1)

                        def turn(i, h):
                            pe.wait_ge(S["exp"], i * H + (H + h + 1))
                            pe.wait_ge(S["turned_read"], i * H + (H + h))
                            for b in range(key_blocks(i, h)):
                                mm = nc.tensor.transpose(p_turned[:, b * P:(b + 1) * P],
                                                         row[:, h % 2, b * P:(b + 1) * P], ident[:])
                            mm.then_inc(S["turned"], 1)

                        def mix_values(i, h):
                            pe.wait_ge(S["turned_read"], i * H + (H + h + 1))
                            if h == 0:
                                pe.wait_ge(S["normed"], i + 1)
                            c = heads[h]["column"]
                            n = key_blocks(i, h)
                            for b, v in enumerate(heads[h]["values"](i)):
                                mm = nc.tensor.matmul(p_mixed[:, c:c + 64], probs[:, h % 2, b * P:(b + 1) * P], v,
                                                      start=b == 0, stop=b == n - 1)
                            mm.then_inc(S["mixed"], 1)

                        with pe.Fori(0, blocks) as i:
                            scores(i, 0)
                            for h in range(H):
                                if h + 1 < H:
                                    scores(i, h + 1)
                                turn(i, h)
                                if h >= 1:
                                    mix_values(i, h - 1)
                            mix_values(i, H - 1)
                            pe.wait_ge(S["normed"], i + 2)
                            pe.wait_ge(S["out_read"], i + 1)
                            for c in range(chunks):
                                mm = nc.tensor.transpose(p_out[:, c * P:(c + 1) * P], mixed[:, c * P:(c + 1) * P],
                                                         ident[:])
                            mm.then_inc(S["out"], 1)

                    @block.vector
                    def _(dve):
                        def read_scores(i, h):
                            head = heads[h]
                            if lse is not None and h == 0:
                                dve.wait_ge(S["lse"], i + 1)
                            dve.wait_ge(S["scores"], i * H + (H + h + 1))
                            dve.wait_ge(S["turned"], before(i, h, 2))
                            if head["sink"] is not None:
                                n = key_blocks(i, h) * P
                                nc.vector.tensor_copy(row[:, h % 2, n:n + 1], head["sink"])
                            for b, (s, m, _, mask) in enumerate(head["keys"](i)):
                                if mask is None:
                                    last = nc.vector.tensor_scalar(row[:, h % 2, s:s + m], p_scores[:, h % 2, b, 0:m],
                                                                   scale, None, ALU.mult)
                                else:
                                    last = nc.vector.scalar_tensor_tensor(
                                        row[:, h % 2, s:s + m], p_scores[:, h % 2, b, 0:m], scale, mask,
                                        ALU.mult, ALU.add)
                            last.then_inc(S["scores_read"], 1)
                            dve.wait_ge(S["scores_read"], i * H + (H + h + 1))
                            n = key_blocks(i, h) * P + has_sink
                            nc.vector.tensor_reduce(minus_max[:, slot_of(h)], row[:, h % 2, 0:n], AX_X, ALU.max,
                                                    negate=True).then_inc(S["maximum"], 1)

                        with dve.Fori(0, blocks) as i:
                            for h in range(H):
                                read_scores(i, h)
                            dve.wait_ge(S["mixed"], i * H + 2 * H)
                            nc.vector.reciprocal(inverse[:], total[:]).then_inc(S["reciprocal"], 1)
                            dve.wait_ge(S["reciprocal"], i + 2)
                            dve.wait_ge(S["out"], i + 1)
                            nc.vector.tensor_tensor(
                                mixed[:].rearrange("p (h n) -> p h n", n=64),
                                p_mixed[:, 0:cols_out].rearrange("p (h n) -> p h n", n=64),
                                inverse[:].rearrange("p (h o) -> p h o", o=1).broadcast_to([P, H, 64]), ALU.mult)\
                                .then_inc(S["normed"], 1)
                            if lse is not None:
                                dve.wait_ge(S["log"], i + 2)
                                nc.vector.tensor_tensor(lse[:, bass.ds(i, 1), :].rearrange("p o h -> p (o h)"),
                                                        log_total[:], minus_max[:], ALU.subtract)\
                                    .then_inc(S["lse"], 1)

                    @block.scalar
                    def _(act):
                        def exponent(i, h):
                            act.wait_ge(S["maximum"], i * H + (H + h + 1))
                            n = key_blocks(i, h) * P + has_sink
                            nc.scalar.activation(row[:, h % 2, 0:n], row[:, h % 2, 0:n], ACT.Exp,
                                                 bias=minus_max[:, slot_of(h)], accum_out=total[:, slot_of(h)])\
                                .then_inc(S["exp"], 1)

                        def copy_turned(i, h):
                            act.wait_ge(S["turned"], i * H + (H + h + 1))
                            act.wait_ge(S["mixed"], before(i, h, 2))
                            n = key_blocks(i, h) * P
                            nc.scalar.copy(probs[:, h % 2, 0:n], p_turned[:, 0:n]).then_inc(S["turned_read"], 1)

                        with act.Fori(0, blocks) as i:
                            act.wait_ge(S["scores"], i * H + H)
                            for dst, src in q_copies(i):
                                last = nc.scalar.copy(dst, src)
                            last.then_inc(S["queries"], 1)
                            exponent(i, 0)
                            for h in range(H):
                                if h + 1 < H:
                                    exponent(i, h + 1)
                                copy_turned(i, h)
                            if lse is not None:
                                act.wait_ge(S["exp"], i * H + 2 * H)
                                act.wait_ge(S["lse"], i + 1)
                                nc.scalar.activation(log_total[:], total[:], ACT.Ln).then_inc(S["log"], 1)
                            act.wait_ge(S["out"], i + 2)
                            for dst, src in out_copies(i, p_out):
                                last = nc.scalar.copy(dst, src)
                            last.then_inc(S["out_read"], 1)

        mixed_0 = sb(mix, "mixed_0", [P, DC, TOK])
        normed_scope = ExitStack()
        n_hi = sb(normed_scope, "norm_a_hi", [P, DC, TOK], F32R)
        n_lo = sb(normed_scope, "norm_a_lo", [P, DC, TOK], F32R)
        norm_split(x_all, [group(0, 0, 0, 0, LAT), group(0, 0, 1, LAT, CTX)], n_hi, n_lo)

        attn = ExitStack()
        qk = sb(attn, "qk", [P, 5, TOK])
        k_pad = sb(attn, "k_pad", [P, P + LAT + P + CTX])
        v_pad = sb(attn, "v_pad", [P, 8, P])
        pad_ready = sem("pads_zeroed")

        linear("aq", n_hi, n_lo, feature_units(ALL), copy_units(qk, 0))

        def evac_akv(act, t, j, count, res):
            act.wait_ge(unit_done, count(0))
            nc.scalar.copy(qk[:, 4, 0:LAT], res[0][:, 0, :])
            nc.scalar.copy(qk[:, 4, LAT:TOK], res[0][:, 1, 0:CTX]).then_inc(unit_free, 1)
            for b in range(6):
                act.wait_ge(unit_done, count(1 + b))
                nc.scalar.copy(v_pad[:, b + 1 if b < 4 else b + 2, :], res[1 + b][:, 0, 0:P]).then_inc(unit_free, 1)

        linear("akv", n_hi, n_lo, [("F", 0, ALL)] + [("T", slice(b * P, (b + 1) * P), P, P) for b in range(6)],
               evac_akv)

        hn = {k: sem("headnorm_" + k) for k in ("tables", "squares", "summed", "root", "rstd", "normed", "rotated",
                                               "cosine", "sine", "done")}
        with ExitStack() as scope:
            axial = sb(scope, "axial", [P, 2, LAT])
            rotT = sb(scope, "rotT", [P, P])
            ones64 = sb(scope, "ones64", [P, P])
            squares = sb(scope, "head_squares", [P, 2, TOK])
            rstd = sb(scope, "head_rstd", [P, 2, TOK])
            unit = sb(scope, "head_unit", [P, 2, TOK])
            turn_c = sb(scope, "head_cosine", [P, 2, LAT])
            turn_s = sb(scope, "head_sine", [P, 2, LAT])
            p_sum = psum(scope, "head_sum", [P, 2, 2, 512])
            p_rot = psum(scope, "head_rot", [P, 2, 512])
            with stage_block() as block:
                @block.sync
                def _(sp):
                    for dst, src in ((axial, "axial"), (rotT, "rotT"), (ones64, "ones64")):
                        sp.dma_start(dst[:], io[src]).then_inc(hn["tables"], 16)

                @block.gpsimd
                def _(pool):
                    for pad in (k_pad[:, 0:P], k_pad[:, P + LAT:2 * P + LAT], v_pad[:, 0, :], v_pad[:, 5, :]):
                        nc.gpsimd.memset(pad, 0.0).then_inc(pad_ready, 1)
                    pool.wait_ge(pad_ready, 4)

                @block.scalar
                def _(act):
                    for c in range(5):
                        if c >= 2:
                            act.wait_ge(hn["summed"], c - 1)
                        nc.scalar.activation(squares[:, c % 2, :], qk[:, c, :], ACT.Square).then_inc(hn["squares"], 1)
                        act.wait_ge(hn["summed"], c + 1)
                        if c >= 2:
                            act.wait_ge(hn["normed"], c - 1)
                        nc.scalar.activation(rstd[:, c % 2, 0:LAT], p_sum[:, c % 2, 0, :], ACT.Sqrt, bias=eps_col,
                                             scale=1.0 / 64)
                        nc.scalar.activation(rstd[:, c % 2, LAT:TOK], p_sum[:, c % 2, 1, 0:CTX], ACT.Sqrt, bias=eps_col,
                                             scale=1.0 / 64).then_inc(hn["root"], 1)

                @block.tensor
                def _(pe):
                    pe.wait_ge(hn["tables"], 48)

                    def rotate(c):
                        pe.wait_ge(hn["normed"], c + 1)
                        if c >= 2:
                            pe.wait_ge(hn["sine"], c - 1)
                        nc.tensor.matmul(p_rot[:, c % 2, :], rotT[:], unit[:, c % 2, 0:LAT], start=True, stop=True)\
                            .then_inc(hn["rotated"], 1)

                    for c in range(5):
                        pe.wait_ge(hn["squares"], c + 1)
                        if c >= 2:
                            pe.wait_ge(hn["root"], c - 1)
                        nc.tensor.matmul(p_sum[:, c % 2, 0, :], ones64[:], squares[:, c % 2, 0:LAT], start=True, stop=True)
                        nc.tensor.matmul(p_sum[:, c % 2, 1, 0:CTX], ones64[:], squares[:, c % 2, LAT:TOK],
                                         start=True, stop=True).then_inc(hn["summed"], 1)
                        if c >= 1:
                            rotate(c - 1)
                    rotate(4)

                @block.vector
                def _(dve):
                    dve.wait_ge(hn["tables"], 48)
                    for c in range(5):
                        g = cols("qk_g")[:, 0:1] if c < 4 else cols("qk_g")[:, 1:2]
                        dve.wait_ge(hn["root"], c + 1)
                        nc.vector.reciprocal(rstd[:, c % 2, :], rstd[:, c % 2, :]).then_inc(hn["rstd"], 1)
                        dve.wait_ge(hn["rstd"], c + 1)
                        nc.vector.scalar_tensor_tensor(unit[:, c % 2, :], qk[:, c, :], g, rstd[:, c % 2, :],
                                                       ALU.mult, ALU.mult).then_inc(hn["normed"], 1)
                        dve.wait_ge(hn["normed"], c + 1)
                        nc.vector.tensor_tensor(turn_c[:, c % 2, :], unit[:, c % 2, 0:LAT], axial[:, 0, :], ALU.mult)\
                            .then_inc(hn["cosine"], 1)
                        dve.wait_ge(hn["rotated"], c + 1)
                        nc.vector.tensor_tensor(turn_s[:, c % 2, :], p_rot[:, c % 2, :], axial[:, 1, :], ALU.mult)\
                            .then_inc(hn["sine"], 1)
                        dve.wait_ge(hn["sine"], c + 1)
                        lat, ctx = ((qk[:, c, 0:LAT], qk[:, c, LAT:TOK]) if c < 4 else
                                    (k_pad[:, P:P + LAT], k_pad[:, 2 * P + LAT:2 * P + TOK]))
                        nc.vector.tensor_copy(ctx, unit[:, c % 2, LAT:TOK])
                        nc.vector.tensor_tensor(lat, turn_c[:, c % 2, :], turn_s[:, c % 2, :], ALU.add)\
                            .then_inc(hn["done"], 1)

        with ExitStack() as scope:
            q_zero = sb(scope, "q_zero", [P, 8, P])
            window = sb(scope, "window", [P, 4, 3 * P])
            window_ready, zeroed = sem("window_loaded"), sem("queries_zeroed")
            with stage_block() as block:
                @block.sync
                def _(sp):
                    sp.dma_start(window[:], io["window"]).then_inc(window_ready, 16)
                    sp.wait_ge(window_ready, 16)

                @block.vector
                def _(dve):
                    nc.vector.memset(q_zero[:], 0.0).then_inc(zeroed, 1)

            k_ctx = k_pad[:, 2 * P + LAT:2 * P + TOK]

            def head_of(h, with_lat):
                g = h // 4
                half = slice(64 * g, 64 * g + 64)

                def keys(i):
                    ctx = (3 * P if with_lat else 0, CTX, k_ctx, None)
                    if not with_lat:
                        return [ctx]
                    mask = window[:, bass.ds(i, 1), :].rearrange("p o n -> p (o n)")
                    return [(0, 3 * P, k_pad[:, bass.ds(i * P, 3 * P)], mask), ctx]

                def values(i):
                    lat = [v_pad[:, bass.ds(i + b, 1), half].rearrange("p o n -> p (o n)") for b in range(3)]
                    return lat * with_lat + [v_pad[:, 6, half], v_pad[:, 7, half]]

                return dict(q=q_zero[:, h, :], keys=keys, values=values, column=(h % 4) * P + 64 * g,
                            sink=cols("sink")[:, h:h + 1])

            def q_copies_from(first):
                def copies(i):
                    return [(q_zero[64 * g:64 * g + 64, 4 * g:4 * g + 4, :],
                             qk[64 * g:64 * g + 64, 0:4, bass.ds(i * P + first, P)]) for g in range(2)]
                return copies

            def out_copies_to(first):
                def copies(i, p_out):
                    return [(mixed_0[:, 0:4, bass.ds(i * P + first, P)],
                             p_out[:, 0:512].rearrange("p (c n) -> p c n", c=4))]
                return copies

            attend("win", LAT // P, [head_of(h, True) for h in range(8)], q_copies_from(0), out_copies_to(0),
                   3 * P + CTX, 5, 512, 64.0 ** -0.5)
            attend("ctxa", CTX // P, [head_of(h, False) for h in range(8)], q_copies_from(LAT), out_copies_to(LAT),
                   CTX, 2, 512, 64.0 ** -0.5)
        attn.close()

        head_norm_sem = {k: sem("head_norm_" + k) for k in ("squares", "summed", "root", "rstd", "scaled", "gated")}

        def head_norm(tag, heads, per, width, out, gain=None, gate=None):
            S = counted_from(head_norm_sem, {})
            segs = [(s, min(512, width - s)) for s in range(0, width, 512)]
            with ExitStack() as scope:
                squares = sb(scope, f"{tag}_squares", [P, 2, width])
                rstd = sb(scope, f"{tag}_rstd", [P, 2, width])
                total = psum(scope, f"{tag}_sums", [P, 2, len(segs), 512])
                with stage_block() as block:
                    @block.scalar
                    def _(act):
                        def root(h):
                            act.wait_ge(S["summed"], (h + 1) * per)
                            if h >= 2:
                                act.wait_ge(S["scaled"], h - 1)
                            for b, (s, m) in enumerate(segs):
                                last = nc.scalar.activation(rstd[:, h % 2, s:s + m], total[:, h % 2, b, 0:m], ACT.Sqrt,
                                                            bias=eps_col, scale=1.0 / (per * P))
                            last.then_inc(S["root"], 1)

                        for h in range(heads):
                            for j in range(per):
                                n = h * per + j
                                if n >= 2:
                                    act.wait_ge(S["summed"], n - 1)
                                nc.scalar.activation(squares[:, n % 2, :], out(h, j), ACT.Square)\
                                    .then_inc(S["squares"], 1)
                            if h >= 1:
                                root(h - 1)
                        root(heads - 1)

                    @block.tensor
                    def _(pe):
                        for h in range(heads):
                            if h >= 2:
                                pe.wait_ge(S["root"], h - 1)
                            for j in range(per):
                                n = h * per + j
                                pe.wait_ge(S["squares"], n + 1)
                                for b, (s, m) in enumerate(segs):
                                    mm = nc.tensor.matmul(total[:, h % 2, b, 0:m], ones[:], squares[:, n % 2, s:s + m],
                                                          start=j == 0, stop=j == per - 1)
                                mm.then_inc(S["summed"], 1)

                    @block.vector
                    def _(dve):
                        for h in range(heads):
                            dve.wait_ge(S["root"], h + 1)
                            nc.vector.reciprocal(rstd[:, h % 2, :], rstd[:, h % 2, :]).then_inc(S["rstd"], 1)
                            dve.wait_ge(S["rstd"], h + 1)
                            for j in range(per):
                                g = gain(j) if callable(gain) else gain
                                if g is None:
                                    last = nc.vector.tensor_tensor(out(h, j), out(h, j), rstd[:, h % 2, :], ALU.mult)
                                else:
                                    last = nc.vector.scalar_tensor_tensor(out(h, j), out(h, j), g, rstd[:, h % 2, :],
                                                                          ALU.mult, ALU.mult)
                            last.then_inc(S["scaled"], 1)
                            if gate is not None:
                                dve.wait_ge(S["scaled"], h + 1)
                                for j in range(per):
                                    last = nc.vector.tensor_tensor(out(h, j), out(h, j), gate(h, j), ALU.mult)
                                last.then_inc(S["gated"], 1)

        gla = ExitStack()
        q_silu = sb(gla, "hgrn_q", [P, GLA_H, TOK])
        keep = sb(gla, "hgrn_forget", [P, 2 * GLA_H, TOK])
        i_tok = sb(gla, "hgrn_i", [P, TOK // P, 512])
        g_silu = sb(gla, "hgrn_gate", [P, GLA_H, TOK])
        linear("bq", n_hi, n_lo, feature_units(ALL), copy_units(q_silu, 0, func=ACT.Silu))
        linear("bg", n_hi, n_lo, feature_units(ALL), copy_units(g_silu, 0, func=ACT.Silu))
        linear("bf", n_hi, n_lo, feature_units(ALL), copy_units(keep, 0, func=ACT.Sigmoid))

        def token_units(blocks, nt=256):
            return [("T", slice(b * P, (b + 1) * P), 0, nt) for b in range(blocks)]

        def copy_token_units(buf, blocks, first=0):
            def evac(act, t, j, count, res):
                for b in range(blocks):
                    act.wait_ge(unit_done, count(b))
                    nc.scalar.copy(buf[:, first + b, bass.ds(t * 256, 256)], res[b][:, 0, 0:256]).then_inc(unit_free, 1)
            return evac

        linear("bi", n_hi, n_lo, token_units(6), copy_token_units(i_tok, 6))
        normed_scope.close()

        CH = TOK // 64
        ORDER = ([8, 9, 10, 11, 0, 1, 2, 3, 4, 5, 6, 7], [11, 10, 9, 8, 7, 6, 5, 4, 3, 2, 1, 0])
        REF, LAST = (32, 31), (63, 0)
        gs = {k: sem("hgrn_" + k) for k in ("tables", "zeroed", "top", "bound_exp", "bound", "f", "ln", "k", "cum", "dist",
                                           "exp", "q_scaled", "k_scaled", "turned", "turned_read", "scores", "masked",
                                           "kv", "link", "states", "out", "out_read")}
        with ExitStack() as scope:
            tri64 = sb(scope, "tri64", [P, 2, 64])
            restart = sb(scope, "restart", [P, 2, TOK])
            bound = sb(scope, "hgrn_bound", [P, 6, GLA_H])
            log_f = sb(scope, "hgrn_log_f", [P, TOK])
            cum = sb(scope, "hgrn_cum", [P, TOK])
            to_ref = sb(scope, "hgrn_to_ref", [P, TOK])
            q_ref = sb(scope, "hgrn_q_ref", [P, TOK])
            k_ref = sb(scope, "hgrn_k_ref", [P, TOK])
            k_end = sb(scope, "hgrn_k_end", [P, TOK])
            k_end_tok = sb(scope, "hgrn_k_end_tok", [P, CH, P])
            q_cum = sb(scope, "hgrn_q_cum", [P, 2, TOK])
            decay = sb(scope, "hgrn_decay", [P, 2, CH])
            state = sb(scope, "hgrn_state", [P, 2, CH, P])
            scores = sb(scope, "hgrn_scores", [P, 2, CH, 64])
            p_turned = psum(scope, "hgrn_p_turned", [P, 1024])
            p_scores = psum(scope, "hgrn_p_scores", [P, 512])
            p_kv = psum(scope, "hgrn_p_kv", [P, 1536])
            p_out = psum(scope, "hgrn_p_out", [P, 1024])

            def by_chunk(ap):
                return ap.rearrange("p (c n) -> p c n", n=64)

            def at_chunk(ap, place):
                return by_chunk(ap)[:, :, place:place + 1].broadcast_to([P, CH, 64])

            with stage_block() as block:
                @block.sync
                def _(sp):
                    sp.dma_start(tri64[:], io["tri64"]).then_inc(gs["tables"], 16)
                    sp.dma_start(restart[:], io["restart"]).then_inc(gs["tables"], 16)

                @block.vector
                def _(dve):
                    a, b = cols("lb")[:, 0:GLA_H], cols("lb")[:, GLA_H:2 * GLA_H]
                    nc.vector.tensor_tensor(bound[:, 0, :], a, b, ALU.max).then_inc(gs["top"], 1)
                    dve.wait_ge(gs["top"], 1)
                    nc.vector.tensor_tensor(bound[:, 1, :], a, bound[:, 0, :], ALU.subtract)
                    nc.vector.tensor_tensor(bound[:, 2, :], b, bound[:, 0, :], ALU.subtract).then_inc(gs["top"], 1)
                    dve.wait_ge(gs["bound_exp"], 1)
                    nc.vector.tensor_tensor(bound[:, 3, :], bound[:, 1, :], bound[:, 2, :], ALU.add).then_inc(gs["bound"], 1)
                    dve.wait_ge(gs["bound"], 1)
                    nc.vector.reciprocal(bound[:, 3, :], bound[:, 3, :]).then_inc(gs["bound"], 1)
                    dve.wait_ge(gs["bound"], 2)
                    nc.vector.tensor_tensor(bound[:, 4, :], bound[:, 1, :], bound[:, 3, :], ALU.mult)
                    nc.vector.tensor_tensor(bound[:, 5, :], bound[:, 2, :], bound[:, 3, :], ALU.mult).then_inc(gs["bound"], 1)
                    nc.vector.memset(scores[:], 0.0)
                    nc.vector.memset(p_scores[:], 0.0)
                    nc.vector.memset(k_end_tok[:], 0.0)
                    for d in range(2):
                        last = nc.vector.memset(state[:, d, ORDER[d][0], :], 0.0)
                    last.then_inc(gs["zeroed"], 1)
                    dve.wait_ge(gs["zeroed"], 1)
                    dve.wait_ge(gs["bound"], 3)
                    dve.wait_ge(gs["tables"], 32)
                    links = 0
                    for h in range(GLA_H):
                        for d in range(2):
                            n = 2 * h + d
                            f = keep[:, GLA_H * d + h, :]
                            nc.vector.tensor_scalar(f, f, bound[:, 5, h:h + 1], bound[:, 4, h:h + 1], ALU.mult, ALU.add)\
                                .then_inc(gs["f"], 1)
                            dve.wait_ge(gs["ln"], n + 1)
                            nc.vector.tensor_scalar(f, f, -1.0, 1.0, ALU.mult, ALU.add).then_inc(gs["k"], 1)
                            dve.wait_ge(gs["exp"], n)
                            way = slice(None, None, 1 if d == 0 else -1)
                            nc.vector.tensor_tensor_scan(cum[:, way], restart[:, d, way], log_f[:, way], 0.0,
                                                         ALU.mult, ALU.add).then_inc(gs["cum"], 1)
                            dve.wait_ge(gs["cum"], n + 1)
                            nc.vector.tensor_tensor(by_chunk(to_ref[:]), by_chunk(cum[:]), at_chunk(cum[:], REF[d]),
                                                    ALU.subtract)
                            nc.vector.tensor_tensor(by_chunk(log_f[:]), at_chunk(cum[:], LAST[d]), by_chunk(cum[:]),
                                                    ALU.subtract).then_inc(gs["dist"], 1)
                            dve.wait_ge(gs["exp"], n + 1)
                            nc.vector.tensor_tensor(q_ref[:], q_ref[:], q_silu[:, h, :], ALU.mult)
                            nc.vector.tensor_tensor(q_cum[:, d, :], q_cum[:, d, :], q_silu[:, h, :], ALU.mult)\
                                .then_inc(gs["q_scaled"], 1)
                            if h >= 1:
                                dve.wait_ge(gs["out"], h)
                            dve.wait_ge(gs["scores"], n + 1)
                            for odd in range(2):
                                part = slice(64 * odd, 64 * odd + 64)
                                last = nc.vector.copy_predicated(
                                    scores[part, d, odd:CH:2, :],
                                    tri64[part, d:d + 1, :].bitcast(U32).broadcast_to([64, CH // 2, 64]),
                                    p_scores[part, 0:CH * 32].rearrange("p (c n) -> p c n", n=64))
                            last.then_inc(gs["masked"], 1)
                            dve.wait_ge(gs["kv"], n + 1)
                            for a, b in zip(ORDER[d], ORDER[d][1:]):
                                last = nc.vector.scalar_tensor_tensor(
                                    state[:, d, b, :], state[:, d, a, :], decay[:, d, a:a + 1],
                                    p_kv[:, a * P:(a + 1) * P], ALU.mult, ALU.add).then_inc(gs["link"], 1)
                                links += 1
                                dve.wait_ge(gs["link"], links)
                            nc.vector.engine_nop().then_inc(gs["states"], 1)

                @block.scalar
                def _(act):
                    act.wait_ge(gs["top"], 2)
                    nc.scalar.activation(bound[:, 1:3, :], bound[:, 1:3, :], ACT.Exp).then_inc(gs["bound_exp"], 1)
                    for h in range(GLA_H):
                        for d in range(2):
                            n = 2 * h + d
                            if n == 0:
                                act.wait_ge(gs["zeroed"], 1)
                            act.wait_ge(gs["f"], n + 1)
                            nc.scalar.activation(log_f[:], keep[:, GLA_H * d + h, :], ACT.Ln).then_inc(gs["ln"], 1)
                            act.wait_ge(gs["dist"], n + 1)
                            wait(act, gs["scores"], n)
                            wait(act, gs["turned"], n)
                            wait(act, gs["out"], h)
                            nc.scalar.activation(q_ref[:], to_ref[:], ACT.Exp)
                            nc.scalar.activation(k_ref[:], to_ref[:], ACT.Exp, scale=-1.0)
                            nc.scalar.activation(q_cum[:, d, :], cum[:], ACT.Exp)
                            nc.scalar.activation(decay[:, d, :], by_chunk(cum[:])[:, :, LAST[d]], ACT.Exp)
                            nc.scalar.activation(k_end[:], log_f[:], ACT.Exp).then_inc(gs["exp"], 1)
                            act.wait_ge(gs["turned"], n + 1)
                            wait(act, gs["kv"], n)
                            for odd in range(2):
                                part = slice(64 * odd, 64 * odd + 64)
                                last = nc.scalar.copy(k_end_tok[part, odd:CH:2, :],
                                                      p_turned[part, 0:TOK].rearrange("p (c n) -> p c n", n=P))
                            last.then_inc(gs["turned_read"], 1)
                        act.wait_ge(gs["out"], h + 1)
                        nc.scalar.copy(mixed_0[:, 4 + h, :], p_out[:, 0:TOK]).then_inc(gs["out_read"], 1)

                @block.gpsimd
                def _(pool):
                    for h in range(GLA_H):
                        for d in range(2):
                            n = 2 * h + d
                            k = keep[:, GLA_H * d + h, :]
                            pool.wait_ge(gs["k"], n + 1)
                            pool.wait_ge(gs["exp"], n + 1)
                            nc.gpsimd.tensor_tensor(k_end[:], k_end[:], k, ALU.mult).then_inc(gs["k_scaled"], 1)
                            nc.gpsimd.tensor_tensor(k_ref[:], k_ref[:], k, ALU.mult).then_inc(gs["k_scaled"], 1)

                @block.tensor
                def _(pe):
                    pe.wait_ge(gs["zeroed"], 1)
                    for h in range(GLA_H):
                        for d in range(2):
                            n = 2 * h + d
                            pe.wait_ge(gs["k_scaled"], 2 * n + 2)
                            wait(pe, gs["turned_read"], n)
                            for b in range(TOK // P):
                                mm = nc.tensor.transpose(p_turned[:, b * P:(b + 1) * P], k_end[:, b * P:(b + 1) * P], ident[:])
                            mm.then_inc(gs["turned"], 1)
                            pe.wait_ge(gs["q_scaled"], n + 1)
                            wait(pe, gs["masked"], n)
                            for c in range(CH):
                                for half in range(2):
                                    key = c * 64 + 32 * half
                                    first, width = (0, 64) if half == d else (32 * half, 32)
                                    part, col = slice(key % P, key % P + 32), (c // 2) * 64 + first
                                    mm = nc.tensor.matmul(p_scores[part, col:col + width], k_ref[:, key:key + 32],
                                                          q_ref[:, c * 64 + first:c * 64 + first + width],
                                                          start=True, stop=True, tile_position=(0, key % P))
                            mm.then_inc(gs["scores"], 1)
                            pe.wait_ge(gs["turned_read"], n + 1)
                            wait(pe, gs["states"], n)
                            for c in range(CH):
                                mm = nc.tensor.matmul(p_kv[:, c * P:(c + 1) * P], k_end_tok[:, c, :],
                                                      i_tok[:, c // 2, h * P:(h + 1) * P], start=True, stop=True)
                            mm.then_inc(gs["kv"], 1)
                        pe.wait_ge(gs["masked"], 2 * h + 2)
                        pe.wait_ge(gs["states"], 2 * h + 2)
                        wait(pe, gs["out_read"], h)
                        for c in range(CH):
                            tok = slice(c * 64, c * 64 + 64)
                            for d in range(2):
                                nc.tensor.matmul(p_out[:, tok], state[:, d, c, :], q_cum[:, d, tok], start=d == 0, stop=False)
                            for d in range(2):
                                mm = nc.tensor.matmul(p_out[:, tok], i_tok[:, c // 2, h * P:(h + 1) * P],
                                                      scores[:, d, c, :], start=False, stop=d == 1)
                        mm.then_inc(gs["out"], 1)

        head_norm("hgrn_norm", GLA_H, 1, TOK, lambda h, j: mixed_0[:, 4 + h, :], cols("hgrn_g"),
                  lambda h, j: g_silu[:, h, :])
        gla.close()

        with ExitStack() as scope:
            m_hi = sb(scope, "mixed_0_hi", [P, DC, TOK], F32R)
            m_lo = sb(scope, "mixed_0_lo", [P, DC, TOK], F32R)
            cut(mixed_0, m_hi, m_lo, DC)
            linear("eo", m_hi, m_lo, feature_units(ALL), None,
                   add_residual(ALL, [gates_of(0, 0, 0), gates_of(0, 0, 1)], 2))
        mix.close()

        with ExitStack() as scope:
            f_hi = sb(scope, "norm_b_hi", [P, DC, TOK], F32R)
            f_lo = sb(scope, "norm_b_lo", [P, DC, TOK], F32R)
            norm_split(x_all, [group(0, 1, 0, 0, LAT), group(0, 1, 1, LAT, CTX)], f_hi, f_lo)
            feed_forward(0, f_hi, f_lo, ALL, add_residual(ALL, [gates_of(0, 1, 0), gates_of(0, 1, 1)], 1))

        ret = ExitStack()
        ret_keys = ExitStack()
        k_ctx1 = sb(ret_keys, "ret_k_ctx", [P, DC, CTX])
        v_tok = sb(ret_keys, "ret_v", [P, TOK // P, 2048])
        with ExitStack() as scope:
            c_hi = sb(scope, "norm_c_hi", [P, DC, CTX], F32R)
            c_lo = sb(scope, "norm_c_lo", [P, DC, CTX], F32R)
            norm_split(lambda c, s, m: x_ctx[0][:, c, s:s + m], [group(1, 0, 1, 0, CTX)], c_hi, c_lo)
            linear("ckv0", c_hi, c_lo, feature_units([(0, CTX)]), copy_units(k_ctx1, 0))
            linear("ckv1", c_hi, c_lo, token_units(2), copy_token_units(v_tok, 2, LAT // P))
        ctx_scope.close()

        normed_1 = ExitStack()
        n1_hi = sb(normed_1, "norm_d_hi", [P, DC, LAT], F32R)
        n1_lo = sb(normed_1, "norm_d_lo", [P, DC, LAT], F32R)

        def x_only(c, s, m):
            return x_lat[:, c, s:s + m]

        norm_split(x_only, [group(1, 0, 0, 0, LAT)], n1_hi, n1_lo)
        qk_ret = sb(ret, "ret_qk", [P, 2 * DC, LAT])
        with ExitStack() as scope:
            rope = sb(scope, "ret_rope", [P, 2, LAT])
            part = sb(scope, "ret_rope_parts", [P, 4, LAT])
            with stage_block() as block:
                @block.sync
                def _(sp):
                    sp.dma_start(rope[:], io["retrope"]).then_inc(rope_loaded, 16)
                    sp.wait_ge(rope_loaded, 16)

            def evac_rope(dve, t, j, count, res):
                dve.wait_ge(rope_turned, t + 1)
                for u in range(2):
                    dve.wait_ge(unit_done, count(u))
                    nc.vector.tensor_tensor(part[:, 2 * u, :], res[u][:, 0, :], rope[:, 0, :], ALU.mult)
                    nc.vector.tensor_tensor(part[:, 2 * u + 1, :], res[u][:, 0, :], rope[:, 1, :], ALU.mult)\
                        .then_inc(unit_free, 1)
                dve.wait_ge(unit_free, count(1))
                nc.vector.tensor_tensor(qk_ret[:, bass.ds(2 * t, 1), :].rearrange("p o n -> p (o n)"),
                                        part[:, 0, :], part[:, 3, :], ALU.subtract)
                nc.vector.tensor_tensor(qk_ret[:, bass.ds(2 * t + 1, 1), :].rearrange("p o n -> p (o n)"),
                                        part[:, 2, :], part[:, 1, :], ALU.add).then_inc(rope_turned, 1)

            linear("rqk", n1_hi, n1_lo, feature_units(ONLY_LAT), None, evac_rope)
        linear("rv", n1_hi, n1_lo, token_units(4), copy_token_units(v_tok, 4))

        KB = TOK // P

        def ret_out(h, j):
            return qk_ret[:, 2 * h + j if j < 2 else 8 + 2 * h + j - 2, :]

        rs = {k: sem("ret_" + k) for k in ("table_0", "table_1", "scores", "decayed", "mixed", "mixed_read")}
        with ExitStack() as scope:
            table = sb(scope, "ret_decay", [P, 2, 12 * P])
            decayed = sb(scope, "ret_decayed", [P, 3, LAT])
            p_scores = psum(scope, "ret_p_scores", [P, 2, 512])
            p_mixed = psum(scope, "ret_p_mixed", [P, 4, 512])
            with stage_block() as block:
                @block.sync
                def _(sp):
                    for h in range(RET_H):
                        if h >= 2:
                            sp.wait_ge(rs["decayed"], (h - 1) * KB)
                        sp.dma_start(table[:, h % 2, :], io["decay"][h]).then_inc(rs[f"table_{h % 2}"], 16)

                @block.tensor
                def _(pe):
                    def scores(n):
                        h, b = divmod(n, KB)
                        if n >= 2:
                            pe.wait_ge(rs["decayed"], n - 1)
                        for j in range(2):
                            k = qk_ret[:, 8 + 2 * h + j, b * P:(b + 1) * P] if b < 4 else \
                                k_ctx1[:, 2 * h + j, (b - 4) * P:(b - 3) * P]
                            mm = nc.tensor.matmul(p_scores[:, n % 2, :], k, qk_ret[:, 2 * h + j, :],
                                                  start=j == 0, stop=j == 1)
                        mm.then_inc(rs["scores"], 1)

                    scores(0)
                    for n in range(RET_H * KB):
                        h, b = divmod(n, KB)
                        if n + 1 < RET_H * KB:
                            scores(n + 1)
                        pe.wait_ge(rs["decayed"], n + 1)
                        if b == 0 and h >= 1:
                            pe.wait_ge(rs["mixed_read"], h)
                        for e in range(4):
                            mm = nc.tensor.matmul(p_mixed[:, e, :], v_tok[:, b, h * 512 + e * P:h * 512 + (e + 1) * P],
                                                  decayed[:, n % 3, :], start=b == 0, stop=b == KB - 1)
                        mm.then_inc(rs["mixed"], 1)

                @block.vector
                def _(dve):
                    for n in range(RET_H * KB):
                        h, b = divmod(n, KB)
                        if b == 0:
                            dve.wait_ge(rs[f"table_{h % 2}"], 16 * (h // 2 + 1))
                        dve.wait_ge(rs["scores"], n + 1)
                        if n >= 3:
                            dve.wait_ge(rs["mixed"], n - 2)
                        at = (3 - b) * P if b < 4 else 7 * P + (5 - b) * P
                        nc.vector.tensor_tensor(decayed[:, n % 3, :], p_scores[:, n % 2, :],
                                                table[:, h % 2, at:at + LAT], ALU.mult).then_inc(rs["decayed"], 1)

                @block.scalar
                def _(act):
                    for h in range(RET_H):
                        act.wait_ge(rs["mixed"], (h + 1) * KB)
                        for e in range(4):
                            last = nc.scalar.copy(ret_out(h, e), p_mixed[:, e, :])
                        last.then_inc(rs["mixed_read"], 1)

        ret_keys.close()
        head_norm("ret_norm", RET_H, 4, LAT, ret_out)

        gate_sem = sem("gate_ready")
        gates_done = [0]

        def gate_linear(name, x_hi, x_lo, buf, func, other=None):
            n = shapes[name][0]
            base = gates_done[0]
            gates_done[0] += 2 * n
            with ExitStack() as scope:
                gate = sb(scope, f"{name}_gate", [P, 2, LAT])
                gated = sem(f"{name}_gated") if other is not None else None

                def evac_act(act, t, j, count, res):
                    for u in range(2):
                        act.wait_ge(unit_done, count(u))
                        act.wait_ge(unit_free, count(0) - 1)
                        nc.scalar.activation(gate[:, u, :], res[u][:, 0, :], func).then_inc(gate_sem, 1)

                def evac_dve(dve, t, j, count, res):
                    for u in range(2):
                        b = buf[:, bass.ds(2 * t + u, 1), :].rearrange("p o n -> p (o n)")
                        dve.wait_ge(gate_sem, 2 * t + (base + u + 1))
                        if other is None:
                            nc.vector.tensor_tensor(b, b, gate[:, u, :], ALU.mult).then_inc(unit_free, 1)
                        else:
                            o = other[:, bass.ds(2 * t + u, 1), :].rearrange("p o n -> p (o n)")
                            nc.vector.tensor_tensor(b, b, gate[:, u, :], ALU.mult).then_inc(gated, 1)
                            dve.wait_ge(gated, 2 * t + (u + 1))
                            nc.vector.tensor_tensor(o, o, b, ALU.add).then_inc(unit_free, 1)

                linear(name, x_hi, x_lo, feature_units(ONLY_LAT), evac_act, evac_dve)

        gate_linear("rg", n1_hi, n1_lo, qk_ret, ACT.Silu)
        normed_1.close()
        with ExitStack() as scope:
            m_hi = sb(scope, "mixed_1_hi", [P, 2 * DC, LAT], F32R)
            m_lo = sb(scope, "mixed_1_lo", [P, 2 * DC, LAT], F32R)
            cut(qk_ret, m_hi, m_lo, 2 * DC)
            linear("ro", m_hi, m_lo, [("F", 0, ONLY_LAT)], None, add_residual(ONLY_LAT, [gates_of(1, 0, 0)], 1))
        ret.close()
        with ExitStack() as scope:
            f_hi = sb(scope, "norm_e_hi", [P, DC, LAT], F32R)
            f_lo = sb(scope, "norm_e_lo", [P, DC, LAT], F32R)
            norm_split(x_only, [group(1, 1, 0, 0, LAT)], f_hi, f_lo)
            feed_forward(1, f_hi, f_lo, ONLY_LAT, add_residual(ONLY_LAT, [gates_of(1, 1, 0)], 1))

        two = ExitStack()
        t_hi = sb(two, "norm_f_hi", [P, DC, LAT], F32R)
        t_lo = sb(two, "norm_f_lo", [P, DC, LAT], F32R)
        norm_split(x_only, [(0, LAT, lambda c: scale_2[:, c:c + 1], lambda c: ada[:, c:c + 1])], t_hi, t_lo)

        NB = LAT // P
        y_a = sb(two, "y_a", [P, DC, LAT])
        dn = ExitStack()
        qkv = sb(dn, "dn_qkv", [P, 3 * DN_H, LAT])
        ba = sb(dn, "dn_beta_a", [P, NB, 16])
        with ExitStack() as scope:
            conv = sb(scope, "conv_sum", [P, 2, LAT])

            def evac_conv(dve, t, j, count, res):
                for u in range(2):
                    def tap(k):
                        c, _ = SMALL["conv"]
                        return small[:, bass.ds(8 * t + (c + 4 * u + k), 1)]

                    dve.wait_ge(unit_done, count(u))
                    dve.wait_ge(silu_sem, 2 * t + 2)
                    nc.vector.tensor_scalar(conv[:, u, :], res[u][:, 0, :], tap(3), None, ALU.mult).then_inc(conv_sem, 1)
                    for k in (2, 1, 0):
                        dve.wait_ge(conv_sem, 8 * t + (4 * u + 3 - k))
                        lag = 3 - k
                        last = nc.vector.scalar_tensor_tensor(conv[:, u, lag:], res[u][:, 0, 0:LAT - lag], tap(k),
                                                              conv[:, u, lag:], ALU.mult, ALU.add)
                        last.then_inc(conv_sem, 1)
                    dve.wait_ge(conv_sem, 8 * t + (4 * u + 4))
                    dve.sem_inc(unit_free, 1)

            def evac_silu(act, t, j, count, res):
                for u in range(2):
                    act.wait_ge(conv_sem, 8 * t + (4 * u + 4))
                    nc.scalar.activation(qkv[:, bass.ds(2 * t + u, 1), :].rearrange("p o n -> p (o n)"), conv[:, u, :],
                                         ACT.Silu).then_inc(silu_sem, 1)

            linear("dqkv", t_hi, t_lo, feature_units(ONLY_LAT), evac_silu, evac_conv)

        def evac_ba(act, t, j, count, res):
            for b in range(NB):
                act.wait_ge(unit_done, count(b))
                nc.scalar.copy(ba[:, b, :], res[b][:, 0, 0:16]).then_inc(unit_free, 1)

        linear("dba", t_hi, t_lo, [("T", slice(b * P, (b + 1) * P), 0, 16) for b in range(NB)], evac_ba)

        dc = {k: sem("dn_" + k) for k in ("tables", "a", "abs", "exp", "log", "g", "cum", "ready")}
        beta = sb(dn, "dn_beta", [P, NB, DN_H])
        g_tok = sb(dn, "dn_g", [P, NB, DN_H])
        g_cum = sb(dn, "dn_g_cum", [P, NB, DN_H])
        upper = sb(dn, "upper", [P, P])
        levels = sb(dn, "levels", [P, 7, P])
        with ExitStack() as scope:
            a_in = sb(scope, "dn_a_in", [P, NB, DN_H])
            a_abs = sb(scope, "dn_a_abs", [P, NB, DN_H])
            rate = sb(scope, "dn_rate", [P, DN_H])
            p_cum = psum(scope, "dn_p_cum", [P, NB * DN_H])

            def per_head(ap):
                return ap.rearrange("p (o h) -> p o h", o=1).broadcast_to([P, NB, DN_H])

            with stage_block() as block:
                @block.sync
                def _(sp):
                    sp.dma_start(upper[:], io["upper"]).then_inc(dc["tables"], 16)
                    sp.dma_start(levels[:], io["levels"]).then_inc(dc["tables"], 16)
                    sp.wait_ge(dc["tables"], 32)

                @block.scalar
                def _(act):
                    nc.scalar.activation(beta[:], ba[:, :, 0:DN_H], ACT.Sigmoid)
                    nc.scalar.activation(rate[:], cols("a_log"), ACT.Exp)
                    act.wait_ge(dc["a"], 1)
                    nc.scalar.activation(a_abs[:], a_in[:], ACT.Abs).then_inc(dc["abs"], 1)
                    act.wait_ge(dc["abs"], 1)
                    nc.scalar.activation(a_abs[:], a_abs[:], ACT.Exp, scale=-1.0).then_inc(dc["exp"], 1)
                    act.wait_ge(dc["exp"], 1)
                    nc.scalar.activation(a_abs[:], a_abs[:], ACT.Ln, bias=1.0).then_inc(dc["log"], 1)

                @block.vector
                def _(dve):
                    nc.vector.tensor_tensor(a_in[:], ba[:, :, DN_H:2 * DN_H], per_head(cols("dt_bias")), ALU.add)\
                        .then_inc(dc["a"], 1)
                    dve.wait_ge(dc["log"], 1)
                    nc.vector.scalar_tensor_tensor(a_in[:], a_in[:], 0.0, a_abs[:], ALU.max, ALU.add).then_inc(dc["g"], 1)
                    dve.wait_ge(dc["g"], 1)
                    nc.vector.scalar_tensor_tensor(g_tok[:], a_in[:], -1.0, per_head(rate[:]), ALU.mult, ALU.mult)\
                        .then_inc(dc["g"], 1)
                    dve.wait_ge(dc["cum"], 1)
                    nc.vector.tensor_copy(g_cum[:].rearrange("p c h -> p (c h)"), p_cum[:]).then_inc(dc["ready"], 1)

                @block.tensor
                def _(pe):
                    pe.wait_ge(dc["tables"], 32)
                    pe.wait_ge(dc["g"], 2)
                    nc.tensor.matmul(p_cum[:], upper[:], g_tok[:].rearrange("p c h -> p (c h)"), start=True, stop=True)\
                        .then_inc(dc["cum"], 1)

        d = {k: sem("delta_" + k) for k in (
            "columns", "squares", "sums", "roots", "rstd", "unit", "spread", "distances", "exps", "small", "products",
            "turned", "tokens", "grams", "masked", "lower", "eye", "join", "half", "half_read", "step", "next",
            "solved", "solved_read", "seen", "written", "fresh", "stored", "out", "out_read", "gram_read")}
        pair_scope = ExitStack()

        def two_of(name, shape, count=2):
            return [sb(pair_scope, f"delta_{name}_{a}", shape) for a in range(count)]

        g_col, c_col, b_col = (two_of(n, [P, NB]) for n in ("g_col", "c_col", "b_col"))
        last_col, end_col, bg_col = (two_of(n, [P, NB]) for n in ("last_col", "end_col", "bg_col"))
        root = two_of("root", [P, 2, LAT])
        (q_unit, k_unit, v_copy, grow, low, high, k_beta, k_end_t, v_beta, join, inv, inv_t, half_t, fresh) = (
            two_of(n, [P, LAT]) for n in ("q_unit", "k_unit", "v_copy", "grow", "low", "high", "k_beta", "k_end",
                                         "v_beta", "join", "inv", "inv_t", "half_t", "fresh"))
        state2 = two_of("state", [P, P])
        banks = [[psum(pair_scope, f"delta_p{a}{b}", [P, LAT]) for b in range(4)] for a in range(2)]

        def ch(ap, c):
            return ap[:, c * P:(c + 1) * P]

        def chunks(ap):
            return ap.rearrange("p (c n) -> p c n", n=P)

        def over_cols(ap):
            return ap.rearrange("p (c o) -> p c o", o=1).broadcast_to([P, NB, P])

        def over_chunks(ap):
            return ap.rearrange("p (o n) -> p o n", o=1).broadcast_to([P, NB, P])

        with nc.Fori(0, DN_H // 2) as pair:
            with stage_block() as block:
                @block.vector
                def _(dve):
                    for s in d.values():
                        dve.sem_clear(s)

            def head(a, part):
                return qkv[:, bass.ds(2 * pair + (8 * part + a), 1), :].rearrange("p o n -> p (o n)")

            with stage_block() as block:
                @block.scalar
                def _(act):
                    for a in range(2):
                        nc.scalar.activation(root[a][:, 0, :], head(a, 0), ACT.Square)
                        nc.scalar.activation(root[a][:, 1, :], head(a, 1), ACT.Square).then_inc(d["squares"], 1)
                    for a in range(2):
                        act.wait_ge(d["sums"], a + 1)
                        for r in range(2):
                            last = nc.scalar.activation(root[a][:, r, :], banks[a][r][:], ACT.Sqrt, bias=eps_col)
                        last.then_inc(d["roots"], 1)
                    for a in range(2):
                        act.wait_ge(d["distances"], a + 1)
                        nc.scalar.activation(grow[a][:], banks[a][2][:], ACT.Exp)
                        nc.scalar.activation(low[a][:], low[a][:], ACT.Exp, scale=-1.0)
                        nc.scalar.activation(high[a][:], high[a][:], ACT.Exp)
                        nc.scalar.activation(end_col[a][:], end_col[a][:], ACT.Exp)
                        nc.scalar.activation(bg_col[a][:], c_col[a][:], ACT.Exp)
                        nc.scalar.activation(last_col[a][:], last_col[a][:], ACT.Exp).then_inc(d["exps"], 1)
                    for m in range(7):
                        for a in range(2):
                            n = 2 * m + a
                            act.wait_ge(d["half"], n + 1)
                            nc.scalar.copy(half_t[a][:], banks[a][0][:]).then_inc(d["half_read"], 1)
                    for a in range(2):
                        act.wait_ge(d["solved"], a + 1)
                        nc.scalar.copy(half_t[a][:], banks[a][0][:])
                        nc.scalar.copy(join[a][:], banks[a][1][:]).then_inc(d["solved_read"], 1)
                    for a in range(2):
                        act.wait_ge(d["out"], a + 1)
                        nc.scalar.copy(y_a[:, bass.ds(2 * pair + a, 1), :].rearrange("p o n -> p (o n)"), banks[a][3][:])\
                            .then_inc(d["out_read"], 1)

                @block.vector
                def _(dve):
                    for a in range(2):
                        for dst, src in ((g_col, g_tok), (c_col, g_cum), (b_col, beta)):
                            last = nc.vector.tensor_copy(dst[a][:].rearrange("p (c o) -> p c o", o=1),
                                                         src[:, :, bass.ds(2 * pair + a, 1)])
                        last.then_inc(d["columns"], 1)
                        nc.vector.tensor_copy(v_copy[a][:], head(a, 2)).then_inc(d["small"], 1)
                    for a in range(2):
                        dve.wait_ge(d["roots"], a + 1)
                        nc.vector.reciprocal(root[a][:], root[a][:]).then_inc(d["rstd"], 1)
                        dve.wait_ge(d["rstd"], a + 1)
                        nc.vector.scalar_tensor_tensor(q_unit[a][:], head(a, 0), P ** -0.5, root[a][:, 0, :],
                                                       ALU.mult, ALU.mult)
                        nc.vector.tensor_tensor(k_unit[a][:], head(a, 1), root[a][:, 1, :], ALU.mult)\
                            .then_inc(d["unit"], 1)
                    for a in range(2):
                        dve.wait_ge(d["spread"], a + 1)
                        spread = banks[a][2]
                        dve.wait_ge(d["columns"], a + 1)
                        nc.vector.tensor_copy(last_col[a][:], spread[:, P - 1:LAT:P]).then_inc(d["small"], 1)
                        for c in range(NB):
                            nc.vector.tensor_scalar(ch(low[a], c), ch(spread, c), c_col[a][:, c:c + 1], 0.0,
                                                    ALU.subtract, ALU.max)
                            nc.vector.tensor_scalar(ch(high[a], c), ch(spread, c), c_col[a][:, c:c + 1], 0.0,
                                                    ALU.subtract, ALU.min)
                        dve.wait_ge(d["small"], 2 + a + 1)
                        nc.vector.tensor_tensor(end_col[a][:], last_col[a][:], c_col[a][:], ALU.subtract)\
                            .then_inc(d["distances"], 1)
                    for a in range(2):
                        dve.wait_ge(d["exps"], a + 1)
                        nc.vector.tensor_tensor(bg_col[a][:], bg_col[a][:], b_col[a][:], ALU.mult).then_inc(d["small"], 1)
                        nc.vector.tensor_tensor(grow[a][:], grow[a][:], q_unit[a][:], ALU.mult)
                        dve.wait_ge(d["turned"], a + 1)
                        dve.wait_ge(d["small"], 4 + a + 1)
                        keys, values = banks[a][0], banks[a][1]
                        nc.vector.tensor_tensor(chunks(k_beta[a][:]), chunks(keys[:]), over_cols(bg_col[a][:]), ALU.mult)
                        nc.vector.tensor_tensor(chunks(k_end_t[a][:]), chunks(keys[:]), over_cols(end_col[a][:]), ALU.mult)
                        nc.vector.tensor_tensor(chunks(v_beta[a][:]), chunks(values[:]), over_cols(b_col[a][:]), ALU.mult)\
                            .then_inc(d["tokens"], 1)
                    for a in range(2):
                        dve.wait_ge(d["grams"], a + 1)
                        dve.wait_ge(d["masked"], 2 * a + 2)
                        nc.vector.tensor_tensor(high[a][:], banks[a][3][:], high[a][:], ALU.mult)
                        nc.vector.tensor_tensor(low[a][:], banks[a][2][:], low[a][:], ALU.mult).then_inc(d["lower"], 1)
                    for m in range(7):
                        for a in range(2):
                            n = 2 * m + a
                            dve.wait_ge(d["step"], n + 1)
                            if m < 6:
                                nc.vector.tensor_tensor(inv[a][:], inv[a][:], banks[a][1][:], ALU.subtract)
                            nc.vector.tensor_tensor(inv_t[a][:], inv_t[a][:], banks[a][3][:], ALU.subtract)\
                                .then_inc(d["next"], 1)
                    for c in range(NB):
                        for a in range(2):
                            if c:
                                dve.wait_ge(d["seen"], 2 * (c - 1) + a + 1)
                                nc.vector.tensor_tensor(ch(fresh[a], c), ch(half_t[a], c), banks[a][0][:, 0:P], ALU.subtract)\
                                    .then_inc(d["fresh"], 1)
                            else:
                                dve.wait_ge(d["solved_read"], a + 1)
                                nc.vector.tensor_copy(ch(fresh[a], c), ch(half_t[a], c)).then_inc(d["fresh"], 1)
                        for a in range(2):
                            if c < NB - 1:
                                dve.wait_ge(d["written"], 2 * c + a + 1)
                                if c:
                                    nc.vector.scalar_tensor_tensor(state2[a][:], state2[a][:], last_col[a][:, c:c + 1],
                                                                   banks[a][1][:, 0:P], ALU.mult, ALU.add)\
                                        .then_inc(d["stored"], 1)
                                else:
                                    nc.vector.tensor_copy(state2[a][:], banks[a][1][:, 0:P]).then_inc(d["stored"], 1)

                @block.gpsimd
                def _(pool):
                    for a in range(2):
                        for m in (inv, inv_t):
                            nc.gpsimd.tensor_copy(chunks(m[a][:]), over_chunks(ident[:])).then_inc(d["eye"], 1)
                    for a in range(2):
                        pool.wait_ge(d["exps"], a + 1)
                        nc.gpsimd.tensor_tensor(chunks(high[a][:]), chunks(high[a][:]), over_chunks(upper[:]), ALU.mult)\
                            .then_inc(d["masked"], 1)
                        pool.wait_ge(d["columns"], a + 1)
                        nc.gpsimd.tensor_tensor(chunks(low[a][:]), chunks(low[a][:]), over_cols(b_col[a][:]), ALU.mult)\
                            .then_inc(d["masked"], 1)
                    for m in range(7):
                        for a in range(2):
                            n = 2 * m + a
                            pool.wait_ge(d["lower"], a + 1)
                            if m:
                                pool.wait_ge(d["half"], n - 1)
                            nc.gpsimd.tensor_tensor(chunks(join[a][:]), chunks(low[a][:]), over_chunks(levels[:, m, :]),
                                                    ALU.mult).then_inc(d["join"], 1)

                @block.tensor
                def _(pe):
                    for a in range(2):
                        pe.wait_ge(d["squares"], a + 1)
                        for r in range(2):
                            mm = nc.tensor.matmul(banks[a][r][:], ones[:], root[a][:, r, :], start=True, stop=True)
                        mm.then_inc(d["sums"], 1)
                        pe.wait_ge(d["columns"], a + 1)
                        for c in range(NB):
                            mm = nc.tensor.matmul(ch(banks[a][2], c), g_col[a][:, c:c + 1].broadcast_to([P, P]), upper[:],
                                                  start=True, stop=True)
                        mm.then_inc(d["spread"], 1)
                    for a in range(2):
                        pe.wait_ge(d["unit"], a + 1)
                        pe.wait_ge(d["small"], a + 1)
                        for c in range(NB):
                            nc.tensor.transpose(ch(banks[a][0], c), ch(k_unit[a], c), ident[:])
                        for c in range(NB):
                            mm = nc.tensor.transpose(ch(banks[a][1], c), ch(v_copy[a], c), ident[:])
                        mm.then_inc(d["turned"], 1)
                    for a in range(2):
                        pe.wait_ge(d["exps"], a + 1)
                        for c in range(NB):
                            nc.tensor.matmul(ch(banks[a][2], c), ch(k_unit[a], c), ch(k_unit[a], c), start=True, stop=True)
                        for c in range(NB):
                            mm = nc.tensor.matmul(ch(banks[a][3], c), ch(k_unit[a], c), ch(q_unit[a], c), start=True, stop=True)
                        mm.then_inc(d["grams"], 1)
                    pe.wait_ge(d["eye"], 4)
                    for a in range(2):
                        pe.wait_ge(d["tokens"], a + 1)
                    def half_step(m, a):
                        n = 2 * m + a
                        pe.wait_ge(d["join"], n + 1)
                        if m:
                            pe.wait_ge(d["next"], n - 1)
                        for c in range(NB):
                            mm = nc.tensor.matmul(ch(banks[a][0], c), ch(join[a], c), ch(inv_t[a], c), start=True, stop=True)
                        mm.then_inc(d["half"], 1)

                    def full_step(m, a):
                        n = 2 * m + a
                        pe.wait_ge(d["half_read"], n + 1)
                        for c in range(NB):
                            if m < 6:
                                nc.tensor.matmul(ch(banks[a][1], c), ch(half_t[a], c), ch(inv[a], c), start=True, stop=True)
                        for c in range(NB):
                            mm = nc.tensor.matmul(ch(banks[a][3], c), ch(inv[a], c), ch(half_t[a], c), start=True, stop=True)
                        mm.then_inc(d["step"], 1)

                    for m in range(7):
                        half_step(m, 0)
                        half_step(m, 1)
                        full_step(m, 0)
                        full_step(m, 1)
                    for a in range(2):
                        pe.wait_ge(d["next"], 12 + a + 1)
                        for c in range(NB):
                            nc.tensor.matmul(ch(banks[a][0], c), ch(inv_t[a], c), ch(v_beta[a], c), start=True, stop=True)
                        for c in range(NB):
                            mm = nc.tensor.matmul(ch(banks[a][1], c), ch(k_beta[a], c), ch(inv_t[a], c), start=True, stop=True)
                        mm.then_inc(d["solved"], 1)
                    for c in range(NB):
                        for a in range(2):
                            pe.wait_ge(d["solved_read"], a + 1)
                            if c:
                                pe.wait_ge(d["stored"], 2 * (c - 1) + a + 1)
                                nc.tensor.matmul(banks[a][0][:, 0:P], ch(join[a], c), state2[a][:], start=True, stop=True)\
                                    .then_inc(d["seen"], 1)
                        for a in range(2):
                            pe.wait_ge(d["fresh"], 2 * c + a + 1)
                            if c:
                                nc.tensor.matmul(ch(banks[a][3], c), state2[a][:], ch(grow[a], c), start=True, stop=False)
                            if c < NB - 1:
                                nc.tensor.matmul(banks[a][1][:, 0:P], ch(k_end_t[a], c), ch(fresh[a], c), start=True, stop=True)\
                                    .then_inc(d["written"], 1)
                            mm = nc.tensor.matmul(ch(banks[a][3], c), ch(fresh[a], c), ch(high[a], c), start=c == 0, stop=True)
                            if c == NB - 1:
                                mm.then_inc(d["out"], 1)
        pair_scope.close()
        dn.close()

        head_norm("dn_norm", DN_H, 1, LAT, lambda h, j: y_a[:, h, :], cols("dn_w"))
        gate_linear("dz", t_hi, t_lo, y_a, ACT.Silu)

        with ExitStack() as scope:
            m_hi = sb(scope, "delta_hi", [P, DC, LAT], F32R)
            m_lo = sb(scope, "delta_lo", [P, DC, LAT], F32R)
            cut(y_a, m_hi, m_lo, DC)
            linear("pa", m_hi, m_lo, feature_units(ONLY_LAT), copy_units(y_a, 0))
        gate_linear("ga", t_hi, t_lo, y_a, ACT.Sigmoid)

        WC = 6
        y_b = sb(two, "y_b", [P, WC, LAT])
        lse = sb(two, "dil_lse", [P, 4, 2 * WC])
        dil_scope = ExitStack()
        qk_t = sb(dil_scope, "dil_qk", [P, 2 * WC, P + LAT])
        v_t = sb(dil_scope, "dil_v", [P, 5, 2 * WC * 64])
        q_zero_t = sb(dil_scope, "dil_q_zero", [P, 2 * WC, P])
        near = sb(dil_scope, "dil_near", [P, 4, 2 * P])
        dil = sb(dil_scope, "dil_masks", [P, 2, P])
        dil_tables, dil_zeroed = sem("dil_tables"), sem("dil_zeroed")
        with stage_block() as block:
            @block.sync
            def _(sp):
                sp.dma_start(near[:], io["near"]).then_inc(dil_tables, 16)
                sp.dma_start(dil[:], io["dil"]).then_inc(dil_tables, 16)
                sp.wait_ge(dil_tables, 32)

            @block.vector
            def _(dve):
                nc.vector.memset(qk_t[:, :, 0:P], 0.0)
                nc.vector.memset(v_t[:, 0, :], 0.0)
                nc.vector.memset(q_zero_t[:], 0.0).then_inc(dil_zeroed, 1)

        def evac_tqk(act, t, j, count, res):
            for u in range(2):
                act.wait_ge(unit_done, count(u))
                nc.scalar.copy(qk_t[:, bass.ds(2 * t + u, 1), P:P + LAT], res[u][:, 0:1, :]).then_inc(unit_free, 1)

        def value_units(t):
            return [("T", slice(b * P, (b + 1) * P) if t == 0 else slice(b, LAT, 4), 0, 256) for b in range(4)]

        linear("tqk", t_hi, t_lo, feature_units(ONLY_LAT), evac_tqk)
        linear("tv", t_hi, t_lo, value_units, copy_token_units(v_t, 4, 1))

        def strided(first):
            return bass.ds(first, P, 4)

        def dilated_head(h):
            g, c = h // 4, h // 2
            cols64 = slice(64 * h, 64 * h + 64)

            def keys(i):
                if g == 0:
                    return [(0, 2 * P, qk_t[:, WC + c, bass.ds(i * P, 2 * P)],
                             near[:, bass.ds(i, 1), :].rearrange("p o n -> p (o n)"))]
                return [(0, P, qk_t[:, WC + c, strided(i + P)], dil[:, g - 1, :])]

            def values(i):
                return [v_t[:, bass.ds(i + b, 1), cols64].rearrange("p o n -> p (o n)")
                        for b in ((0, 1) if g == 0 else (1,))]

            return dict(q=q_zero_t[:, h, :], keys=keys, values=values, column=64 * h, sink=None)

        def dilated_queries(i):
            copies = []
            for half in range(2):
                part = slice(64 * half, 64 * half + 64)
                copies += [(q_zero_t[part, half:4:2, :], qk_t[part, 0:2, bass.ds(i * P + P, P)]),
                           (q_zero_t[part, 4 + half:12:2, :], qk_t[part, 2:WC, strided(i + P)])]
            return copies

        def dilated_results(i, p_out):
            out = p_out[:, 0:WC * P].rearrange("p (c n) -> p c n", n=P)
            return [(y_b[:, 0:2, bass.ds(i * P, P)], out[:, 0:2, :]), (y_b[:, 2:WC, strided(i)], out[:, 2:WC, :])]

        attend("dil", 4, [dilated_head(h) for h in range(2 * WC)], dilated_queries, dilated_results,
               2 * P, 2, WC * P, 64.0 ** -0.5, lse)
        dil_scope.close()

        gw = {k: sem("groups_" + k) for k in ("pair", "turned", "logs", "max", "shifted", "exp", "sum", "weights",
                                             "spread")}
        with ExitStack() as scope:
            pair_of = sb(scope, "groups_pair", [P, 2, P])
            logs = sb(scope, "groups_logs", [4, 3, LAT])
            top_log = sb(scope, "groups_top", [4, LAT])
            p_logs = psum(scope, "groups_p_logs", [P, 3, 512])
            p_spread = psum(scope, "groups_p_spread", [P, 5, 512])

            def over_groups(ap):
                return ap.rearrange("p (o n) -> p o n", o=1).broadcast_to([4, 3, LAT])

            with stage_block() as block:
                @block.sync
                def _(sp):
                    sp.dma_start(pair_of[:], io["pair"]).then_inc(gw["pair"], 16)

                @block.tensor
                def _(pe):
                    for g in range(3):
                        for i in range(4):
                            mm = nc.tensor.transpose(p_logs[0:4, g, i * P:(i + 1) * P], lse[:, i, 4 * g:4 * g + 4],
                                                     ident[:])
                    mm.then_inc(gw["turned"], 1)
                    pe.wait_ge(gw["pair"], 16)
                    pe.wait_ge(gw["weights"], 1)
                    for c in range(WC):
                        if c == 5:
                            pe.wait_ge(gw["spread"], 1)
                        nc.tensor.matmul(p_spread[:, c % 5, :], pair_of[0:4, c % 2, :], logs[:, c // 2, :],
                                         start=True, stop=True).then_inc(gw["turned"], 1)

                @block.scalar
                def _(act):
                    act.wait_ge(gw["shifted"], 1)
                    nc.scalar.activation(logs[:], logs[:], ACT.Exp).then_inc(gw["exp"], 1)

                @block.vector
                def _(dve):
                    dve.wait_ge(gw["turned"], 1)
                    nc.vector.tensor_copy(logs[:, 0, :], p_logs[0:4, 0, :])
                    nc.vector.tensor_copy(logs[:, 1:3, :].rearrange("p g (n r) -> p g r n", r=4),
                                          p_logs[0:4, 1:3, :].rearrange("p g (r n) -> p g r n", r=4))\
                        .then_inc(gw["logs"], 1)
                    dve.wait_ge(gw["logs"], 1)
                    nc.vector.tensor_tensor(top_log[:], logs[:, 0, :], logs[:, 1, :], ALU.max).then_inc(gw["max"], 1)
                    dve.wait_ge(gw["max"], 1)
                    nc.vector.tensor_tensor(top_log[:], top_log[:], logs[:, 2, :], ALU.max).then_inc(gw["max"], 1)
                    dve.wait_ge(gw["max"], 2)
                    nc.vector.tensor_tensor(logs[:], logs[:], over_groups(top_log[:]), ALU.subtract)\
                        .then_inc(gw["shifted"], 1)
                    dve.wait_ge(gw["exp"], 1)
                    nc.vector.tensor_tensor(top_log[:], logs[:, 0, :], logs[:, 1, :], ALU.add).then_inc(gw["sum"], 1)
                    dve.wait_ge(gw["sum"], 1)
                    nc.vector.tensor_tensor(top_log[:], top_log[:], logs[:, 2, :], ALU.add).then_inc(gw["sum"], 1)
                    dve.wait_ge(gw["sum"], 2)
                    nc.vector.reciprocal(top_log[:], top_log[:]).then_inc(gw["sum"], 1)
                    dve.wait_ge(gw["sum"], 3)
                    nc.vector.tensor_tensor(logs[:], logs[:], over_groups(top_log[:]), ALU.mult)\
                        .then_inc(gw["weights"], 1)
                    for c in range(WC):
                        dve.wait_ge(gw["turned"], c + 2)
                        nc.vector.tensor_tensor(y_b[:, c, :], y_b[:, c, :], p_spread[:, c % 5, :], ALU.mult)\
                            .then_inc(gw["spread"], 1)

        gate_linear("tz", t_hi, t_lo, y_b, ACT.Silu)

        merge = ExitStack()
        y_proj = sb(merge, "y_b_projected", [P, DC, LAT])
        with ExitStack() as scope:
            m_hi = sb(scope, "dilated_hi", [P, WC, LAT], F32R)
            m_lo = sb(scope, "dilated_lo", [P, WC, LAT], F32R)
            cut(y_b, m_hi, m_lo, WC)
            linear("pb", m_hi, m_lo, feature_units(ONLY_LAT), copy_units(y_proj, 0))
        gate_linear("gb", t_hi, t_lo, y_proj, ACT.Sigmoid, y_a)
        merge.close()
        with ExitStack() as scope:
            m_hi = sb(scope, "merged_hi", [P, DC, LAT], F32R)
            m_lo = sb(scope, "merged_lo", [P, DC, LAT], F32R)
            cut(y_a, m_hi, m_lo, DC)
            linear("wo", m_hi, m_lo, feature_units(ONLY_LAT), None, add_residual(ONLY_LAT, [ada[:, 16:24]], 2))
        two.close()
        head_norm("final", 1, DC, LAT, lambda h, j: x_lat[:, j, :], lambda j: cols("final_w")[:, j:j + 1])
        with stage_block() as block:
            @block.sync
            def _(sp):
                sp.dma_start(io["y"], x_lat[:]).then_inc(stored, 16)
                sp.wait_ge(stored, 16)


def layout(inp):
    f = {k: np.asarray(v) for k, v in inp.items()}

    def fm(a):
        return np.ascontiguousarray(a.reshape(a.shape[0] // P, P, -1).transpose(1, 0, 2))

    def col(a):
        return a.reshape(-1, P).T

    def rows(a):
        return np.broadcast_to(a.reshape(1, -1), (P, a.size))

    def tiles(w, nt=256):
        k, n = w.shape
        w = w.reshape(k // P, P, n // nt, nt).transpose(2, 1, 0, 3)
        return np.ascontiguousarray(w).reshape(n // nt, P, -1)

    out = dict(constants())
    out["x"] = fm(f["x"][0].T)
    out["ctx"] = fm(f["ctx"][0].T)
    parts = dict(
        mod_b=col(f["mod_b"].reshape(-1)), ada_b=col(f["ada_b_2"][0]), norm_g=col(f["norm_g"].reshape(-1)),
        norm_w=col(f["norm_w_2"][0]), final_w=col(f["final_norm_w_2"]),
        qk_g=np.tile(f["attn_qk_norm_g"][0].T, (2, 1)), sink=rows(f["attn_sink"][0]),
        lb=col(f["hgrn_lb"].reshape(-1)), hgrn_g=f["hgrn_out_norm_g"][0].reshape(P, 1),
        conv=f["conv_w_2"][0].reshape(4, 24, P).transpose(2, 1, 0).reshape(P, 96),
        a_log=rows(f["a_log_2"][0]), dt_bias=rows(f["dt_bias_2"][0]), dn_w=f["dn_norm_w_2"][0].reshape(P, 1),
        cond=np.concatenate([col(f["c"][0]), col(f["c_ctx"])], 1), cond_2=col(f["c_2"][0]),
        eps=np.full((P, 1), EPS, np.float32))
    out["small"] = np.concatenate([parts[k] for k in SMALL], axis=1)

    out["w_mod"] = np.concatenate([tiles(f["mod_w"][0]), tiles(f["mod_w"][1]), tiles(f["ada_w_2"][0])])
    w = f["even_w_in"][0]
    wq = w[:, 0:512].reshape(D, 2, 4, 64).transpose(0, 2, 1, 3).reshape(D, 512)
    out["w_aq"], out["w_akv"] = tiles(wq), tiles(w[:, 512:768])
    out["w_bq"], out["w_bf"] = tiles(w[:, 768:1280]), tiles(w[:, 1280:2304])
    out["w_bi"], out["w_bg"] = tiles(w[:, 2304:2816]), tiles(w[:, 2816:3328])
    w = f["even_w_out"][0]
    wa = w[0:512].reshape(2, 4, 64, D).transpose(1, 0, 2, 3).reshape(512, D)
    out["w_eo"] = tiles(np.concatenate([wa, w[512:]], axis=0))
    for layer in (0, 1):
        w = f["ffn_w_in"][layer].reshape(DC, P, 2, FFN // P, P).transpose(3, 1, 0, 2, 4)
        w = np.ascontiguousarray(w).reshape(FFN // P, P, -1)
        wo = f["ffn_w_out"][layer].reshape(2, HALF * P, D)
        for half in (0, 1):
            out[f"w_f{layer}i{half}"] = w[half * HALF:(half + 1) * HALF]
            out[f"w_f{layer}o{half}"] = tiles(wo[half], P)
    w = f["odd_w_in"][0]
    out["w_rqk"], out["w_rv"] = tiles(w[:, 0:2048]), tiles(w[:, 2048:4096])
    wg = w[:, 4096:].reshape(D, RET_H, 2, 256).transpose(0, 2, 1, 3).reshape(D, 2048)
    out["w_rg"] = tiles(wg)
    wo = f["odd_w_out"][0].reshape(RET_H, 2, 256, D).transpose(1, 0, 2, 3).reshape(2048, D)
    out["w_ro"] = tiles(wo, P)
    w = f["w_in_2"][0]
    out["w_dqkv"], out["w_dz"], out["w_dba"] = tiles(w[:, 0:3072]), tiles(w[:, 3072:4096]), tiles(w[:, 4096:4112], 16)
    out["w_tqk"], out["w_tv"], out["w_tz"] = tiles(w[:, 4112:5648]), tiles(w[:, 5648:6416]), tiles(w[:, 6416:7184])
    out["w_ga"], out["w_gb"] = tiles(w[:, 7184:8208]), tiles(w[:, 8208:9232])
    out["w_pa"], out["w_pb"], out["w_wo"] = tiles(f["w_proj_a_2"][0]), tiles(f["w_proj_b_2"][0]), tiles(f["w_out_2"][0])
    return out


def kernel(**inputs):
    import concourse.bacc as bacc
    from concourse.bass_utils import run_bass_kernel_spmd

    nc = bacc.Bacc("TRN2", target_bir_lowering=False, num_devices=1)
    arrays = {"in_" + k: np.ascontiguousarray(a) for k, a in layout(inputs).items()}
    io = {k[3:]: nc.dram_tensor(k, a.shape, mybir.dt.from_np(a.dtype), kind="ExternalInput").ap()
          for k, a in arrays.items()}
    io["y"] = nc.dram_tensor("y", (P, DC, LAT), F32, kind="ExternalOutput").ap()
    program(nc, io)
    got = run_bass_kernel_spmd(nc, [arrays], core_ids=[0]).results[0]["y"]
    return np.ascontiguousarray(got.transpose(2, 1, 0).reshape(1, LAT, D))
```

```python
from contextlib import ExitStack

import numpy as np

import concourse.bass as bass
from concourse import mybir

F32 = mybir.dt.float32
F32R = mybir.dt.float32r
U32 = mybir.dt.uint32
ALU = mybir.AluOpType
ACT = mybir.ActivationFunctionType
AX_X = mybir.AxisListType.X

P = 128
D = 1024
DC = D // P
LAT, CTX = 512, 256
TOK = LAT + CTX
EPS = 1e-6
FFN = 2816
HALF = FFN // P // 2
SLOT = 2048
RET_H = 4
GLA_H = 4
DN_H = 8
NEG = -1e30


def constants():
    f = np.float32
    p = np.arange(P)
    out = {}
    out["ident"] = np.eye(P, dtype=f)
    out["ones"] = np.ones((P, P), f)
    out["ones64"] = np.kron(np.eye(2), np.ones((64, 64))).astype(f)
    rot = np.zeros((P, P), f)
    for b in (0, 64):
        for i in range(32):
            rot[b + i, b + 32 + i] = -1.0
            rot[b + 32 + i, b + i] = 1.0
    out["rotT"] = np.ascontiguousarray(rot.T)
    out["upper"] = (p[:, None] <= p[None, :]).astype(f)
    tok = np.arange(LAT)
    inv = f(10000.0) ** (-np.arange(16, dtype=f) / f(16))
    ang = np.concatenate([(tok // 64).astype(f)[:, None] * inv, (tok % 64).astype(f)[:, None] * inv], axis=-1)
    out["axial"] = np.stack([np.tile(np.cos(ang).T, (4, 1)), np.tile(np.sin(ang).T, (4, 1))], 1).astype(f)
    theta = f(1.0) / (f(10000.0) ** np.linspace(0.0, 1.0, P, dtype=f))
    ang = tok.astype(f)[:, None] * theta
    out["retrope"] = np.stack([np.cos(ang).T, np.sin(ang).T], 1).astype(f)
    q, k = p[:, None], np.arange(3 * P)[None, :]
    win = np.where((k >= q) & (k <= q + 2 * P), 0.0, NEG)
    four = np.stack([win] * 4, 1)
    four[:, 0, :P] = NEG
    four[:, 3, 2 * P:] = NEG
    out["window"] = four.astype(f)
    s, t = (p % 64)[:, None], np.arange(64)[None, :]
    out["tri64"] = np.stack([s <= t, s >= t], 1).astype(f)
    out["restart"] = np.broadcast_to((np.arange(TOK) % 64 != 0).astype(f), (P, TOK)).copy()
    g = np.log(1.0 - 2.0 ** (-5.0 - np.arange(RET_H, dtype=np.float64)))
    lat_u = (np.arange(7 * P) - 3 * P)[None, :] - p[:, None]
    ctx_u = (np.arange(5 * P) + P)[None, :] - p[:, None]
    tables = []
    for h in range(RET_H):
        fw, bw = g[h], g[RET_H - 1 - h]
        lat = np.where(lat_u >= 0, np.exp(fw * np.maximum(lat_u, 0)), 0.0)
        lat = lat + np.where(lat_u <= 0, np.exp(bw * np.maximum(-lat_u, 0)), 0.0)
        tables.append(np.concatenate([lat, np.exp(fw * ctx_u) + np.exp(bw * (LAT + CTX - ctx_u))], 1))
    out["decay"] = (np.stack(tables) * 256.0 ** -0.5).astype(f)
    lev = [((p[:, None] // (2 * b) == p[None, :] // (2 * b)) & (p[:, None] // b % 2 == 1)
            & (p[None, :] // b % 2 == 0)) for b in (1, 2, 4, 8, 16, 32, 64)]
    out["levels"] = np.stack(lev, 1).astype(f)
    k = np.arange(2 * P)[None, :]
    near = np.where((k >= q) & (k <= q + P), 0.0, NEG)
    first = np.where((k >= P) & (k <= q + P), 0.0, NEG)
    k = np.arange(P)[None, :]
    dil4 = np.where(k <= q, 0.0, NEG)
    dil16 = np.where((k <= q) & (k % 4 == q % 4), 0.0, NEG)
    out["near"] = np.stack([first, near, near, near], 1).astype(f)
    out["dil"] = np.stack([dil4, dil16], 1).astype(f)
    pair = np.zeros((P, 2, P), f)
    for s in range(4):
        pair[s, s // 2, (s % 2) * 64:(s % 2) * 64 + 64] = 1.0
    out["pair"] = pair
    return out


SMALL = {}
_at = 0
for _name, _width in (("mod_b", 96), ("ada_b", 24), ("norm_g", 32), ("norm_w", 8), ("final_w", 8),
                      ("qk_g", 2), ("sink", 8), ("lb", 8), ("hgrn_g", 1), ("conv", 96), ("a_log", 8),
                      ("dt_bias", 8), ("dn_w", 1), ("cond", 16), ("cond_2", 8), ("eps", 1)):
    SMALL[_name] = (_at, _at + _width)
    _at += _width
SMALLS = _at

STREAM = [("aq", 2, 8, 256), ("akv", 1, 8, 256), ("bq", 2, 8, 256),
          ("bg", 2, 8, 256), ("bf", 4, 8, 256), ("bi", 2, 8, 256), ("eo", 4, 8, 256)]
STREAM += [(f"f0{part}{half}", *shape) for half in (0, 1)
           for part, shape in (("i", (HALF, 8, 256)), ("o", (8, HALF, 128)))]
STREAM += [("ckv0", 4, 8, 256), ("ckv1", 8, 8, 256), ("rqk", 8, 8, 256), ("rv", 8, 8, 256),
           ("rg", 8, 8, 256), ("ro", 8, 16, 128)]
STREAM += [(f"f1{part}{half}", *shape) for half in (0, 1)
           for part, shape in (("i", (HALF, 8, 256)), ("o", (8, HALF, 128)))]
STREAM += [("dqkv", 12, 8, 256), ("dba", 1, 8, 16), ("dz", 4, 8, 256), ("pa", 4, 8, 256), ("ga", 4, 8, 256),
           ("tqk", 6, 8, 256), ("tv", 3, 8, 256), ("tz", 3, 8, 256), ("pb", 4, 6, 256), ("gb", 4, 8, 256),
           ("wo", 4, 8, 256)]
SHARED = {"ckv0": ("rqk", 4), "ckv1": ("rv", 0)}


class Ring:

    def __init__(self, plan):
        self.plan = plan
        self.tile = 0
        self.issued = 0
        self.split = 0
        self.unit = 8


class Map:

    def __init__(self, first, end):
        self.free = [(first, end)]

    def take(self, size):
        for n, (a, b) in enumerate(self.free):
            if b - a >= size:
                self.free[n:n + 1] = [(a + size, b)] if b - a > size else []
                return a
        raise ValueError(f"no room for {size} bytes in {self.free}")

    def give(self, at, size):
        joined = []
        for a, b in sorted(self.free + [(at, at + size)]):
            if joined and joined[-1][1] == a:
                joined[-1] = (joined[-1][0], b)
            else:
                joined.append((a, b))
        self.free = joined


def wait(eng, sem, count):
    if not isinstance(count, int) or count > 0:
        eng.wait_ge(sem, count)


def over_tiles(eng, n, body, peel=0):
    pairs = (n - 1) // 2
    first = min(peel, pairs)
    if pairs - first == 1:
        first = pairs
    for t in range(2 * first):
        body(t, t % 2, False)
    if pairs > first:
        with eng.Fori(first, pairs) as i:
            body(2 * i, 0, False)
            body(2 * i + 1, 1, False)
    for t in range(2 * pairs, n):
        body(t, t % 2, t == n - 1)


def program(nc, io):
    plan = []
    for name, n, kc, nt in STREAM:
        src, first = SHARED.get(name, (name, 0))
        plan += [(io["w_" + src], first + t, kc * nt) for t in range(n)]
    shapes = {name: (n, kc, nt) for name, n, kc, nt in STREAM}
    ring = Ring(plan)
    room = Map(-(-nc.sbuf_base // 32) * 32, nc.sbuf_top // 32 * 32)

    with ExitStack() as top:
        def sem(name):
            return top.enter_context(nc.semaphore(name))

        def sb(scope, name, shape, dtype=F32):
            size = -(-int(np.prod(shape[1:])) * 4 // 32) * 32
            at = room.take(size)
            scope.callback(room.give, at, size)
            return nc.alloc_sbuf_tensor_at(name, shape, dtype, offset=at)

        def psum(scope, name, shape):
            return scope.enter_context(nc.psum_tensor(name, shape, F32))

        def stage_block():
            return nc.Block(no_gpsimd_drain=True)

        small = sb(top, "small", [P, SMALLS])
        ident = sb(top, "ident", [P, P])
        ones = sb(top, "ones", [P, P])
        stage = sb(top, "stage", [P, 2, SLOT])
        x_lat = sb(top, "x_lat", [P, DC, LAT])
        mods = sb(top, "mods", [P, 2, 48, 2])
        ada = sb(top, "ada", [P, 24])
        scale_of = sb(top, "scale_of", [P, 2, 2, 2, DC])
        scale_2 = sb(top, "scale_2", [P, DC])

        def cols(name):
            a, b = SMALL[name]
            return small[:, a:b]

        eps_col = cols("eps")

        small_loaded, loaded = sem("vectors_loaded"), sem("inputs_loaded")
        w_landed = [sem("weights_landed_0"), sem("weights_landed_1")]
        hi_ready = sem("weights_hi_ready")
        lo_ready = sem("weights_lo_ready")
        unit_done = sem("unit_summed")
        unit_free = sem("unit_read")
        stored = sem("output_stored")

        def issue(sp, parity_of, t_expr, src, index, words):
            wait(sp, lo_ready, t_expr - 1)
            sp.dma_start(stage[:, parity_of, 0:words], src[bass.ds(index, 1)].rearrange("o p n -> p (o n)"))\
                .then_inc(w_landed[parity_of], 16)

        def issue_next(sp, upto_tile):
            while ring.issued < min(upto_tile, len(plan)):
                src, index, words = plan[ring.issued]
                issue(sp, ring.issued % 2, ring.issued, src, index, words)
                ring.issued += 1

        def issue_stage(sp, n):
            if ring.issued == ring.tile + 2 and n > 4:
                src, first, words = plan[ring.issued]
                base = ring.issued
                pairs = (n - 2) // 2
                with sp.Fori(0, pairs) as i:
                    for j in range(2):
                        issue(sp, (base + j) % 2, 2 * i + (base + j), src, 2 * i + (first + j), words)
                ring.issued += 2 * pairs
            issue_next(sp, ring.tile + n + 2)

        def landed(eng, t, parity):
            slot = (ring.tile + parity) % 2
            half = (t - parity) // 2 if isinstance(t, int) else None
            first = (ring.tile + parity) // 2 + 1
            if half is not None:
                eng.wait_ge(w_landed[slot], 16 * (first + half))
            else:
                eng.wait_ge(w_landed[slot], 8 * (t - parity) + 16 * first)
            return slot

        used_before = set()

        def counted_from(sems, first):
            again = id(sems) in used_before
            used_before.add(id(sems))
            if again or first:
                with stage_block() as block:
                    @block.vector
                    def _(dve):
                        for k, s in sems.items():
                            if again:
                                dve.sem_clear(s)
                            if k in first:
                                dve.sem_inc(s, first[k])
            return sems

        def linear(name, x_hi, x_lo, units, evac_act=None, evac_dve=None, source=None):
            n, kc, nt = shapes[name]
            assert plan[ring.tile][0] is io["w_" + SHARED.get(name, (name, 0))[0]]
            words = kc * nt
            units_of = units if callable(units) else lambda t: units
            U = len(units_of(0))
            c0 = ring.unit
            with ExitStack() as scope:
                w_hi = sb(scope, f"{name}_w_hi", [P, 2, words], F32R)
                w_lo = sb(scope, f"{name}_w_lo", [P, 2, words], F32R)
                acc = psum(scope, f"{name}_acc", [P, 2, 2, 512])
                made = source(scope) if source else None

                def results(j):
                    return [acc[:, (c0 + j * U + u) % 2] for u in range(U)]

                def counts(t):
                    return lambda u: t * U + (c0 + u + 1)

                with stage_block() as block:
                    @block.sync
                    def _(sp):
                        issue_stage(sp, n)

                    @block.scalar
                    def _(act):
                        def round_hi(t, j):
                            slot = landed(act, t, j)
                            if not isinstance(t, int) or t >= 2:
                                act.wait_ge(unit_done, (t - 1) * U + c0)
                            nc.scalar.copy(w_hi[:, j, :], stage[:, slot, 0:words]).then_inc(hi_ready, 1)

                        round_hi(0, 0)
                        if made:
                            made["act"](act)

                        def body(t, j, last):
                            if not last:
                                round_hi(t + 1, 1 - j)
                            if evac_act:
                                evac_act(act, t, j, counts(t), results(j))

                        over_tiles(act, n, body)

                    @block.gpsimd
                    def _(pool):
                        def body(t, j, last):
                            pool.wait_ge(hi_ready, t + (ring.split + 1))
                            if not isinstance(t, int) or t >= 2:
                                wait(pool, unit_done, (t - 1) * U + c0)
                            nc.gpsimd.tensor_tensor(w_lo[:, j, :], stage[:, (ring.tile + j) % 2, 0:words],
                                                    w_hi[:, j, :].bitcast(F32), ALU.subtract).then_inc(lo_ready, 1)

                        over_tiles(pool, n, body)

                    @block.tensor
                    def _(pe):
                        if made and made["pe"]:
                            made["pe"](pe)

                        def body(t, j, last):
                            hi = w_hi[:, j, :].rearrange("p (k n) -> p k n", k=kc)
                            lo = w_lo[:, j, :].rearrange("p (k n) -> p k n", k=kc)
                            for u, unit in enumerate(units_of(t)):
                                out = acc[:, (c0 + j * U + u) % 2]
                                if not isinstance(t, int) or c0 + t * U + u >= 2:
                                    wait(pe, unit_free, t * U + (c0 + u - 1))
                                if u == 0:
                                    pe.wait_ge(hi_ready, t + (ring.split + 1))
                                for part in ("hi", "lo"):
                                    if part == "lo" and u == 0:
                                        pe.wait_ge(lo_ready, t + (ring.tile + 1))
                                    w = hi if part == "hi" else lo
                                    for k in range(kc):
                                        if made and part == "hi" and u == 0 and isinstance(t, int) and t == 0:
                                            pe.wait_ge(made["ready"], made["first"] + k + 1)
                                        for xi, x in enumerate((x_hi, x_lo) if part == "hi" else (x_hi,)):
                                            begin = part == "hi" and k == 0 and xi == 0
                                            end = part == "lo" and k == kc - 1
                                            if unit[0] == "F":
                                                for b, (s, m) in enumerate(unit[2]):
                                                    mm = nc.tensor.matmul(out[:, b, 0:m], w[:, k, unit[1]:unit[1] + P],
                                                                          x[:, k, s:s + m], start=begin, stop=end)
                                            else:
                                                mm = nc.tensor.matmul(out[:, 0, 0:unit[3]], x[:, k, unit[1]],
                                                                      w[:, k, unit[2]:unit[2] + unit[3]],
                                                                      start=begin, stop=end)
                                mm.then_inc(unit_done, 1)

                        over_tiles(pe, n, body, peel=1 if made else 0)

                    @block.vector
                    def _(dve):
                        if made:
                            made["dve"](dve)
                        if evac_dve:
                            over_tiles(dve, n, lambda t, j, last: evac_dve(dve, t, j, counts(t), results(j)))

            ring.tile += n
            ring.split += n
            ring.unit += n * U

        ALL = [(0, LAT), (LAT, CTX)]
        ONLY_LAT = [(0, LAT)]

        def feature_units(segs, nt=256):
            return [("F", c, segs) for c in range(0, nt, P)]

        norm_sem = {k: sem("norm_" + k) for k in ("squares", "summed", "root", "rstd", "scaled", "hi", "lo")}
        norms = [0]

        def norm_split(x_of, groups, hi, lo):
            n = norms[0]
            norms[0] += 1
            T = sum(g[1] for g in groups)
            S = norm_sem
            done = {k: norm_done.get(k, 0) for k in S}

            def source(scope):
                squares = sb(scope, f"norm{n}_squares", [P, 2, T])
                rstd = sb(scope, f"norm{n}_rstd", [P, T])
                scaled = squares
                total = psum(scope, f"norm{n}_total", [P, 2, 512])

                def of_act(act):
                    for c in range(DC):
                        if c >= 2:
                            act.wait_ge(S["summed"], done["summed"] + c - 1)
                        for s, m, _, _ in groups:
                            last = nc.scalar.activation(squares[:, c % 2, s:s + m], x_of(c, s, m), ACT.Square)
                        last.then_inc(S["squares"], 1)
                    act.wait_ge(S["summed"], done["summed"] + DC)
                    for b, (s, m, _, _) in enumerate(groups):
                        last = nc.scalar.activation(rstd[:, s:s + m], total[:, b, 0:m], ACT.Sqrt, bias=eps_col,
                                                    scale=1.0 / D)
                    last.then_inc(S["root"], 1)
                    for c in range(DC):
                        act.wait_ge(S["scaled"], done["scaled"] + c + 1)
                        for s, m, _, b in groups:
                            last = nc.scalar.activation(hi[:, c, s:s + m], scaled[:, c % 2, s:s + m],
                                                        ACT.Identity, bias=b(c))
                        last.then_inc(S["hi"], 1)

                def of_pe(pe):
                    for c in range(DC):
                        pe.wait_ge(S["squares"], done["squares"] + c + 1)
                        for b, (s, m, _, _) in enumerate(groups):
                            mm = nc.tensor.matmul(total[:, b, 0:m], ones[:], squares[:, c % 2, s:s + m],
                                                  start=c == 0, stop=c == DC - 1)
                        mm.then_inc(S["summed"], 1)

                def of_dve(dve):
                    dve.wait_ge(S["root"], done["root"] + 1)
                    nc.vector.reciprocal(rstd[:], rstd[:]).then_inc(S["rstd"], 1)
                    dve.wait_ge(S["rstd"], done["rstd"] + 1)

                    def low(c):
                        dve.wait_ge(S["hi"], done["hi"] + c + 1)
                        for s, m, _, b in groups:
                            last = nc.vector.scalar_tensor_tensor(
                                lo[:, c, s:s + m], scaled[:, c % 2, s:s + m], b(c),
                                hi[:, c, s:s + m].bitcast(F32), ALU.add, ALU.subtract)
                        last.then_inc(S["lo"], 1)

                    for c in range(DC):
                        if c >= 2:
                            dve.wait_ge(S["lo"], done["lo"] + c - 1)
                        for s, m, a, _ in groups:
                            last = nc.vector.scalar_tensor_tensor(
                                scaled[:, c % 2, s:s + m], x_of(c, s, m), a(c), rstd[:, s:s + m],
                                ALU.mult, ALU.mult)
                        last.then_inc(S["scaled"], 1)
                        if c >= 1:
                            low(c - 1)
                    low(DC - 1)

                return dict(act=of_act, pe=of_pe, dve=of_dve, ready=S["lo"], first=done["lo"])

            for k, m in (("squares", DC), ("summed", DC), ("root", 1), ("rstd", 1), ("scaled", DC), ("hi", DC),
                         ("lo", DC)):
                norm_done[k] = done[k] + m
            return source

        norm_done = {}

        cut_sem = {"hi": sem("cut_hi"), "lo": sem("cut_lo")}
        cut_done = [0]

        def cut(src, hi, lo, chunks):
            base = cut_done[0]
            cut_done[0] += chunks

            def source(scope):
                def of_act(act):
                    with act.Fori(0, chunks) as c:
                        nc.scalar.copy(hi[:, bass.ds(c, 1), :], src[:, bass.ds(c, 1), :]).then_inc(cut_sem["hi"], 1)

                def of_dve(dve):
                    with dve.Fori(0, chunks) as c:
                        dve.wait_ge(cut_sem["hi"], c + (base + 1))
                        nc.vector.tensor_tensor(lo[:, bass.ds(c, 1), :], src[:, bass.ds(c, 1), :],
                                                hi[:, bass.ds(c, 1), :].bitcast(F32), ALU.subtract)\
                            .then_inc(cut_sem["lo"], 1)

                return dict(act=of_act, pe=None, dve=of_dve, ready=cut_sem["lo"], first=base)

            return source

        ffn_sem = {k: sem("ffn_" + k) for k in ("hi", "lo")}
        ffn_done = [1]

        def feed_forward(layer, x_hi, x_lo, segs, residual, source):
            T = sum(m for _, m in segs)
            for half in (0, 1):
                base = ffn_done[0]
                ffn_done[0] += HALF
                with ExitStack() as scope:
                    h_hi = sb(scope, f"ffn{layer}{half}_hi", [P, HALF, T], F32R)
                    h_lo = sb(scope, f"ffn{layer}{half}_lo", [P, HALF, T], F32R)
                    with ExitStack() as inner:
                        gate = sb(inner, f"ffn{layer}{half}_gate", [P, T])
                        hidden = sb(inner, f"ffn{layer}{half}_hidden", [P, T])

                        def evac_act(act, t, j, count, res):
                            act.wait_ge(unit_done, count(0))
                            for b, (s, m) in enumerate(segs):
                                last = nc.scalar.activation(gate[:, s:s + m], res[0][:, b, 0:m], ACT.Silu)
                            last.then_inc(unit_free, 1)
                            act.wait_ge(unit_free, count(1))
                            nc.scalar.copy(h_hi[:, bass.ds(t, 1), :], hidden[:].rearrange("p (o n) -> p o n", o=1))\
                                .then_inc(ffn_sem["hi"], 1)

                        def evac_dve(dve, t, j, count, res):
                            dve.wait_ge(unit_done, count(1))
                            dve.wait_ge(unit_free, count(0))
                            wait(dve, ffn_sem["lo"], t + base)
                            for b, (s, m) in enumerate(segs):
                                last = nc.vector.tensor_tensor(hidden[:, s:s + m], res[1][:, b, 0:m],
                                                               gate[:, s:s + m], ALU.mult)
                            last.then_inc(unit_free, 1)
                            dve.wait_ge(ffn_sem["hi"], t + (base + 1))
                            nc.vector.tensor_tensor(h_lo[:, bass.ds(t, 1), :],
                                                    hidden[:].rearrange("p (o n) -> p o n", o=1),
                                                    h_hi[:, bass.ds(t, 1), :].bitcast(F32), ALU.subtract)\
                                .then_inc(ffn_sem["lo"], 1)

                        linear(f"f{layer}i{half}", x_hi, x_lo, feature_units(segs), evac_act, evac_dve,
                               source if half == 0 else None)
                    linear(f"f{layer}o{half}", h_hi, h_lo, [("F", 0, segs)], None, residual)

        def add_residual(segs, gates, per_tile):
            def evac(dve, t, j, count, res):
                for u in range(per_tile):
                    dve.wait_ge(unit_done, count(u))
                    for b, (s, m) in enumerate(segs):
                        c = t * per_tile + u
                        x = x_lat[:, bass.ds(c, 1), :] if s == 0 else x_ctx[0][:, bass.ds(c, 1), :]
                        x = x.rearrange("p o n -> p (o n)")
                        last = nc.vector.scalar_tensor_tensor(
                            x, res[u][:, b, 0:m], gates[b][:, bass.ds(c, 1)], x, ALU.mult, ALU.add)
                    last.then_inc(unit_free, 1)
            return evac

        x_ctx = [None]

        rope_loaded, rope_turned = sem("ret_rope_loaded"), sem("ret_rope_turned")
        conv_sem, silu_sem = sem("conv_tap"), sem("conv_silu")
        with stage_block() as block:
            @block.sync
            def _(sp):
                sp.dma_start(small[:], io["small"]).then_inc(small_loaded, 16)
                sp.dma_start(ident[:], io["ident"]).then_inc(loaded, 16)

            @block.vector
            def _(dve):
                for s in (unit_done, unit_free):
                    dve.sem_inc(s, ring.unit)
                for s in ffn_sem.values():
                    dve.sem_inc(s, ffn_done[0])
                dve.sem_inc(rope_turned, 1)
                dve.sem_inc(silu_sem, 2)

        QUAD = 4
        quads, quads_main = 60 // QUAD, 48 // QUAD
        quad_landed = [sem(f"mod_weights_landed_{s}") for s in range(4)]
        cond_ready, quad_used, modded = sem("cond_ready"), sem("mod_weights_used"), sem("modulation_ready")
        rows_copied, cols_turned = sem("mod_rows_copied"), sem("mod_columns_turned")
        with ExitStack() as scope:
            cond = sb(scope, "cond_silu", [P, 24])
            mod_w = sb(scope, "mod_weights", [P, 4, QUAD, 2048])
            rows = sb(scope, "mod_rows", [2, 2, QUAD * 256])
            p_rows = psum(scope, "mod_p_rows", [P, 2, 2, 512])
            mod_sum = psum(scope, "mod_sum", [P, 512])
            with stage_block() as block:
                @block.sync
                def _(sp):
                    for q in range(quads):
                        if q >= 4:
                            sp.wait_ge(quad_used, q - 3)
                        sp.dma_start(mod_w[:, q % 4, :, :],
                                     io["w_mod"][q * QUAD:(q + 1) * QUAD].rearrange("o p n -> p o n"))\
                            .then_inc(quad_landed[q % 4], 16)
                        if q == 3:
                            for dst, src in ((ones, "ones"), (x_lat, "x")):
                                sp.dma_start(dst[:], io[src]).then_inc(loaded, 16)
                            issue_next(sp, 2)

                @block.scalar
                def _(act):
                    act.wait_ge(small_loaded, 16)
                    a, b = SMALL["cond"][0], SMALL["cond_2"][1]
                    nc.scalar.activation(cond[:], small[:, a:b], ACT.Silu).then_inc(cond_ready, 1)
                    for q in range(quads):
                        m = 2 if q < quads_main else 1
                        act.wait_ge(quad_used, q + 1)
                        if q >= 2:
                            act.wait_ge(cols_turned, q - 1)
                        nc.scalar.copy(rows[0:m, q % 2, :].rearrange("p (b n) -> p b n", n=512),
                                       p_rows[0:m, q % 2, :, :]).then_inc(rows_copied, 1)

                @block.tensor
                def _(pe):
                    pe.wait_ge(cond_ready, 1)

                    def sum_quad(q):
                        pe.wait_ge(quad_landed[q % 4], 16 * (q // 4 + 1))
                        if q >= 2:
                            pe.wait_ge(rows_copied, q - 1)
                        for b in range(2):
                            for k in range(DC):
                                who = cond[:, k:16:8] if q < quads_main else cond[:, 16 + k:17 + k]
                                w = mod_w[:, q % 4, 2 * b:2 * b + 2, k * 256:(k + 1) * 256]
                                mm = nc.tensor.matmul(p_rows[0:who.shape[1], q % 2, b, :], who, w,
                                                      start=k == 0, stop=k == DC - 1)
                        mm.then_inc(quad_used, 1)

                    def turn_quad(q):
                        m = 2 if q < quads_main else 1
                        at = 16 * q if q < quads_main else 16 * quads_main + 8 * (q - quads_main)
                        if q == 0:
                            pe.wait_ge(loaded, 48)
                        pe.wait_ge(rows_copied, q + 1)
                        for c in range(8):
                            mm = nc.tensor.transpose(mod_sum[:, at + c * m:at + (c + 1) * m],
                                                     rows[0:m, q % 2, c * P:(c + 1) * P], ident[0:m, 0:m])
                        mm.then_inc(cols_turned, 1)

                    for q in range(quads):
                        sum_quad(q)
                        if q >= 1:
                            turn_quad(q - 1)
                    turn_quad(quads - 1)

                @block.vector
                def _(dve):
                    dve.wait_ge(loaded, 48)
                    dve.wait_ge(cols_turned, quads)
                    a, b = SMALL["mod_b"]
                    bias = small[:, a:b].rearrange("p (m o) -> p m o", o=1).broadcast_to([P, 96, 2])
                    nc.vector.tensor_tensor(mods[:].rearrange("p l m v -> p (l m) v"),
                                            mod_sum[:, 0:192].rearrange("p (m v) -> p m v", v=2), bias, ALU.add)
                    nc.vector.tensor_tensor(ada[:], mod_sum[:, 192:216], cols("ada_b"), ALU.add).then_inc(modded, 1)
                    dve.wait_ge(modded, 1)
                    gain = cols("norm_g").rearrange("p (l w c) -> p l w c", l=2, w=2)
                    for layer in range(2):
                        for which in range(2):
                            for v in range(2):
                                m = 24 * which + 8
                                nc.vector.scalar_tensor_tensor(
                                    scale_of[:, layer, which, v, :], mods[:, layer, m:m + 8, v], 1.0,
                                    gain[:, layer, which, :], ALU.add, ALU.mult)
                    nc.vector.scalar_tensor_tensor(scale_2[:], ada[:, 8:16], 1.0, cols("norm_w"), ALU.add, ALU.mult)

        def group(layer, which, v, first, tokens):
            return (first, tokens, lambda c: scale_of[:, layer, which, v, c:c + 1],
                    lambda c: mods[:, layer, 24 * which + c, v:v + 1])

        def gates_of(layer, which, v):
            m = 24 * which + 16
            return mods[:, layer, m:m + 8, v]

        def copy_units(buf, first, per_tile=2, func=ACT.Identity):
            def evac(act, t, j, count, res):
                for u in range(per_tile):
                    act.wait_ge(unit_done, count(u))
                    width = buf.shape[2]
                    for b, s in enumerate(range(0, width, 512)):
                        m = min(512, width - s)
                        last = nc.scalar.activation(
                            buf[:, bass.ds(t * per_tile + (first + u), 1), s:s + m],
                            res[u][:, b:b + 1, 0:m], func)
                    last.then_inc(unit_free, 1)
            return evac

        mix = ExitStack()

        ctx_scope = ExitStack()
        x_ctx[0] = sb(ctx_scope, "x_ctx", [P, DC, CTX])
        ctx_loaded = sem("context_loaded")
        with stage_block() as block:
            @block.sync
            def _(sp):
                sp.dma_start(x_ctx[0][:], io["ctx"]).then_inc(ctx_loaded, 16)
                sp.wait_ge(ctx_loaded, 16)

        def x_all(c, s, m):
            return x_lat[:, c, s:s + m] if s < LAT else x_ctx[0][:, c, s - LAT:s - LAT + m]

        attend_jobs = ("scores", "scores_read", "maximum", "exp", "turned", "turned_read", "mixed")
        attend_sem = {}
        for k in attend_jobs + ("queries", "reciprocal", "normed", "out", "out_read", "log", "lse"):
            attend_sem[k] = sem("attend_" + k)

        def attend(tag, blocks, heads, q_copies, out_copies, width, kb_max, cols_out, scale, lse=None):
            H = len(heads)
            S = counted_from(attend_sem, {k: H if k in attend_jobs else 1 for k in attend_sem})
            chunks = cols_out // P
            with ExitStack() as scope:
                has_sink = heads[0]["sink"] is not None
                row = sb(scope, f"{tag}_row", [P, 3, width + has_sink])
                minus_max = sb(scope, f"{tag}_minus_max", [P, H])
                total = sb(scope, f"{tag}_total", [P, H])
                inverse = sb(scope, f"{tag}_inverse", [P, H])
                log_total = sb(scope, f"{tag}_log_total", [P, H])
                probs = sb(scope, f"{tag}_probs", [P, 2, kb_max * P])
                mixed = sb(scope, f"{tag}_mixed", [P, cols_out])
                sbanks = (width + 511) // 512
                p_scores = psum(scope, f"{tag}_p_scores", [P, 2, sbanks, 512])
                p_turned = psum(scope, f"{tag}_p_turned", [P, (kb_max + 3) // 4 * 512])
                p_mixed = psum(scope, f"{tag}_p_mixed", [P, (cols_out + 511) // 512 * 512])
                p_out = psum(scope, f"{tag}_p_out", [P, (cols_out + 511) // 512 * 512])

                def slot_of(h):
                    n = heads[h]["column"] // 64
                    return slice(n, n + 1)

                def before(i, h, lag):
                    return i * H + (H + max(h + 1 - lag, 0))

                def key_blocks(i, h):
                    return sum(k[1] for k in heads[h]["keys"](i)) // P

                with stage_block() as block:
                    @block.tensor
                    def _(pe):
                        def scores(i, h):
                            if h == 0:
                                pe.wait_ge(S["queries"], i + 2)
                            pe.wait_ge(S["scores_read"], before(i, h, 2))
                            for b, (_, m, rhs, _) in enumerate(heads[h]["keys"](i)):
                                mm = nc.tensor.matmul(p_scores[:, h % 2, b, 0:m], heads[h]["q"], rhs,
                                                      start=True, stop=True)
                            mm.then_inc(S["scores"], 1)

                        def turn(i, h):
                            pe.wait_ge(S["exp"], i * H + (H + h + 1))
                            pe.wait_ge(S["turned_read"], i * H + (H + h))
                            for b in range(key_blocks(i, h)):
                                mm = nc.tensor.transpose(p_turned[:, b * P:(b + 1) * P],
                                                         row[:, h % 3, b * P:(b + 1) * P], ident[:])
                            mm.then_inc(S["turned"], 1)

                        def mix_values(i, h):
                            pe.wait_ge(S["turned_read"], i * H + (H + h + 1))
                            if h == 0:
                                pe.wait_ge(S["normed"], i + 1)
                            c = heads[h]["column"]
                            n = key_blocks(i, h)
                            for b, v in enumerate(heads[h]["values"](i)):
                                mm = nc.tensor.matmul(p_mixed[:, c:c + 64], probs[:, h % 2, b * P:(b + 1) * P], v,
                                                      start=b == 0, stop=b == n - 1)
                            mm.then_inc(S["mixed"], 1)

                        with pe.Fori(0, blocks) as i:
                            scores(i, 0)
                            scores(i, 1)
                            for h in range(H):
                                if h + 2 < H:
                                    scores(i, h + 2)
                                turn(i, h)
                                if h >= 1:
                                    mix_values(i, h - 1)
                            mix_values(i, H - 1)
                            pe.wait_ge(S["normed"], i + 2)
                            pe.wait_ge(S["out_read"], i + 1)
                            for c in range(chunks):
                                mm = nc.tensor.transpose(p_out[:, c * P:(c + 1) * P], mixed[:, c * P:(c + 1) * P],
                                                         ident[:])
                            mm.then_inc(S["out"], 1)

                    @block.vector
                    def _(dve):
                        def read_scores(i, h):
                            head = heads[h]
                            if lse is not None and h == 0:
                                dve.wait_ge(S["lse"], i + 1)
                            dve.wait_ge(S["scores"], i * H + (H + h + 1))
                            dve.wait_ge(S["turned"], before(i, h, 3))
                            if head["sink"] is not None:
                                n = key_blocks(i, h) * P
                                nc.vector.tensor_copy(row[:, h % 3, n:n + 1], head["sink"])
                            for b, (s, m, _, mask) in enumerate(head["keys"](i)):
                                if mask is None:
                                    last = nc.vector.tensor_scalar(row[:, h % 3, s:s + m], p_scores[:, h % 2, b, 0:m],
                                                                   scale, None, ALU.mult)
                                else:
                                    last = nc.vector.scalar_tensor_tensor(
                                        row[:, h % 3, s:s + m], p_scores[:, h % 2, b, 0:m], scale, mask,
                                        ALU.mult, ALU.add)
                            last.then_inc(S["scores_read"], 1)
                            dve.wait_ge(S["scores_read"], i * H + (H + h + 1))
                            n = key_blocks(i, h) * P + has_sink
                            nc.vector.tensor_reduce(minus_max[:, slot_of(h)], row[:, h % 3, 0:n], AX_X, ALU.max,
                                                    negate=True).then_inc(S["maximum"], 1)

                        with dve.Fori(0, blocks) as i:
                            for h in range(H):
                                read_scores(i, h)
                            dve.wait_ge(S["mixed"], i * H + 2 * H)
                            nc.vector.reciprocal(inverse[:], total[:]).then_inc(S["reciprocal"], 1)
                            dve.wait_ge(S["reciprocal"], i + 2)
                            dve.wait_ge(S["out"], i + 1)
                            nc.vector.tensor_tensor(
                                mixed[:].rearrange("p (h n) -> p h n", n=64),
                                p_mixed[:, 0:cols_out].rearrange("p (h n) -> p h n", n=64),
                                inverse[:].rearrange("p (h o) -> p h o", o=1).broadcast_to([P, H, 64]), ALU.mult)\
                                .then_inc(S["normed"], 1)
                            if lse is not None:
                                dve.wait_ge(S["log"], i + 2)
                                nc.vector.tensor_tensor(lse[:, bass.ds(i, 1), :].rearrange("p o h -> p (o h)"),
                                                        log_total[:], minus_max[:], ALU.subtract)\
                                    .then_inc(S["lse"], 1)

                    @block.scalar
                    def _(act):
                        def exponent(i, h):
                            act.wait_ge(S["maximum"], i * H + (H + h + 1))
                            n = key_blocks(i, h) * P + has_sink
                            nc.scalar.activation(row[:, h % 3, 0:n], row[:, h % 3, 0:n], ACT.Exp,
                                                 bias=minus_max[:, slot_of(h)], accum_out=total[:, slot_of(h)])\
                                .then_inc(S["exp"], 1)

                        def copy_turned(i, h):
                            act.wait_ge(S["turned"], i * H + (H + h + 1))
                            act.wait_ge(S["mixed"], before(i, h, 2))
                            n = key_blocks(i, h) * P
                            nc.scalar.copy(probs[:, h % 2, 0:n], p_turned[:, 0:n]).then_inc(S["turned_read"], 1)

                        with act.Fori(0, blocks) as i:
                            act.wait_ge(S["scores"], i * H + H)
                            for dst, src in q_copies(i):
                                last = nc.scalar.copy(dst, src)
                            last.then_inc(S["queries"], 1)
                            exponent(i, 0)
                            for h in range(H):
                                if h + 1 < H:
                                    exponent(i, h + 1)
                                copy_turned(i, h)
                            if lse is not None:
                                act.wait_ge(S["exp"], i * H + 2 * H)
                                act.wait_ge(S["lse"], i + 1)
                                nc.scalar.activation(log_total[:], total[:], ACT.Ln).then_inc(S["log"], 1)
                            act.wait_ge(S["out"], i + 2)
                            for dst, src in out_copies(i, p_out):
                                last = nc.scalar.copy(dst, src)
                            last.then_inc(S["out_read"], 1)

        mixed_0 = sb(mix, "mixed_0", [P, DC, TOK])
        normed_scope = ExitStack()
        n_hi = sb(normed_scope, "norm_a_hi", [P, DC, TOK], F32R)
        n_lo = sb(normed_scope, "norm_a_lo", [P, DC, TOK], F32R)
        norm_a = norm_split(x_all, [group(0, 0, 0, 0, LAT), group(0, 0, 1, LAT, CTX)], n_hi, n_lo)

        attn = ExitStack()
        qk = sb(attn, "qk", [P, 5, TOK])
        k_pad = sb(attn, "k_pad", [P, P + LAT + P + CTX])
        v_pad = sb(attn, "v_pad", [P, 8, P])
        pad_ready = sem("pads_zeroed")

        linear("aq", n_hi, n_lo, feature_units(ALL), copy_units(qk, 0), source=norm_a)

        def evac_akv(act, t, j, count, res):
            act.wait_ge(unit_done, count(0))
            nc.scalar.copy(qk[:, 4, 0:LAT], res[0][:, 0, :])
            nc.scalar.copy(qk[:, 4, LAT:TOK], res[0][:, 1, 0:CTX]).then_inc(unit_free, 1)
            for b in range(6):
                act.wait_ge(unit_done, count(1 + b))
                nc.scalar.copy(v_pad[:, b + 1 if b < 4 else b + 2, :], res[1 + b][:, 0, 0:P]).then_inc(unit_free, 1)

        linear("akv", n_hi, n_lo, [("F", 0, ALL)] + [("T", slice(b * P, (b + 1) * P), P, P) for b in range(6)],
               evac_akv)

        hn = {k: sem("headnorm_" + k) for k in ("tables", "squares", "summed", "root", "rstd", "normed", "rotated",
                                               "cosine", "sine", "done")}
        with ExitStack() as scope:
            axial = sb(scope, "axial", [P, 2, LAT])
            rotT = sb(scope, "rotT", [P, P])
            ones64 = sb(scope, "ones64", [P, P])
            squares = sb(scope, "head_squares", [P, 2, TOK])
            rstd = sb(scope, "head_rstd", [P, 2, TOK])
            unit = sb(scope, "head_unit", [P, 2, TOK])
            turn_c = sb(scope, "head_cosine", [P, 2, LAT])
            turn_s = sb(scope, "head_sine", [P, 2, LAT])
            p_sum = psum(scope, "head_sum", [P, 2, 2, 512])
            p_rot = psum(scope, "head_rot", [P, 2, 512])
            with stage_block() as block:
                @block.sync
                def _(sp):
                    for dst, src in ((axial, "axial"), (rotT, "rotT"), (ones64, "ones64")):
                        sp.dma_start(dst[:], io[src]).then_inc(hn["tables"], 16)

                @block.gpsimd
                def _(pool):
                    for pad in (k_pad[:, 0:P], k_pad[:, P + LAT:2 * P + LAT], v_pad[:, 0, :], v_pad[:, 5, :]):
                        nc.gpsimd.memset(pad, 0.0).then_inc(pad_ready, 1)
                    pool.wait_ge(pad_ready, 4)

                @block.scalar
                def _(act):
                    for c in range(5):
                        if c >= 2:
                            act.wait_ge(hn["summed"], c - 1)
                        nc.scalar.activation(squares[:, c % 2, :], qk[:, c, :], ACT.Square).then_inc(hn["squares"], 1)
                        act.wait_ge(hn["summed"], c + 1)
                        if c >= 2:
                            act.wait_ge(hn["normed"], c - 1)
                        nc.scalar.activation(rstd[:, c % 2, 0:LAT], p_sum[:, c % 2, 0, :], ACT.Sqrt, bias=eps_col,
                                             scale=1.0 / 64)
                        nc.scalar.activation(rstd[:, c % 2, LAT:TOK], p_sum[:, c % 2, 1, 0:CTX], ACT.Sqrt, bias=eps_col,
                                             scale=1.0 / 64).then_inc(hn["root"], 1)

                @block.tensor
                def _(pe):
                    pe.wait_ge(hn["tables"], 48)

                    def rotate(c):
                        pe.wait_ge(hn["normed"], c + 1)
                        if c >= 2:
                            pe.wait_ge(hn["sine"], c - 1)
                        nc.tensor.matmul(p_rot[:, c % 2, :], rotT[:], unit[:, c % 2, 0:LAT], start=True, stop=True)\
                            .then_inc(hn["rotated"], 1)

                    for c in range(5):
                        pe.wait_ge(hn["squares"], c + 1)
                        if c >= 2:
                            pe.wait_ge(hn["root"], c - 1)
                        nc.tensor.matmul(p_sum[:, c % 2, 0, :], ones64[:], squares[:, c % 2, 0:LAT], start=True, stop=True)
                        nc.tensor.matmul(p_sum[:, c % 2, 1, 0:CTX], ones64[:], squares[:, c % 2, LAT:TOK],
                                         start=True, stop=True).then_inc(hn["summed"], 1)
                        if c >= 1:
                            rotate(c - 1)
                    rotate(4)

                @block.vector
                def _(dve):
                    dve.wait_ge(hn["tables"], 48)
                    for c in range(5):
                        g = cols("qk_g")[:, 0:1] if c < 4 else cols("qk_g")[:, 1:2]
                        dve.wait_ge(hn["root"], c + 1)
                        nc.vector.reciprocal(rstd[:, c % 2, :], rstd[:, c % 2, :]).then_inc(hn["rstd"], 1)
                        dve.wait_ge(hn["rstd"], c + 1)
                        nc.vector.scalar_tensor_tensor(unit[:, c % 2, :], qk[:, c, :], g, rstd[:, c % 2, :],
                                                       ALU.mult, ALU.mult).then_inc(hn["normed"], 1)
                        dve.wait_ge(hn["normed"], c + 1)
                        nc.vector.tensor_tensor(turn_c[:, c % 2, :], unit[:, c % 2, 0:LAT], axial[:, 0, :], ALU.mult)\
                            .then_inc(hn["cosine"], 1)
                        dve.wait_ge(hn["rotated"], c + 1)
                        nc.vector.tensor_tensor(turn_s[:, c % 2, :], p_rot[:, c % 2, :], axial[:, 1, :], ALU.mult)\
                            .then_inc(hn["sine"], 1)
                        dve.wait_ge(hn["sine"], c + 1)
                        lat, ctx = ((qk[:, c, 0:LAT], qk[:, c, LAT:TOK]) if c < 4 else
                                    (k_pad[:, P:P + LAT], k_pad[:, 2 * P + LAT:2 * P + TOK]))
                        nc.vector.tensor_copy(ctx, unit[:, c % 2, LAT:TOK])
                        nc.vector.tensor_tensor(lat, turn_c[:, c % 2, :], turn_s[:, c % 2, :], ALU.add)\
                            .then_inc(hn["done"], 1)

        with ExitStack() as scope:
            q_zero = sb(scope, "q_zero", [P, 8, P])
            window = sb(scope, "window", [P, 4, 3 * P])
            window_ready, zeroed = sem("window_loaded"), sem("queries_zeroed")
            with stage_block() as block:
                @block.sync
                def _(sp):
                    sp.dma_start(window[:], io["window"]).then_inc(window_ready, 16)
                    sp.wait_ge(window_ready, 16)

                @block.vector
                def _(dve):
                    nc.vector.memset(q_zero[:], 0.0).then_inc(zeroed, 1)

            k_ctx = k_pad[:, 2 * P + LAT:2 * P + TOK]

            def head_of(h, with_lat):
                g = h // 4
                half = slice(64 * g, 64 * g + 64)

                def keys(i):
                    ctx = (3 * P if with_lat else 0, CTX, k_ctx, None)
                    if not with_lat:
                        return [ctx]
                    mask = window[:, bass.ds(i, 1), :].rearrange("p o n -> p (o n)")
                    return [(0, 3 * P, k_pad[:, bass.ds(i * P, 3 * P)], mask), ctx]

                def values(i):
                    lat = [v_pad[:, bass.ds(i + b, 1), half].rearrange("p o n -> p (o n)") for b in range(3)]
                    return lat * with_lat + [v_pad[:, 6, half], v_pad[:, 7, half]]

                return dict(q=q_zero[:, h, :], keys=keys, values=values, column=(h % 4) * P + 64 * g,
                            sink=cols("sink")[:, h:h + 1])

            def q_copies_from(first):
                def copies(i):
                    return [(q_zero[64 * g:64 * g + 64, 4 * g:4 * g + 4, :],
                             qk[64 * g:64 * g + 64, 0:4, bass.ds(i * P + first, P)]) for g in range(2)]
                return copies

            def out_copies_to(first):
                def copies(i, p_out):
                    return [(mixed_0[:, 0:4, bass.ds(i * P + first, P)],
                             p_out[:, 0:512].rearrange("p (c n) -> p c n", c=4))]
                return copies

            attend("win", LAT // P, [head_of(h, True) for h in range(8)], q_copies_from(0), out_copies_to(0),
                   3 * P + CTX, 5, 512, 64.0 ** -0.5)
            attend("ctxa", CTX // P, [head_of(h, False) for h in range(8)], q_copies_from(LAT), out_copies_to(LAT),
                   CTX, 2, 512, 64.0 ** -0.5)
        attn.close()

        head_norm_sem = {k: sem("head_norm_" + k) for k in ("squares", "summed", "root", "rstd", "scaled", "gated")}

        def head_norm(tag, heads, per, width, out, gain=None, gate=None):
            S = counted_from(head_norm_sem, {})
            segs = [(s, min(512, width - s)) for s in range(0, width, 512)]
            with ExitStack() as scope:
                squares = sb(scope, f"{tag}_squares", [P, 2, width])
                rstd = sb(scope, f"{tag}_rstd", [P, 2, width])
                total = psum(scope, f"{tag}_sums", [P, 2, len(segs), 512])
                with stage_block() as block:
                    @block.scalar
                    def _(act):
                        def root(h):
                            act.wait_ge(S["summed"], (h + 1) * per)
                            if h >= 2:
                                act.wait_ge(S["scaled"], h - 1)
                            for b, (s, m) in enumerate(segs):
                                last = nc.scalar.activation(rstd[:, h % 2, s:s + m], total[:, h % 2, b, 0:m], ACT.Sqrt,
                                                            bias=eps_col, scale=1.0 / (per * P))
                            last.then_inc(S["root"], 1)

                        for h in range(heads):
                            for j in range(per):
                                n = h * per + j
                                if n >= 2:
                                    act.wait_ge(S["summed"], n - 1)
                                nc.scalar.activation(squares[:, n % 2, :], out(h, j), ACT.Square)\
                                    .then_inc(S["squares"], 1)
                            if h >= 1:
                                root(h - 1)
                        root(heads - 1)

                    @block.tensor
                    def _(pe):
                        for h in range(heads):
                            if h >= 2:
                                pe.wait_ge(S["root"], h - 1)
                            for j in range(per):
                                n = h * per + j
                                pe.wait_ge(S["squares"], n + 1)
                                for b, (s, m) in enumerate(segs):
                                    mm = nc.tensor.matmul(total[:, h % 2, b, 0:m], ones[:], squares[:, n % 2, s:s + m],
                                                          start=j == 0, stop=j == per - 1)
                                mm.then_inc(S["summed"], 1)

                    @block.vector
                    def _(dve):
                        for h in range(heads):
                            dve.wait_ge(S["root"], h + 1)
                            nc.vector.reciprocal(rstd[:, h % 2, :], rstd[:, h % 2, :]).then_inc(S["rstd"], 1)
                            dve.wait_ge(S["rstd"], h + 1)
                            for j in range(per):
                                g = gain(j) if callable(gain) else gain
                                if g is None:
                                    last = nc.vector.tensor_tensor(out(h, j), out(h, j), rstd[:, h % 2, :], ALU.mult)
                                else:
                                    last = nc.vector.scalar_tensor_tensor(out(h, j), out(h, j), g, rstd[:, h % 2, :],
                                                                          ALU.mult, ALU.mult)
                            last.then_inc(S["scaled"], 1)
                            if gate is not None:
                                dve.wait_ge(S["scaled"], h + 1)
                                for j in range(per):
                                    last = nc.vector.tensor_tensor(out(h, j), out(h, j), gate(h, j), ALU.mult)
                                last.then_inc(S["gated"], 1)

        gla = ExitStack()
        q_silu = sb(gla, "hgrn_q", [P, GLA_H, TOK])
        keep = sb(gla, "hgrn_forget", [P, 2 * GLA_H, TOK])
        i_tok = sb(gla, "hgrn_i", [P, TOK // P, 512])
        g_silu = sb(gla, "hgrn_gate", [P, GLA_H, TOK])
        linear("bq", n_hi, n_lo, feature_units(ALL), copy_units(q_silu, 0, func=ACT.Silu))
        linear("bg", n_hi, n_lo, feature_units(ALL), copy_units(g_silu, 0, func=ACT.Silu))
        linear("bf", n_hi, n_lo, feature_units(ALL), copy_units(keep, 0, func=ACT.Sigmoid))

        def token_units(blocks, nt=256):
            return [("T", slice(b * P, (b + 1) * P), 0, nt) for b in range(blocks)]

        def copy_token_units(buf, blocks, first=0):
            def evac(act, t, j, count, res):
                for b in range(blocks):
                    act.wait_ge(unit_done, count(b))
                    nc.scalar.copy(buf[:, first + b, bass.ds(t * 256, 256)], res[b][:, 0, 0:256]).then_inc(unit_free, 1)
            return evac

        linear("bi", n_hi, n_lo, token_units(6), copy_token_units(i_tok, 6))
        normed_scope.close()

        CH = TOK // 64
        ORDER = ([8, 9, 10, 11, 0, 1, 2, 3, 4, 5, 6, 7], [11, 10, 9, 8, 7, 6, 5, 4, 3, 2, 1, 0])
        REF, LAST = (32, 31), (63, 0)
        gs = {k: sem("hgrn_" + k) for k in ("tables", "zeroed", "top", "bound_exp", "bound", "f", "ln", "k", "cum", "dist",
                                           "exp", "q_scaled", "k_scaled", "turned", "turned_read", "scores", "masked",
                                           "kv", "link", "states", "out", "out_read")}
        JOBS = 2 * GLA_H
        with ExitStack() as scope:
            tri64 = sb(scope, "tri64", [P, 2, 64])
            restart = sb(scope, "restart", [P, TOK])
            bound = sb(scope, "hgrn_bound", [P, 6, GLA_H])
            log_f = sb(scope, "hgrn_log_f", [P, 2, TOK])
            cum = sb(scope, "hgrn_cum", [P, 2, TOK])
            to_ref = sb(scope, "hgrn_to_ref", [P, 2, TOK])
            q_ref = sb(scope, "hgrn_q_ref", [P, 2, TOK])
            k_ref = sb(scope, "hgrn_k_ref", [P, 2, TOK])
            k_end = sb(scope, "hgrn_k_end", [P, 2, TOK])
            k_end_tok = sb(scope, "hgrn_k_end_tok", [P, CH, P])
            q_cum = sb(scope, "hgrn_q_cum", [P, 4, TOK])
            decay = sb(scope, "hgrn_decay", [P, 4, CH])
            state = sb(scope, "hgrn_state", [P, 2, CH, P])
            scores = sb(scope, "hgrn_scores", [P, 2, CH, 64])
            p_turned = psum(scope, "hgrn_p_turned", [P, 1024])
            p_scores = psum(scope, "hgrn_p_scores", [P, 512])
            p_kv = psum(scope, "hgrn_p_kv", [P, 1536])
            p_out = psum(scope, "hgrn_p_out", [P, 1024])

            def by_chunk(ap):
                return ap.rearrange("p (c n) -> p c n", n=64)

            def at_chunk(ap, place):
                return by_chunk(ap)[:, :, place:place + 1].broadcast_to([P, CH, 64])

            def gate_of(n):
                return keep[:, GLA_H * (n % 2) + n // 2, :]

            with stage_block() as block:
                @block.sync
                def _(sp):
                    sp.dma_start(tri64[:], io["tri64"]).then_inc(gs["tables"], 16)
                    sp.dma_start(restart[:], io["restart"]).then_inc(gs["tables"], 16)

                @block.vector
                def _(dve):
                    a, b = cols("lb")[:, 0:GLA_H], cols("lb")[:, GLA_H:2 * GLA_H]
                    nc.vector.tensor_tensor(bound[:, 0, :], a, b, ALU.max).then_inc(gs["top"], 1)
                    dve.wait_ge(gs["top"], 1)
                    nc.vector.tensor_tensor(bound[:, 1, :], a, bound[:, 0, :], ALU.subtract)
                    nc.vector.tensor_tensor(bound[:, 2, :], b, bound[:, 0, :], ALU.subtract).then_inc(gs["top"], 1)
                    dve.wait_ge(gs["bound_exp"], 1)
                    nc.vector.tensor_tensor(bound[:, 3, :], bound[:, 1, :], bound[:, 2, :], ALU.add).then_inc(gs["bound"], 1)
                    dve.wait_ge(gs["bound"], 1)
                    nc.vector.reciprocal(bound[:, 3, :], bound[:, 3, :]).then_inc(gs["bound"], 1)
                    dve.wait_ge(gs["bound"], 2)
                    nc.vector.tensor_tensor(bound[:, 4, :], bound[:, 1, :], bound[:, 3, :], ALU.mult)
                    nc.vector.tensor_tensor(bound[:, 5, :], bound[:, 2, :], bound[:, 3, :], ALU.mult).then_inc(gs["bound"], 1)
                    dve.wait_ge(gs["bound"], 3)
                    dve.wait_ge(gs["tables"], 32)

                    def exponents(n):
                        f, d, x = gate_of(n), n % 2, n % 2
                        wait(dve, gs["exp"], n - 1)
                        nc.vector.tensor_scalar(f, f, bound[:, 5, n // 2:n // 2 + 1], bound[:, 4, n // 2:n // 2 + 1],
                                                ALU.mult, ALU.add).then_inc(gs["f"], 1)
                        dve.wait_ge(gs["ln"], n + 1)
                        way = slice(None, None, 1 if d == 0 else -1)
                        nc.vector.tensor_tensor_scan(cum[:, x, way], restart[:], log_f[:, x, way], 0.0,
                                                     ALU.mult, ALU.add).then_inc(gs["cum"], 1)
                        dve.wait_ge(gs["cum"], n + 1)
                        nc.vector.tensor_tensor(by_chunk(to_ref[:, x, :]), by_chunk(cum[:, x, :]),
                                                at_chunk(cum[:, x, :], REF[d]), ALU.subtract)
                        nc.vector.tensor_tensor(by_chunk(log_f[:, x, :]), at_chunk(cum[:, x, :], LAST[d]),
                                                by_chunk(cum[:, x, :]), ALU.subtract).then_inc(gs["dist"], 1)

                    def scale_queries(n):
                        q = q_silu[:, n // 2, :]
                        dve.wait_ge(gs["exp"], n + 1)
                        nc.vector.tensor_tensor(q_ref[:, n % 2, :], q_ref[:, n % 2, :], q, ALU.mult)
                        nc.vector.tensor_tensor(q_cum[:, n % 4, :], q_cum[:, n % 4, :], q, ALU.mult)\
                            .then_inc(gs["q_scaled"], 1)

                    def mask_scores(n):
                        d = n % 2
                        wait(dve, gs["out"], n // 2)
                        dve.wait_ge(gs["scores"], n + 1)
                        for odd in range(2):
                            part = slice(64 * odd, 64 * odd + 64)
                            last = nc.vector.copy_predicated(
                                scores[part, d, odd:CH:2, :],
                                tri64[part, d:d + 1, :].bitcast(U32).broadcast_to([64, CH // 2, 64]),
                                p_scores[part, 0:CH * 32].rearrange("p (c n) -> p c n", n=64))
                        last.then_inc(gs["masked"], 1)

                    def chain_states(n):
                        d = n % 2
                        dve.wait_ge(gs["kv"], n + 1)
                        for link, (a, b) in enumerate(zip(ORDER[d], ORDER[d][1:])):
                            nc.vector.scalar_tensor_tensor(
                                state[:, d, b, :], state[:, d, a, :], decay[:, n % 4, a:a + 1],
                                p_kv[:, a * P:(a + 1) * P], ALU.mult, ALU.add).then_inc(gs["link"], 1)
                            dve.wait_ge(gs["link"], n * (CH - 1) + link + 1)
                        nc.vector.engine_nop().then_inc(gs["states"], 1)

                    exponents(0)
                    nc.vector.memset(scores[:], 0.0)
                    nc.vector.memset(p_scores[:], 0.0)
                    nc.vector.memset(k_end_tok[:], 0.0)
                    for d in range(2):
                        last = nc.vector.memset(state[:, d, ORDER[d][0], :], 0.0)
                    last.then_inc(gs["zeroed"], 1)
                    dve.wait_ge(gs["zeroed"], 1)
                    scale_queries(0)
                    for n in range(JOBS):
                        if n + 1 < JOBS:
                            exponents(n + 1)
                        mask_scores(n)
                        chain_states(n)
                        if n + 1 < JOBS:
                            scale_queries(n + 1)

                @block.scalar
                def _(act):
                    def logarithm(n):
                        act.wait_ge(gs["f"], n + 1)
                        nc.scalar.activation(log_f[:, n % 2, :], gate_of(n), ACT.Ln).then_inc(gs["ln"], 1)
                        nc.scalar.activation(gate_of(n), gate_of(n), ACT.Identity, scale=-1.0, bias=1.0)\
                            .then_inc(gs["k"], 1)

                    def exponentials(n):
                        d, x = n % 2, n % 2
                        act.wait_ge(gs["dist"], n + 1)
                        wait(act, gs["scores"], n - 1)
                        wait(act, gs["turned"], n - 1)
                        wait(act, gs["out"], n // 2 - 1)
                        nc.scalar.activation(q_ref[:, x, :], to_ref[:, x, :], ACT.Exp)
                        nc.scalar.activation(k_ref[:, x, :], to_ref[:, x, :], ACT.Exp, scale=-1.0)
                        nc.scalar.activation(q_cum[:, n % 4, :], cum[:, x, :], ACT.Exp)
                        nc.scalar.activation(decay[:, n % 4, :], by_chunk(cum[:, x, :])[:, :, LAST[d]], ACT.Exp)
                        nc.scalar.activation(k_end[:, x, :], log_f[:, x, :], ACT.Exp).then_inc(gs["exp"], 1)

                    def copy_turned(n):
                        act.wait_ge(gs["turned"], n + 1)
                        wait(act, gs["kv"], n)
                        for odd in range(2):
                            part = slice(64 * odd, 64 * odd + 64)
                            last = nc.scalar.copy(k_end_tok[part, odd:CH:2, :],
                                                  p_turned[part, 0:TOK].rearrange("p (c n) -> p c n", n=P))
                        last.then_inc(gs["turned_read"], 1)

                    def copy_out(h):
                        act.wait_ge(gs["out"], h + 1)
                        nc.scalar.copy(mixed_0[:, 4 + h, :], p_out[:, 0:TOK]).then_inc(gs["out_read"], 1)

                    act.wait_ge(gs["top"], 2)
                    nc.scalar.activation(bound[:, 1:3, :], bound[:, 1:3, :], ACT.Exp).then_inc(gs["bound_exp"], 1)
                    logarithm(0)
                    exponentials(0)
                    act.wait_ge(gs["zeroed"], 1)
                    for n in range(JOBS):
                        if n + 1 < JOBS:
                            logarithm(n + 1)
                        if n % 2 == 0 and n:
                            copy_out(n // 2 - 1)
                        copy_turned(n)
                        if n + 1 < JOBS:
                            exponentials(n + 1)
                    copy_out(GLA_H - 1)

                @block.gpsimd
                def _(pool):
                    for n in range(JOBS):
                        pool.wait_ge(gs["k"], n + 1)
                        pool.wait_ge(gs["exp"], n + 1)
                        for scaled in (k_end, k_ref):
                            nc.gpsimd.tensor_tensor(scaled[:, n % 2, :], scaled[:, n % 2, :], gate_of(n), ALU.mult)\
                                .then_inc(gs["k_scaled"], 1)

                @block.tensor
                def _(pe):
                    pe.wait_ge(gs["zeroed"], 1)
                    for n in range(JOBS):
                        h, d, x = n // 2, n % 2, n % 2
                        pe.wait_ge(gs["k_scaled"], 2 * n + 2)
                        wait(pe, gs["turned_read"], n)
                        for b in range(TOK // P):
                            mm = nc.tensor.transpose(p_turned[:, b * P:(b + 1) * P], k_end[:, x, b * P:(b + 1) * P],
                                                     ident[:])
                        mm.then_inc(gs["turned"], 1)
                        pe.wait_ge(gs["q_scaled"], n + 1)
                        wait(pe, gs["masked"], n)
                        for c in range(CH):
                            for half in range(2):
                                key = c * 64 + 32 * half
                                first, width = (0, 64) if half == d else (32 * half, 32)
                                part, col = slice(key % P, key % P + 32), (c // 2) * 64 + first
                                mm = nc.tensor.matmul(p_scores[part, col:col + width], k_ref[:, x, key:key + 32],
                                                      q_ref[:, x, c * 64 + first:c * 64 + first + width],
                                                      start=True, stop=True, tile_position=(0, key % P))
                        mm.then_inc(gs["scores"], 1)
                        pe.wait_ge(gs["turned_read"], n + 1)
                        wait(pe, gs["states"], n)
                        for c in range(CH):
                            mm = nc.tensor.matmul(p_kv[:, c * P:(c + 1) * P], k_end_tok[:, c, :],
                                                  i_tok[:, c // 2, h * P:(h + 1) * P], start=True, stop=True)
                        mm.then_inc(gs["kv"], 1)
                        if d == 1:
                            pe.wait_ge(gs["masked"], n + 1)
                            pe.wait_ge(gs["states"], n + 1)
                            wait(pe, gs["out_read"], h)
                            for c in range(CH):
                                tok = slice(c * 64, c * 64 + 64)
                                for e in range(2):
                                    nc.tensor.matmul(p_out[:, tok], state[:, e, c, :], q_cum[:, (n - 1 + e) % 4, tok],
                                                     start=e == 0, stop=False)
                                for e in range(2):
                                    mm = nc.tensor.matmul(p_out[:, tok], i_tok[:, c // 2, h * P:(h + 1) * P],
                                                          scores[:, e, c, :], start=False, stop=e == 1)
                            mm.then_inc(gs["out"], 1)

        head_norm("hgrn_norm", GLA_H, 1, TOK, lambda h, j: mixed_0[:, 4 + h, :], cols("hgrn_g"),
                  lambda h, j: g_silu[:, h, :])
        gla.close()

        with ExitStack() as scope:
            m_hi = sb(scope, "mixed_0_hi", [P, DC, TOK], F32R)
            m_lo = sb(scope, "mixed_0_lo", [P, DC, TOK], F32R)
            mixed_cut = cut(mixed_0, m_hi, m_lo, DC)
            linear("eo", m_hi, m_lo, feature_units(ALL), None,
                   add_residual(ALL, [gates_of(0, 0, 0), gates_of(0, 0, 1)], 2), mixed_cut)
        mix.close()

        with ExitStack() as scope:
            f_hi = sb(scope, "norm_b_hi", [P, DC, TOK], F32R)
            f_lo = sb(scope, "norm_b_lo", [P, DC, TOK], F32R)
            norm_b = norm_split(x_all, [group(0, 1, 0, 0, LAT), group(0, 1, 1, LAT, CTX)], f_hi, f_lo)
            feed_forward(0, f_hi, f_lo, ALL, add_residual(ALL, [gates_of(0, 1, 0), gates_of(0, 1, 1)], 1), norm_b)

        ret = ExitStack()
        ret_keys = ExitStack()
        k_ctx1 = sb(ret_keys, "ret_k_ctx", [P, DC, CTX])
        v_tok = sb(ret_keys, "ret_v", [P, TOK // P, 2048])
        with ExitStack() as scope:
            c_hi = sb(scope, "norm_c_hi", [P, DC, CTX], F32R)
            c_lo = sb(scope, "norm_c_lo", [P, DC, CTX], F32R)
            norm_c = norm_split(lambda c, s, m: x_ctx[0][:, c, s:s + m], [group(1, 0, 1, 0, CTX)], c_hi, c_lo)
            linear("ckv0", c_hi, c_lo, feature_units([(0, CTX)]), copy_units(k_ctx1, 0), source=norm_c)
            linear("ckv1", c_hi, c_lo, token_units(2), copy_token_units(v_tok, 2, LAT // P))
        ctx_scope.close()

        normed_1 = ExitStack()
        n1_hi = sb(normed_1, "norm_d_hi", [P, DC, LAT], F32R)
        n1_lo = sb(normed_1, "norm_d_lo", [P, DC, LAT], F32R)

        def x_only(c, s, m):
            return x_lat[:, c, s:s + m]

        norm_d = norm_split(x_only, [group(1, 0, 0, 0, LAT)], n1_hi, n1_lo)
        qk_ret = sb(ret, "ret_qk", [P, 2 * DC, LAT])
        with ExitStack() as scope:
            rope = sb(scope, "ret_rope", [P, 2, LAT])
            part = sb(scope, "ret_rope_parts", [P, 4, LAT])
            with stage_block() as block:
                @block.sync
                def _(sp):
                    sp.dma_start(rope[:], io["retrope"]).then_inc(rope_loaded, 16)
                    sp.wait_ge(rope_loaded, 16)

            def evac_rope(dve, t, j, count, res):
                dve.wait_ge(rope_turned, t + 1)
                for u in range(2):
                    dve.wait_ge(unit_done, count(u))
                    nc.vector.tensor_tensor(part[:, 2 * u, :], res[u][:, 0, :], rope[:, 0, :], ALU.mult)
                    nc.vector.tensor_tensor(part[:, 2 * u + 1, :], res[u][:, 0, :], rope[:, 1, :], ALU.mult)\
                        .then_inc(unit_free, 1)
                dve.wait_ge(unit_free, count(1))
                nc.vector.tensor_tensor(qk_ret[:, bass.ds(2 * t, 1), :].rearrange("p o n -> p (o n)"),
                                        part[:, 0, :], part[:, 3, :], ALU.subtract)
                nc.vector.tensor_tensor(qk_ret[:, bass.ds(2 * t + 1, 1), :].rearrange("p o n -> p (o n)"),
                                        part[:, 2, :], part[:, 1, :], ALU.add).then_inc(rope_turned, 1)

            linear("rqk", n1_hi, n1_lo, feature_units(ONLY_LAT), None, evac_rope, norm_d)
        linear("rv", n1_hi, n1_lo, token_units(4), copy_token_units(v_tok, 4))

        KB = TOK // P

        def ret_out(h, j):
            return qk_ret[:, 2 * h + j if j < 2 else 8 + 2 * h + j - 2, :]

        rs = {k: sem("ret_" + k) for k in ("table_0", "table_1", "scores", "decayed", "mixed", "mixed_read")}
        with ExitStack() as scope:
            table = sb(scope, "ret_decay", [P, 2, 12 * P])
            decayed = sb(scope, "ret_decayed", [P, 3, LAT])
            p_scores = psum(scope, "ret_p_scores", [P, 2, 512])
            p_mixed = psum(scope, "ret_p_mixed", [P, 4, 512])
            with stage_block() as block:
                @block.sync
                def _(sp):
                    for h in range(RET_H):
                        if h >= 2:
                            sp.wait_ge(rs["decayed"], (h - 1) * KB)
                        sp.dma_start(table[:, h % 2, :], io["decay"][h]).then_inc(rs[f"table_{h % 2}"], 16)

                @block.tensor
                def _(pe):
                    def scores(n):
                        h, b = divmod(n, KB)
                        if n >= 2:
                            pe.wait_ge(rs["decayed"], n - 1)
                        for j in range(2):
                            k = qk_ret[:, 8 + 2 * h + j, b * P:(b + 1) * P] if b < 4 else \
                                k_ctx1[:, 2 * h + j, (b - 4) * P:(b - 3) * P]
                            mm = nc.tensor.matmul(p_scores[:, n % 2, :], k, qk_ret[:, 2 * h + j, :],
                                                  start=j == 0, stop=j == 1)
                        mm.then_inc(rs["scores"], 1)

                    scores(0)
                    for n in range(RET_H * KB):
                        h, b = divmod(n, KB)
                        if n + 1 < RET_H * KB:
                            scores(n + 1)
                        pe.wait_ge(rs["decayed"], n + 1)
                        if b == 0 and h >= 1:
                            pe.wait_ge(rs["mixed_read"], h)
                        for e in range(4):
                            mm = nc.tensor.matmul(p_mixed[:, e, :], v_tok[:, b, h * 512 + e * P:h * 512 + (e + 1) * P],
                                                  decayed[:, n % 3, :], start=b == 0, stop=b == KB - 1)
                        mm.then_inc(rs["mixed"], 1)

                @block.vector
                def _(dve):
                    for n in range(RET_H * KB):
                        h, b = divmod(n, KB)
                        if b == 0:
                            dve.wait_ge(rs[f"table_{h % 2}"], 16 * (h // 2 + 1))
                        dve.wait_ge(rs["scores"], n + 1)
                        if n >= 3:
                            dve.wait_ge(rs["mixed"], n - 2)
                        at = (3 - b) * P if b < 4 else 7 * P + (5 - b) * P
                        nc.vector.tensor_tensor(decayed[:, n % 3, :], p_scores[:, n % 2, :],
                                                table[:, h % 2, at:at + LAT], ALU.mult).then_inc(rs["decayed"], 1)

                @block.scalar
                def _(act):
                    for h in range(RET_H):
                        act.wait_ge(rs["mixed"], (h + 1) * KB)
                        for e in range(4):
                            last = nc.scalar.copy(ret_out(h, e), p_mixed[:, e, :])
                        last.then_inc(rs["mixed_read"], 1)

        ret_keys.close()
        head_norm("ret_norm", RET_H, 4, LAT, ret_out)

        gate_sem = sem("gate_ready")
        gates_done = [0]

        def gate_linear(name, x_hi, x_lo, buf, func, other=None):
            n = shapes[name][0]
            base = gates_done[0]
            gates_done[0] += 2 * n
            with ExitStack() as scope:
                gate = sb(scope, f"{name}_gate", [P, 2, LAT])
                gated = sem(f"{name}_gated") if other is not None else None

                def evac_act(act, t, j, count, res):
                    for u in range(2):
                        act.wait_ge(unit_done, count(u))
                        act.wait_ge(unit_free, count(0) - 1)
                        nc.scalar.activation(gate[:, u, :], res[u][:, 0, :], func).then_inc(gate_sem, 1)

                def evac_dve(dve, t, j, count, res):
                    for u in range(2):
                        b = buf[:, bass.ds(2 * t + u, 1), :].rearrange("p o n -> p (o n)")
                        dve.wait_ge(gate_sem, 2 * t + (base + u + 1))
                        if other is None:
                            nc.vector.tensor_tensor(b, b, gate[:, u, :], ALU.mult).then_inc(unit_free, 1)
                        else:
                            o = other[:, bass.ds(2 * t + u, 1), :].rearrange("p o n -> p (o n)")
                            nc.vector.tensor_tensor(b, b, gate[:, u, :], ALU.mult).then_inc(gated, 1)
                            dve.wait_ge(gated, 2 * t + (u + 1))
                            nc.vector.tensor_tensor(o, o, b, ALU.add).then_inc(unit_free, 1)

                linear(name, x_hi, x_lo, feature_units(ONLY_LAT), evac_act, evac_dve)

        gate_linear("rg", n1_hi, n1_lo, qk_ret, ACT.Silu)
        normed_1.close()
        with ExitStack() as scope:
            m_hi = sb(scope, "mixed_1_hi", [P, 2 * DC, LAT], F32R)
            m_lo = sb(scope, "mixed_1_lo", [P, 2 * DC, LAT], F32R)
            mixed_cut = cut(qk_ret, m_hi, m_lo, 2 * DC)
            linear("ro", m_hi, m_lo, [("F", 0, ONLY_LAT)], None, add_residual(ONLY_LAT, [gates_of(1, 0, 0)], 1),
                   mixed_cut)
        ret.close()
        with ExitStack() as scope:
            f_hi = sb(scope, "norm_e_hi", [P, DC, LAT], F32R)
            f_lo = sb(scope, "norm_e_lo", [P, DC, LAT], F32R)
            norm_e = norm_split(x_only, [group(1, 1, 0, 0, LAT)], f_hi, f_lo)
            feed_forward(1, f_hi, f_lo, ONLY_LAT, add_residual(ONLY_LAT, [gates_of(1, 1, 0)], 1), norm_e)

        two = ExitStack()
        t_hi = sb(two, "norm_f_hi", [P, DC, LAT], F32R)
        t_lo = sb(two, "norm_f_lo", [P, DC, LAT], F32R)
        norm_f = norm_split(x_only, [(0, LAT, lambda c: scale_2[:, c:c + 1], lambda c: ada[:, c:c + 1])], t_hi, t_lo)

        NB = LAT // P
        y_a = sb(two, "y_a", [P, DC, LAT])
        dn = ExitStack()
        qkv = sb(dn, "dn_qkv", [P, 3 * DN_H, LAT])
        ba = sb(dn, "dn_beta_a", [P, NB, 16])
        with ExitStack() as scope:
            conv = sb(scope, "conv_sum", [P, 2, LAT])

            def evac_conv(dve, t, j, count, res):
                for u in range(2):
                    def tap(k):
                        c, _ = SMALL["conv"]
                        return small[:, bass.ds(8 * t + (c + 4 * u + k), 1)]

                    dve.wait_ge(unit_done, count(u))
                    dve.wait_ge(silu_sem, 2 * t + 2)
                    nc.vector.tensor_scalar(conv[:, u, :], res[u][:, 0, :], tap(3), None, ALU.mult).then_inc(conv_sem, 1)
                    for k in (2, 1, 0):
                        dve.wait_ge(conv_sem, 8 * t + (4 * u + 3 - k))
                        lag = 3 - k
                        last = nc.vector.scalar_tensor_tensor(conv[:, u, lag:], res[u][:, 0, 0:LAT - lag], tap(k),
                                                              conv[:, u, lag:], ALU.mult, ALU.add)
                        last.then_inc(conv_sem, 1)
                    dve.wait_ge(conv_sem, 8 * t + (4 * u + 4))
                    dve.sem_inc(unit_free, 1)

            def evac_silu(act, t, j, count, res):
                for u in range(2):
                    act.wait_ge(conv_sem, 8 * t + (4 * u + 4))
                    nc.scalar.activation(qkv[:, bass.ds(2 * t + u, 1), :].rearrange("p o n -> p (o n)"), conv[:, u, :],
                                         ACT.Silu).then_inc(silu_sem, 1)

            linear("dqkv", t_hi, t_lo, feature_units(ONLY_LAT), evac_silu, evac_conv, norm_f)

        def evac_ba(act, t, j, count, res):
            for b in range(NB):
                act.wait_ge(unit_done, count(b))
                nc.scalar.copy(ba[:, b, :], res[b][:, 0, 0:16]).then_inc(unit_free, 1)

        linear("dba", t_hi, t_lo, [("T", slice(b * P, (b + 1) * P), 0, 16) for b in range(NB)], evac_ba)

        dc = {k: sem("dn_" + k) for k in ("tables", "a", "abs", "exp", "log", "g", "cum", "ready")}
        beta = sb(dn, "dn_beta", [P, NB, DN_H])
        g_tok = sb(dn, "dn_g", [P, NB, DN_H])
        g_cum = sb(dn, "dn_g_cum", [P, NB, DN_H])
        upper = sb(dn, "upper", [P, P])
        levels = sb(dn, "levels", [P, 7, P])
        with ExitStack() as scope:
            a_in = sb(scope, "dn_a_in", [P, NB, DN_H])
            a_abs = sb(scope, "dn_a_abs", [P, NB, DN_H])
            rate = sb(scope, "dn_rate", [P, DN_H])
            p_cum = psum(scope, "dn_p_cum", [P, NB * DN_H])

            def per_head(ap):
                return ap.rearrange("p (o h) -> p o h", o=1).broadcast_to([P, NB, DN_H])

            with stage_block() as block:
                @block.sync
                def _(sp):
                    sp.dma_start(upper[:], io["upper"]).then_inc(dc["tables"], 16)
                    sp.dma_start(levels[:], io["levels"]).then_inc(dc["tables"], 16)
                    sp.wait_ge(dc["tables"], 32)

                @block.scalar
                def _(act):
                    nc.scalar.activation(beta[:], ba[:, :, 0:DN_H], ACT.Sigmoid)
                    nc.scalar.activation(rate[:], cols("a_log"), ACT.Exp)
                    act.wait_ge(dc["a"], 1)
                    nc.scalar.activation(a_abs[:], a_in[:], ACT.Abs).then_inc(dc["abs"], 1)
                    act.wait_ge(dc["abs"], 1)
                    nc.scalar.activation(a_abs[:], a_abs[:], ACT.Exp, scale=-1.0).then_inc(dc["exp"], 1)
                    act.wait_ge(dc["exp"], 1)
                    nc.scalar.activation(a_abs[:], a_abs[:], ACT.Ln, bias=1.0).then_inc(dc["log"], 1)

                @block.vector
                def _(dve):
                    nc.vector.tensor_tensor(a_in[:], ba[:, :, DN_H:2 * DN_H], per_head(cols("dt_bias")), ALU.add)\
                        .then_inc(dc["a"], 1)
                    dve.wait_ge(dc["log"], 1)
                    nc.vector.scalar_tensor_tensor(a_in[:], a_in[:], 0.0, a_abs[:], ALU.max, ALU.add).then_inc(dc["g"], 1)
                    dve.wait_ge(dc["g"], 1)
                    nc.vector.scalar_tensor_tensor(g_tok[:], a_in[:], -1.0, per_head(rate[:]), ALU.mult, ALU.mult)\
                        .then_inc(dc["g"], 1)
                    dve.wait_ge(dc["cum"], 1)
                    nc.vector.tensor_copy(g_cum[:].rearrange("p c h -> p (c h)"), p_cum[:]).then_inc(dc["ready"], 1)

                @block.tensor
                def _(pe):
                    pe.wait_ge(dc["tables"], 32)
                    pe.wait_ge(dc["g"], 2)
                    nc.tensor.matmul(p_cum[:], upper[:], g_tok[:].rearrange("p c h -> p (c h)"), start=True, stop=True)\
                        .then_inc(dc["cum"], 1)

        d = {k: sem("delta_" + k) for k in (
            "columns", "squares", "sums", "roots", "rstd", "unit", "spread", "distances", "exps", "small", "products",
            "turned", "tokens", "grams", "masked", "lower", "eye", "join", "half", "half_read", "step", "next",
            "solved", "solved_read", "seen", "written", "fresh", "stored", "out", "out_read", "gram_read")}
        pair_scope = ExitStack()

        def two_of(name, shape, count=2):
            return [sb(pair_scope, f"delta_{name}_{a}", shape) for a in range(count)]

        g_col, c_col, b_col = (two_of(n, [P, NB]) for n in ("g_col", "c_col", "b_col"))
        last_col, end_col, bg_col = (two_of(n, [P, NB]) for n in ("last_col", "end_col", "bg_col"))
        root = two_of("root", [P, 2, LAT])
        (q_unit, k_unit, v_copy, grow, low, high, k_beta, k_end_t, v_beta, join, inv, inv_t, half_t, fresh) = (
            two_of(n, [P, LAT]) for n in ("q_unit", "k_unit", "v_copy", "grow", "low", "high", "k_beta", "k_end",
                                         "v_beta", "join", "inv", "inv_t", "half_t", "fresh"))
        state2 = two_of("state", [P, P])
        banks = [[psum(pair_scope, f"delta_p{a}{b}", [P, LAT]) for b in range(4)] for a in range(2)]

        def ch(ap, c):
            return ap[:, c * P:(c + 1) * P]

        def chunks(ap):
            return ap.rearrange("p (c n) -> p c n", n=P)

        def over_cols(ap):
            return ap.rearrange("p (c o) -> p c o", o=1).broadcast_to([P, NB, P])

        def over_chunks(ap):
            return ap.rearrange("p (o n) -> p o n", o=1).broadcast_to([P, NB, P])

        with nc.Fori(0, DN_H // 2) as pair:
            with stage_block() as block:
                @block.vector
                def _(dve):
                    for s in d.values():
                        dve.sem_clear(s)

            def head(a, part):
                return qkv[:, bass.ds(2 * pair + (8 * part + a), 1), :].rearrange("p o n -> p (o n)")

            with stage_block() as block:
                @block.scalar
                def _(act):
                    for a in range(2):
                        nc.scalar.activation(root[a][:, 0, :], head(a, 0), ACT.Square)
                        nc.scalar.activation(root[a][:, 1, :], head(a, 1), ACT.Square).then_inc(d["squares"], 1)
                    for a in range(2):
                        act.wait_ge(d["sums"], a + 1)
                        for r in range(2):
                            last = nc.scalar.activation(root[a][:, r, :], banks[a][r][:], ACT.Sqrt, bias=eps_col)
                        last.then_inc(d["roots"], 1)
                    for a in range(2):
                        act.wait_ge(d["distances"], a + 1)
                        nc.scalar.activation(grow[a][:], banks[a][2][:], ACT.Exp)
                        nc.scalar.activation(low[a][:], low[a][:], ACT.Exp, scale=-1.0)
                        nc.scalar.activation(high[a][:], high[a][:], ACT.Exp)
                        nc.scalar.activation(end_col[a][:], end_col[a][:], ACT.Exp)
                        nc.scalar.activation(bg_col[a][:], c_col[a][:], ACT.Exp)
                        nc.scalar.activation(last_col[a][:], last_col[a][:], ACT.Exp).then_inc(d["exps"], 1)
                    for m in range(7):
                        for a in range(2):
                            n = 2 * m + a
                            act.wait_ge(d["half"], n + 1)
                            nc.scalar.copy(half_t[a][:], banks[a][0][:]).then_inc(d["half_read"], 1)
                    for a in range(2):
                        act.wait_ge(d["solved"], a + 1)
                        nc.scalar.copy(half_t[a][:], banks[a][0][:])
                        nc.scalar.copy(join[a][:], banks[a][1][:]).then_inc(d["solved_read"], 1)
                    for a in range(2):
                        act.wait_ge(d["out"], a + 1)
                        nc.scalar.copy(y_a[:, bass.ds(2 * pair + a, 1), :].rearrange("p o n -> p (o n)"), banks[a][3][:])\
                            .then_inc(d["out_read"], 1)

                @block.vector
                def _(dve):
                    for a in range(2):
                        for dst, src in ((g_col, g_tok), (c_col, g_cum), (b_col, beta)):
                            last = nc.vector.tensor_copy(dst[a][:].rearrange("p (c o) -> p c o", o=1),
                                                         src[:, :, bass.ds(2 * pair + a, 1)])
                        last.then_inc(d["columns"], 1)
                        nc.vector.tensor_copy(v_copy[a][:], head(a, 2)).then_inc(d["small"], 1)
                    for a in range(2):
                        dve.wait_ge(d["roots"], a + 1)
                        nc.vector.reciprocal(root[a][:], root[a][:]).then_inc(d["rstd"], 1)
                        dve.wait_ge(d["rstd"], a + 1)
                        nc.vector.scalar_tensor_tensor(q_unit[a][:], head(a, 0), P ** -0.5, root[a][:, 0, :],
                                                       ALU.mult, ALU.mult)
                        nc.vector.tensor_tensor(k_unit[a][:], head(a, 1), root[a][:, 1, :], ALU.mult)\
                            .then_inc(d["unit"], 1)
                    for a in range(2):
                        dve.wait_ge(d["spread"], a + 1)
                        spread = banks[a][2]
                        dve.wait_ge(d["columns"], a + 1)
                        nc.vector.tensor_copy(last_col[a][:], spread[:, P - 1:LAT:P]).then_inc(d["small"], 1)
                        for c in range(NB):
                            nc.vector.tensor_scalar(ch(low[a], c), ch(spread, c), c_col[a][:, c:c + 1], 0.0,
                                                    ALU.subtract, ALU.max)
                            nc.vector.tensor_scalar(ch(high[a], c), ch(spread, c), c_col[a][:, c:c + 1], 0.0,
                                                    ALU.subtract, ALU.min)
                        dve.wait_ge(d["small"], 2 + a + 1)
                        nc.vector.tensor_tensor(end_col[a][:], last_col[a][:], c_col[a][:], ALU.subtract)\
                            .then_inc(d["distances"], 1)
                    for a in range(2):
                        dve.wait_ge(d["exps"], a + 1)
                        nc.vector.tensor_tensor(bg_col[a][:], bg_col[a][:], b_col[a][:], ALU.mult).then_inc(d["small"], 1)
                        nc.vector.tensor_tensor(grow[a][:], grow[a][:], q_unit[a][:], ALU.mult)
                        dve.wait_ge(d["turned"], a + 1)
                        dve.wait_ge(d["small"], 4 + a + 1)
                        keys, values = banks[a][0], banks[a][1]
                        nc.vector.tensor_tensor(chunks(k_beta[a][:]), chunks(keys[:]), over_cols(bg_col[a][:]), ALU.mult)
                        nc.vector.tensor_tensor(chunks(k_end_t[a][:]), chunks(keys[:]), over_cols(end_col[a][:]), ALU.mult)
                        nc.vector.tensor_tensor(chunks(v_beta[a][:]), chunks(values[:]), over_cols(b_col[a][:]), ALU.mult)\
                            .then_inc(d["tokens"], 1)
                    for a in range(2):
                        dve.wait_ge(d["grams"], a + 1)
                        dve.wait_ge(d["masked"], 2 * a + 2)
                        nc.vector.tensor_tensor(high[a][:], banks[a][3][:], high[a][:], ALU.mult)
                        nc.vector.tensor_tensor(low[a][:], banks[a][2][:], low[a][:], ALU.mult).then_inc(d["lower"], 1)
                    for m in range(7):
                        for a in range(2):
                            n = 2 * m + a
                            dve.wait_ge(d["step"], n + 1)
                            if m < 6:
                                nc.vector.tensor_tensor(inv[a][:], inv[a][:], banks[a][1][:], ALU.subtract)
                            nc.vector.tensor_tensor(inv_t[a][:], inv_t[a][:], banks[a][3][:], ALU.subtract)\
                                .then_inc(d["next"], 1)
                    for c in range(NB):
                        for a in range(2):
                            if c:
                                dve.wait_ge(d["seen"], 2 * (c - 1) + a + 1)
                                nc.vector.tensor_tensor(ch(fresh[a], c), ch(half_t[a], c), banks[a][0][:, 0:P], ALU.subtract)\
                                    .then_inc(d["fresh"], 1)
                            else:
                                dve.wait_ge(d["solved_read"], a + 1)
                                nc.vector.tensor_copy(ch(fresh[a], c), ch(half_t[a], c)).then_inc(d["fresh"], 1)
                        for a in range(2):
                            if c < NB - 1:
                                dve.wait_ge(d["written"], 2 * c + a + 1)
                                if c:
                                    nc.vector.scalar_tensor_tensor(state2[a][:], state2[a][:], last_col[a][:, c:c + 1],
                                                                   banks[a][1][:, 0:P], ALU.mult, ALU.add)\
                                        .then_inc(d["stored"], 1)
                                else:
                                    nc.vector.tensor_copy(state2[a][:], banks[a][1][:, 0:P]).then_inc(d["stored"], 1)

                @block.gpsimd
                def _(pool):
                    for a in range(2):
                        for m in (inv, inv_t):
                            nc.gpsimd.tensor_copy(chunks(m[a][:]), over_chunks(ident[:])).then_inc(d["eye"], 1)
                    for a in range(2):
                        pool.wait_ge(d["exps"], a + 1)
                        nc.gpsimd.tensor_tensor(chunks(high[a][:]), chunks(high[a][:]), over_chunks(upper[:]), ALU.mult)\
                            .then_inc(d["masked"], 1)
                        pool.wait_ge(d["columns"], a + 1)
                        nc.gpsimd.tensor_tensor(chunks(low[a][:]), chunks(low[a][:]), over_cols(b_col[a][:]), ALU.mult)\
                            .then_inc(d["masked"], 1)
                    for m in range(7):
                        for a in range(2):
                            n = 2 * m + a
                            pool.wait_ge(d["lower"], a + 1)
                            if m:
                                pool.wait_ge(d["half"], n - 1)
                            nc.gpsimd.tensor_tensor(chunks(join[a][:]), chunks(low[a][:]), over_chunks(levels[:, m, :]),
                                                    ALU.mult).then_inc(d["join"], 1)

                @block.tensor
                def _(pe):
                    for a in range(2):
                        pe.wait_ge(d["squares"], a + 1)
                        for r in range(2):
                            mm = nc.tensor.matmul(banks[a][r][:], ones[:], root[a][:, r, :], start=True, stop=True)
                        mm.then_inc(d["sums"], 1)
                        pe.wait_ge(d["columns"], a + 1)
                        for c in range(NB):
                            mm = nc.tensor.matmul(ch(banks[a][2], c), g_col[a][:, c:c + 1].broadcast_to([P, P]), upper[:],
                                                  start=True, stop=True)
                        mm.then_inc(d["spread"], 1)
                    for a in range(2):
                        pe.wait_ge(d["unit"], a + 1)
                        pe.wait_ge(d["small"], a + 1)
                        for c in range(NB):
                            nc.tensor.transpose(ch(banks[a][0], c), ch(k_unit[a], c), ident[:])
                        for c in range(NB):
                            mm = nc.tensor.transpose(ch(banks[a][1], c), ch(v_copy[a], c), ident[:])
                        mm.then_inc(d["turned"], 1)
                    for a in range(2):
                        pe.wait_ge(d["exps"], a + 1)
                        for c in range(NB):
                            nc.tensor.matmul(ch(banks[a][2], c), ch(k_unit[a], c), ch(k_unit[a], c), start=True, stop=True)
                        for c in range(NB):
                            mm = nc.tensor.matmul(ch(banks[a][3], c), ch(k_unit[a], c), ch(q_unit[a], c), start=True, stop=True)
                        mm.then_inc(d["grams"], 1)
                    pe.wait_ge(d["eye"], 4)
                    for a in range(2):
                        pe.wait_ge(d["tokens"], a + 1)
                    def half_step(m, a):
                        n = 2 * m + a
                        pe.wait_ge(d["join"], n + 1)
                        if m:
                            pe.wait_ge(d["next"], n - 1)
                        for c in range(NB):
                            mm = nc.tensor.matmul(ch(banks[a][0], c), ch(join[a], c), ch(inv_t[a], c), start=True, stop=True)
                        mm.then_inc(d["half"], 1)

                    def full_step(m, a):
                        n = 2 * m + a
                        pe.wait_ge(d["half_read"], n + 1)
                        for c in range(NB):
                            if m < 6:
                                nc.tensor.matmul(ch(banks[a][1], c), ch(half_t[a], c), ch(inv[a], c), start=True, stop=True)
                        for c in range(NB):
                            mm = nc.tensor.matmul(ch(banks[a][3], c), ch(inv[a], c), ch(half_t[a], c), start=True, stop=True)
                        mm.then_inc(d["step"], 1)

                    for m in range(7):
                        half_step(m, 0)
                        half_step(m, 1)
                        full_step(m, 0)
                        full_step(m, 1)
                    for a in range(2):
                        pe.wait_ge(d["next"], 12 + a + 1)
                        for c in range(NB):
                            nc.tensor.matmul(ch(banks[a][0], c), ch(inv_t[a], c), ch(v_beta[a], c), start=True, stop=True)
                        for c in range(NB):
                            mm = nc.tensor.matmul(ch(banks[a][1], c), ch(k_beta[a], c), ch(inv_t[a], c), start=True, stop=True)
                        mm.then_inc(d["solved"], 1)
                    for c in range(NB):
                        for a in range(2):
                            pe.wait_ge(d["solved_read"], a + 1)
                            if c:
                                pe.wait_ge(d["stored"], 2 * (c - 1) + a + 1)
                                nc.tensor.matmul(banks[a][0][:, 0:P], ch(join[a], c), state2[a][:], start=True, stop=True)\
                                    .then_inc(d["seen"], 1)
                        for a in range(2):
                            pe.wait_ge(d["fresh"], 2 * c + a + 1)
                            if c:
                                nc.tensor.matmul(ch(banks[a][3], c), state2[a][:], ch(grow[a], c), start=True, stop=False)
                            if c < NB - 1:
                                nc.tensor.matmul(banks[a][1][:, 0:P], ch(k_end_t[a], c), ch(fresh[a], c), start=True, stop=True)\
                                    .then_inc(d["written"], 1)
                            mm = nc.tensor.matmul(ch(banks[a][3], c), ch(fresh[a], c), ch(high[a], c), start=c == 0, stop=True)
                            if c == NB - 1:
                                mm.then_inc(d["out"], 1)
        pair_scope.close()
        dn.close()

        head_norm("dn_norm", DN_H, 1, LAT, lambda h, j: y_a[:, h, :], cols("dn_w"))
        gate_linear("dz", t_hi, t_lo, y_a, ACT.Silu)

        with ExitStack() as scope:
            m_hi = sb(scope, "delta_hi", [P, DC, LAT], F32R)
            m_lo = sb(scope, "delta_lo", [P, DC, LAT], F32R)
            delta_cut = cut(y_a, m_hi, m_lo, DC)
            linear("pa", m_hi, m_lo, feature_units(ONLY_LAT), copy_units(y_a, 0), source=delta_cut)
        gate_linear("ga", t_hi, t_lo, y_a, ACT.Sigmoid)

        WC = 6
        y_b = sb(two, "y_b", [P, WC, LAT])
        lse = sb(two, "dil_lse", [P, 4, 2 * WC])
        dil_scope = ExitStack()
        qk_t = sb(dil_scope, "dil_qk", [P, 2 * WC, P + LAT])
        v_t = sb(dil_scope, "dil_v", [P, 5, 2 * WC * 64])
        q_zero_t = sb(dil_scope, "dil_q_zero", [P, 2 * WC, P])
        near = sb(dil_scope, "dil_near", [P, 4, 2 * P])
        dil = sb(dil_scope, "dil_masks", [P, 2, P])
        dil_tables, dil_zeroed = sem("dil_tables"), sem("dil_zeroed")
        with stage_block() as block:
            @block.sync
            def _(sp):
                sp.dma_start(near[:], io["near"]).then_inc(dil_tables, 16)
                sp.dma_start(dil[:], io["dil"]).then_inc(dil_tables, 16)
                sp.wait_ge(dil_tables, 32)

            @block.vector
            def _(dve):
                nc.vector.memset(qk_t[:, :, 0:P], 0.0)
                nc.vector.memset(v_t[:, 0, :], 0.0)
                nc.vector.memset(q_zero_t[:], 0.0).then_inc(dil_zeroed, 1)

        def evac_tqk(act, t, j, count, res):
            for u in range(2):
                act.wait_ge(unit_done, count(u))
                nc.scalar.copy(qk_t[:, bass.ds(2 * t + u, 1), P:P + LAT], res[u][:, 0:1, :]).then_inc(unit_free, 1)

        def value_units(t):
            return [("T", slice(b * P, (b + 1) * P) if t == 0 else slice(b, LAT, 4), 0, 256) for b in range(4)]

        linear("tqk", t_hi, t_lo, feature_units(ONLY_LAT), evac_tqk)
        linear("tv", t_hi, t_lo, value_units, copy_token_units(v_t, 4, 1))

        def strided(first):
            return bass.ds(first, P, 4)

        def dilated_head(h):
            g, c = h // 4, h // 2
            cols64 = slice(64 * h, 64 * h + 64)

            def keys(i):
                if g == 0:
                    return [(0, 2 * P, qk_t[:, WC + c, bass.ds(i * P, 2 * P)],
                             near[:, bass.ds(i, 1), :].rearrange("p o n -> p (o n)"))]
                return [(0, P, qk_t[:, WC + c, strided(i + P)], dil[:, g - 1, :])]

            def values(i):
                return [v_t[:, bass.ds(i + b, 1), cols64].rearrange("p o n -> p (o n)")
                        for b in ((0, 1) if g == 0 else (1,))]

            return dict(q=q_zero_t[:, h, :], keys=keys, values=values, column=64 * h, sink=None)

        def dilated_queries(i):
            copies = []
            for half in range(2):
                part = slice(64 * half, 64 * half + 64)
                copies += [(q_zero_t[part, half:4:2, :], qk_t[part, 0:2, bass.ds(i * P + P, P)]),
                           (q_zero_t[part, 4 + half:12:2, :], qk_t[part, 2:WC, strided(i + P)])]
            return copies

        def dilated_results(i, p_out):
            out = p_out[:, 0:WC * P].rearrange("p (c n) -> p c n", n=P)
            return [(y_b[:, 0:2, bass.ds(i * P, P)], out[:, 0:2, :]), (y_b[:, 2:WC, strided(i)], out[:, 2:WC, :])]

        attend("dil", 4, [dilated_head(h) for h in range(2 * WC)], dilated_queries, dilated_results,
               2 * P, 2, WC * P, 64.0 ** -0.5, lse)
        dil_scope.close()

        gw = {k: sem("groups_" + k) for k in ("pair", "turned", "logs", "max", "shifted", "exp", "sum", "weights",
                                             "spread")}
        with ExitStack() as scope:
            pair_of = sb(scope, "groups_pair", [P, 2, P])
            logs = sb(scope, "groups_logs", [4, 3, LAT])
            top_log = sb(scope, "groups_top", [4, LAT])
            p_logs = psum(scope, "groups_p_logs", [P, 3, 512])
            p_spread = psum(scope, "groups_p_spread", [P, 5, 512])

            def over_groups(ap):
                return ap.rearrange("p (o n) -> p o n", o=1).broadcast_to([4, 3, LAT])

            with stage_block() as block:
                @block.sync
                def _(sp):
                    sp.dma_start(pair_of[:], io["pair"]).then_inc(gw["pair"], 16)

                @block.tensor
                def _(pe):
                    for g in range(3):
                        for i in range(4):
                            mm = nc.tensor.transpose(p_logs[0:4, g, i * P:(i + 1) * P], lse[:, i, 4 * g:4 * g + 4],
                                                     ident[:])
                    mm.then_inc(gw["turned"], 1)
                    pe.wait_ge(gw["pair"], 16)
                    pe.wait_ge(gw["weights"], 1)
                    for c in range(WC):
                        if c == 5:
                            pe.wait_ge(gw["spread"], 1)
                        nc.tensor.matmul(p_spread[:, c % 5, :], pair_of[0:4, c % 2, :], logs[:, c // 2, :],
                                         start=True, stop=True).then_inc(gw["turned"], 1)

                @block.scalar
                def _(act):
                    act.wait_ge(gw["shifted"], 1)
                    nc.scalar.activation(logs[:], logs[:], ACT.Exp).then_inc(gw["exp"], 1)

                @block.vector
                def _(dve):
                    dve.wait_ge(gw["turned"], 1)
                    nc.vector.tensor_copy(logs[:, 0, :], p_logs[0:4, 0, :])
                    nc.vector.tensor_copy(logs[:, 1:3, :].rearrange("p g (n r) -> p g r n", r=4),
                                          p_logs[0:4, 1:3, :].rearrange("p g (r n) -> p g r n", r=4))\
                        .then_inc(gw["logs"], 1)
                    dve.wait_ge(gw["logs"], 1)
                    nc.vector.tensor_tensor(top_log[:], logs[:, 0, :], logs[:, 1, :], ALU.max).then_inc(gw["max"], 1)
                    dve.wait_ge(gw["max"], 1)
                    nc.vector.tensor_tensor(top_log[:], top_log[:], logs[:, 2, :], ALU.max).then_inc(gw["max"], 1)
                    dve.wait_ge(gw["max"], 2)
                    nc.vector.tensor_tensor(logs[:], logs[:], over_groups(top_log[:]), ALU.subtract)\
                        .then_inc(gw["shifted"], 1)
                    dve.wait_ge(gw["exp"], 1)
                    nc.vector.tensor_tensor(top_log[:], logs[:, 0, :], logs[:, 1, :], ALU.add).then_inc(gw["sum"], 1)
                    dve.wait_ge(gw["sum"], 1)
                    nc.vector.tensor_tensor(top_log[:], top_log[:], logs[:, 2, :], ALU.add).then_inc(gw["sum"], 1)
                    dve.wait_ge(gw["sum"], 2)
                    nc.vector.reciprocal(top_log[:], top_log[:]).then_inc(gw["sum"], 1)
                    dve.wait_ge(gw["sum"], 3)
                    nc.vector.tensor_tensor(logs[:], logs[:], over_groups(top_log[:]), ALU.mult)\
                        .then_inc(gw["weights"], 1)
                    for c in range(WC):
                        dve.wait_ge(gw["turned"], c + 2)
                        nc.vector.tensor_tensor(y_b[:, c, :], y_b[:, c, :], p_spread[:, c % 5, :], ALU.mult)\
                            .then_inc(gw["spread"], 1)

        gate_linear("tz", t_hi, t_lo, y_b, ACT.Silu)

        merge = ExitStack()
        y_proj = sb(merge, "y_b_projected", [P, DC, LAT])
        with ExitStack() as scope:
            m_hi = sb(scope, "dilated_hi", [P, WC, LAT], F32R)
            m_lo = sb(scope, "dilated_lo", [P, WC, LAT], F32R)
            dilated_cut = cut(y_b, m_hi, m_lo, WC)
            linear("pb", m_hi, m_lo, feature_units(ONLY_LAT), copy_units(y_proj, 0), source=dilated_cut)
        gate_linear("gb", t_hi, t_lo, y_proj, ACT.Sigmoid, y_a)
        merge.close()
        with ExitStack() as scope:
            m_hi = sb(scope, "merged_hi", [P, DC, LAT], F32R)
            m_lo = sb(scope, "merged_lo", [P, DC, LAT], F32R)
            merged_cut = cut(y_a, m_hi, m_lo, DC)
            linear("wo", m_hi, m_lo, feature_units(ONLY_LAT), None, add_residual(ONLY_LAT, [ada[:, 16:24]], 2),
                   merged_cut)
        two.close()
        head_norm("final", 1, DC, LAT, lambda h, j: x_lat[:, j, :], lambda j: cols("final_w")[:, j:j + 1])
        with stage_block() as block:
            @block.sync
            def _(sp):
                sp.dma_start(io["y"], x_lat[:]).then_inc(stored, 16)
                sp.wait_ge(stored, 16)


def layout(inp):
    f = {k: np.asarray(v) for k, v in inp.items()}

    def fm(a):
        return np.ascontiguousarray(a.reshape(a.shape[0] // P, P, -1).transpose(1, 0, 2))

    def col(a):
        return a.reshape(-1, P).T

    def rows(a):
        return np.broadcast_to(a.reshape(1, -1), (P, a.size))

    def tiles(w, nt=256):
        k, n = w.shape
        w = w.reshape(k // P, P, n // nt, nt).transpose(2, 1, 0, 3)
        return np.ascontiguousarray(w).reshape(n // nt, P, -1)

    out = dict(constants())
    out["x"] = fm(f["x"][0].T)
    out["ctx"] = fm(f["ctx"][0].T)
    parts = dict(
        mod_b=col(f["mod_b"].reshape(-1)), ada_b=col(f["ada_b_2"][0]), norm_g=col(f["norm_g"].reshape(-1)),
        norm_w=col(f["norm_w_2"][0]), final_w=col(f["final_norm_w_2"]),
        qk_g=np.tile(f["attn_qk_norm_g"][0].T, (2, 1)), sink=rows(f["attn_sink"][0]),
        lb=col(f["hgrn_lb"].reshape(-1)), hgrn_g=f["hgrn_out_norm_g"][0].reshape(P, 1),
        conv=f["conv_w_2"][0].reshape(4, 24, P).transpose(2, 1, 0).reshape(P, 96),
        a_log=rows(f["a_log_2"][0]), dt_bias=rows(f["dt_bias_2"][0]), dn_w=f["dn_norm_w_2"][0].reshape(P, 1),
        cond=np.concatenate([col(f["c"][0]), col(f["c_ctx"])], 1), cond_2=col(f["c_2"][0]),
        eps=np.full((P, 1), EPS, np.float32))
    out["small"] = np.concatenate([parts[k] for k in SMALL], axis=1)

    out["w_mod"] = np.concatenate([tiles(f["mod_w"][0]), tiles(f["mod_w"][1]), tiles(f["ada_w_2"][0])])
    w = f["even_w_in"][0]
    wq = w[:, 0:512].reshape(D, 2, 4, 64).transpose(0, 2, 1, 3).reshape(D, 512)
    out["w_aq"], out["w_akv"] = tiles(wq), tiles(w[:, 512:768])
    out["w_bq"], out["w_bf"] = tiles(w[:, 768:1280]), tiles(w[:, 1280:2304])
    out["w_bi"], out["w_bg"] = tiles(w[:, 2304:2816]), tiles(w[:, 2816:3328])
    w = f["even_w_out"][0]
    wa = w[0:512].reshape(2, 4, 64, D).transpose(1, 0, 2, 3).reshape(512, D)
    out["w_eo"] = tiles(np.concatenate([wa, w[512:]], axis=0))
    for layer in (0, 1):
        w = f["ffn_w_in"][layer].reshape(DC, P, 2, FFN // P, P).transpose(3, 1, 0, 2, 4)
        w = np.ascontiguousarray(w).reshape(FFN // P, P, -1)
        wo = f["ffn_w_out"][layer].reshape(2, HALF * P, D)
        for half in (0, 1):
            out[f"w_f{layer}i{half}"] = w[half * HALF:(half + 1) * HALF]
            out[f"w_f{layer}o{half}"] = tiles(wo[half], P)
    w = f["odd_w_in"][0]
    out["w_rqk"], out["w_rv"] = tiles(w[:, 0:2048]), tiles(w[:, 2048:4096])
    wg = w[:, 4096:].reshape(D, RET_H, 2, 256).transpose(0, 2, 1, 3).reshape(D, 2048)
    out["w_rg"] = tiles(wg)
    wo = f["odd_w_out"][0].reshape(RET_H, 2, 256, D).transpose(1, 0, 2, 3).reshape(2048, D)
    out["w_ro"] = tiles(wo, P)
    w = f["w_in_2"][0]
    out["w_dqkv"], out["w_dz"], out["w_dba"] = tiles(w[:, 0:3072]), tiles(w[:, 3072:4096]), tiles(w[:, 4096:4112], 16)
    out["w_tqk"], out["w_tv"], out["w_tz"] = tiles(w[:, 4112:5648]), tiles(w[:, 5648:6416]), tiles(w[:, 6416:7184])
    out["w_ga"], out["w_gb"] = tiles(w[:, 7184:8208]), tiles(w[:, 8208:9232])
    out["w_pa"], out["w_pb"], out["w_wo"] = tiles(f["w_proj_a_2"][0]), tiles(f["w_proj_b_2"][0]), tiles(f["w_out_2"][0])
    return out


def kernel(**inputs):
    import concourse.bacc as bacc
    from concourse.bass_utils import run_bass_kernel_spmd

    nc = bacc.Bacc("TRN2", target_bir_lowering=False, num_devices=1)
    arrays = {"in_" + k: np.ascontiguousarray(a) for k, a in layout(inputs).items()}
    io = {k[3:]: nc.dram_tensor(k, a.shape, mybir.dt.from_np(a.dtype), kind="ExternalInput").ap()
          for k, a in arrays.items()}
    io["y"] = nc.dram_tensor("y", (P, DC, LAT), F32, kind="ExternalOutput").ap()
    program(nc, io)
    got = run_bass_kernel_spmd(nc, [arrays], core_ids=[0]).results[0]["y"]
    return np.ascontiguousarray(got.transpose(2, 1, 0).reshape(1, LAT, D))
```

```python
from contextlib import ExitStack

import numpy as np

import concourse.bass as bass
from concourse import mybir

F32 = mybir.dt.float32
F32R = mybir.dt.float32r
U32 = mybir.dt.uint32
ALU = mybir.AluOpType
ACT = mybir.ActivationFunctionType
AX_X = mybir.AxisListType.X

P = 128
D = 1024
DC = D // P
LAT, CTX = 512, 256
TOK = LAT + CTX
EPS = 1e-6
FFN = 2816
HALF = FFN // P // 2
SLOT = 2048
RET_H = 4
GLA_H = 4
DN_H = 8
NEG = -1e30


def constants():
    f = np.float32
    p = np.arange(P)
    out = {}
    out["ident"] = np.eye(P, dtype=f)
    out["ones"] = np.ones((P, P), f)
    out["ones64"] = np.kron(np.eye(2), np.ones((64, 64))).astype(f)
    rot = np.zeros((P, P), f)
    for b in (0, 64):
        for i in range(32):
            rot[b + i, b + 32 + i] = -1.0
            rot[b + 32 + i, b + i] = 1.0
    out["rotT"] = np.ascontiguousarray(rot.T)
    out["upper"] = (p[:, None] <= p[None, :]).astype(f)
    tok = np.arange(LAT)
    inv = f(10000.0) ** (-np.arange(16, dtype=f) / f(16))
    ang = np.concatenate([(tok // 64).astype(f)[:, None] * inv, (tok % 64).astype(f)[:, None] * inv], axis=-1)
    out["axial"] = np.stack([np.tile(np.cos(ang).T, (4, 1)), np.tile(np.sin(ang).T, (4, 1))], 1).astype(f)
    theta = f(1.0) / (f(10000.0) ** np.linspace(0.0, 1.0, P, dtype=f))
    ang = tok.astype(f)[:, None] * theta
    out["retrope"] = np.stack([np.cos(ang).T, np.sin(ang).T], 1).astype(f)
    q, k = p[:, None], np.arange(3 * P)[None, :]
    win = np.where((k >= q) & (k <= q + 2 * P), 0.0, NEG)
    four = np.stack([win] * 4, 1)
    four[:, 0, :P] = NEG
    four[:, 3, 2 * P:] = NEG
    out["window"] = four.astype(f)
    s, t = (p % 64)[:, None], np.arange(64)[None, :]
    out["tri64"] = np.stack([s <= t, s >= t], 1).astype(f)
    out["restart"] = np.broadcast_to((np.arange(TOK) % 64 != 0).astype(f), (P, TOK)).copy()
    g = np.log(1.0 - 2.0 ** (-5.0 - np.arange(RET_H, dtype=np.float64)))
    lat_u = (np.arange(7 * P) - 3 * P)[None, :] - p[:, None]
    ctx_u = (np.arange(5 * P) + P)[None, :] - p[:, None]
    tables = []
    for h in range(RET_H):
        fw, bw = g[h], g[RET_H - 1 - h]
        lat = np.where(lat_u >= 0, np.exp(fw * np.maximum(lat_u, 0)), 0.0)
        lat = lat + np.where(lat_u <= 0, np.exp(bw * np.maximum(-lat_u, 0)), 0.0)
        tables.append(np.concatenate([lat, np.exp(fw * ctx_u) + np.exp(bw * (LAT + CTX - ctx_u))], 1))
    out["decay"] = (np.stack(tables) * 256.0 ** -0.5).astype(f)
    lev = [((p[:, None] // (2 * b) == p[None, :] // (2 * b)) & (p[:, None] // b % 2 == 1)
            & (p[None, :] // b % 2 == 0)) for b in (1, 2, 4, 8, 16, 32, 64)]
    out["levels"] = np.stack(lev, 1).astype(f)
    k = np.arange(2 * P)[None, :]
    near = np.where((k >= q) & (k <= q + P), 0.0, NEG)
    first = np.where((k >= P) & (k <= q + P), 0.0, NEG)
    k = np.arange(P)[None, :]
    dil4 = np.where(k <= q, 0.0, NEG)
    dil16 = np.where((k <= q) & (k % 4 == q % 4), 0.0, NEG)
    out["near"] = np.stack([first, near, near, near], 1).astype(f)
    out["dil"] = np.stack([dil4, dil16], 1).astype(f)
    pair = np.zeros((P, 2, P), f)
    for s in range(4):
        pair[s, s // 2, (s % 2) * 64:(s % 2) * 64 + 64] = 1.0
    out["pair"] = pair
    return out


SMALL = {}
_at = 0
for _name, _width in (("mod_b", 96), ("ada_b", 24), ("norm_g", 32), ("norm_w", 8), ("final_w", 8),
                      ("qk_g", 2), ("sink", 8), ("lb", 8), ("hgrn_g", 1), ("conv", 96), ("a_log", 8),
                      ("dt_bias", 8), ("dn_w", 1), ("cond", 16), ("cond_2", 8), ("eps", 1)):
    SMALL[_name] = (_at, _at + _width)
    _at += _width
SMALLS = _at

STREAM = [("aq", 2, 8, 256), ("akv", 1, 8, 256), ("bq", 2, 8, 256),
          ("bg", 2, 8, 256), ("bf", 4, 8, 256), ("bi", 2, 8, 256), ("eo", 4, 8, 256)]
STREAM += [(f"f0{part}{half}", *shape) for half in (0, 1)
           for part, shape in (("i", (HALF, 8, 256)), ("o", (8, HALF, 128)))]
STREAM += [("ckv0", 4, 8, 256), ("ckv1", 8, 8, 256), ("rqk", 8, 8, 256), ("rv", 8, 8, 256),
           ("rg", 8, 8, 256), ("ro", 8, 16, 128)]
STREAM += [(f"f1{part}{half}", *shape) for half in (0, 1)
           for part, shape in (("i", (HALF, 8, 256)), ("o", (8, HALF, 128)))]
STREAM += [("dqkv", 12, 8, 256), ("dba", 1, 8, 16), ("dz", 4, 8, 256), ("pa", 4, 8, 256), ("ga", 4, 8, 256),
           ("tqk", 6, 8, 256), ("tv", 3, 8, 256), ("tz", 3, 8, 256), ("pb", 4, 6, 256), ("gb", 4, 8, 256),
           ("wo", 4, 8, 256)]
SHARED = {"ckv0": ("rqk", 4), "ckv1": ("rv", 0)}


class Ring:

    def __init__(self, plan):
        self.plan = plan
        self.tile = 0
        self.buffers = None
        self.begun = False
        self.issued = 0
        self.split = 0
        self.unit = 8


class Map:

    def __init__(self, first, end):
        self.free = [(first, end)]

    def take(self, size):
        for n, (a, b) in enumerate(self.free):
            if b - a >= size:
                self.free[n:n + 1] = [(a + size, b)] if b - a > size else []
                return a
        raise ValueError(f"no room for {size} bytes in {self.free}")

    def give(self, at, size):
        joined = []
        for a, b in sorted(self.free + [(at, at + size)]):
            if joined and joined[-1][1] == a:
                joined[-1] = (joined[-1][0], b)
            else:
                joined.append((a, b))
        self.free = joined


def wait(eng, sem, count):
    if not isinstance(count, int) or count > 0:
        eng.wait_ge(sem, count)


def over_tiles(eng, n, body, peel=0):
    pairs = (n - 1) // 2
    first = min(peel, pairs)
    if pairs - first == 1:
        first = pairs
    for t in range(2 * first):
        body(t, t % 2, False)
    if pairs > first:
        with eng.Fori(first, pairs) as i:
            body(2 * i, 0, False)
            body(2 * i + 1, 1, False)
    for t in range(2 * pairs, n):
        body(t, t % 2, t == n - 1)


def program(nc, io):
    plan = []
    for name, n, kc, nt in STREAM:
        src, first = SHARED.get(name, (name, 0))
        plan += [(io["w_" + src], first + t, kc * nt) for t in range(n)]
    shapes = {name: (n, kc, nt) for name, n, kc, nt in STREAM}
    ring = Ring(plan)
    room = Map(-(-nc.sbuf_base // 32) * 32, nc.sbuf_top // 32 * 32)

    with ExitStack() as top:
        def sem(name):
            return top.enter_context(nc.semaphore(name))

        def sb(scope, name, shape, dtype=F32):
            size = -(-int(np.prod(shape[1:])) * 4 // 32) * 32
            at = room.take(size)
            scope.callback(room.give, at, size)
            return nc.alloc_sbuf_tensor_at(name, shape, dtype, offset=at)

        def psum(scope, name, shape):
            return scope.enter_context(nc.psum_tensor(name, shape, F32))

        def stage_block():
            return nc.Block(no_gpsimd_drain=True)

        small = sb(top, "small", [P, SMALLS])
        ident = sb(top, "ident", [P, P])
        ones = sb(top, "ones", [P, P])
        stage = sb(top, "stage", [P, 2, SLOT])
        x_lat = sb(top, "x_lat", [P, DC, LAT])
        mods = sb(top, "mods", [P, 2, 48, 2])
        ada = sb(top, "ada", [P, 24])
        scale_of = sb(top, "scale_of", [P, 2, 2, 2, DC])
        scale_2 = sb(top, "scale_2", [P, DC])

        def cols(name):
            a, b = SMALL[name]
            return small[:, a:b]

        eps_col = cols("eps")

        small_loaded, loaded = sem("vectors_loaded"), sem("inputs_loaded")
        w_landed = [sem("weights_landed_0"), sem("weights_landed_1")]
        hi_ready = sem("weights_hi_ready")
        lo_ready = sem("weights_lo_ready")
        unit_done = sem("unit_summed")
        unit_free = sem("unit_read")
        stored = sem("output_stored")

        def issue(sp, parity_of, t_expr, src, index, words):
            wait(sp, lo_ready, t_expr - 1)
            sp.dma_start(stage[:, parity_of, 0:words], src[bass.ds(index, 1)].rearrange("o p n -> p (o n)"))\
                .then_inc(w_landed[parity_of], 16)

        def issue_next(sp, upto_tile):
            while ring.issued < min(upto_tile, len(plan)):
                src, index, words = plan[ring.issued]
                issue(sp, ring.issued % 2, ring.issued, src, index, words)
                ring.issued += 1

        def issue_stage(sp, n):
            if ring.issued == ring.tile + 2 and n > 4:
                src, first, words = plan[ring.issued]
                base = ring.issued
                pairs = (n - 2) // 2
                with sp.Fori(0, pairs) as i:
                    for j in range(2):
                        issue(sp, (base + j) % 2, 2 * i + (base + j), src, 2 * i + (first + j), words)
                ring.issued += 2 * pairs
            issue_next(sp, ring.tile + n + 2)

        def landed(eng, t, parity):
            slot = (ring.tile + parity) % 2
            half = (t - parity) // 2 if isinstance(t, int) else None
            first = (ring.tile + parity) // 2 + 1
            if half is not None:
                eng.wait_ge(w_landed[slot], 16 * (first + half))
            else:
                eng.wait_ge(w_landed[slot], 8 * (t - parity) + 16 * first)
            return slot

        used_before = set()

        def counted_from(sems, first):
            again = id(sems) in used_before
            used_before.add(id(sems))
            if again or first:
                with stage_block() as block:
                    @block.vector
                    def _(dve):
                        for k, s in sems.items():
                            if again:
                                dve.sem_clear(s)
                            if k in first:
                                dve.sem_inc(s, first[k])
            return sems

        def linear(name, x_hi, x_lo, units, evac_act=None, evac_dve=None, source=None, ahead=False,
                   loads=()):
            n, kc, nt = shapes[name]
            assert plan[ring.tile][0] is io["w_" + SHARED.get(name, (name, 0))[0]]
            words = kc * nt
            units_of = units if callable(units) else lambda t: units
            U = len(units_of(0))
            c0 = ring.unit
            with ExitStack() as scope:
                if ring.buffers is None:
                    w_hi = sb(scope, f"{name}_w_hi", [P, 2, words], F32R)
                    w_lo = sb(scope, f"{name}_w_lo", [P, 2, words], F32R)
                else:
                    w_hi, w_lo = ring.buffers
                begun = ring.begun
                ring.begun = ahead
                next_words = ring.plan[ring.tile + n][2] if ahead else 0

                def slot_of(t_parity):
                    return (ring.tile + t_parity) % 2
                acc = psum(scope, f"{name}_acc", [P, 2, 2, 512])
                made = source(scope) if source else None

                def results(j):
                    return [acc[:, (c0 + j * U + u) % 2] for u in range(U)]

                def counts(t):
                    return lambda u: t * U + (c0 + u + 1)

                with stage_block() as block:
                    @block.sync
                    def _(sp):
                        for dst, table, ready in loads:
                            sp.dma_start(dst, io[table]).then_inc(ready, 16)
                        issue_stage(sp, n)

                    @block.scalar
                    def _(act):
                        def round_hi(t, j, size=words):
                            slot = landed(act, t, j)
                            if not isinstance(t, int) or t >= 2:
                                act.wait_ge(unit_done, (t - 1) * U + c0)
                            nc.scalar.copy(w_hi[:, slot, 0:size], stage[:, slot, 0:size]).then_inc(hi_ready, 1)

                        if not begun:
                            round_hi(0, 0)
                        if made:
                            made["act"](act)

                        def body(t, j, last):
                            if not last:
                                round_hi(t + 1, 1 - j)
                            elif ahead:
                                round_hi(n, n % 2, next_words)
                            if evac_act:
                                evac_act(act, t, j, counts(t), results(j))

                        over_tiles(act, n, body)

                    @block.gpsimd
                    def _(pool):
                        def take_lo(t, j, size=words):
                            pool.wait_ge(hi_ready, t + (ring.split + 1))
                            if not isinstance(t, int) or t >= 2:
                                wait(pool, unit_done, (t - 1) * U + c0)
                            slot = slot_of(j)
                            nc.gpsimd.tensor_tensor(w_lo[:, slot, 0:size], stage[:, slot, 0:size],
                                                    w_hi[:, slot, 0:size].bitcast(F32), ALU.subtract)\
                                .then_inc(lo_ready, 1)

                        def body(t, j, last):
                            if not (begun and isinstance(t, int) and t == 0):
                                take_lo(t, j)

                        over_tiles(pool, n, body, peel=1 if begun else 0)
                        if ahead:
                            take_lo(n, n % 2, next_words)

                    @block.tensor
                    def _(pe):
                        if made and made["pe"]:
                            made["pe"](pe)

                        def body(t, j, last):
                            hi = w_hi[:, slot_of(j), 0:words].rearrange("p (k n) -> p k n", k=kc)
                            lo = w_lo[:, slot_of(j), 0:words].rearrange("p (k n) -> p k n", k=kc)
                            for u, unit in enumerate(units_of(t)):
                                out = acc[:, (c0 + j * U + u) % 2]
                                if not isinstance(t, int) or c0 + t * U + u >= 2:
                                    wait(pe, unit_free, t * U + (c0 + u - 1))
                                if u == 0:
                                    pe.wait_ge(hi_ready, t + (ring.split + 1))
                                for part in ("hi", "lo"):
                                    if part == "lo" and u == 0:
                                        pe.wait_ge(lo_ready, t + (ring.tile + 1))
                                    w = hi if part == "hi" else lo
                                    for k in range(kc):
                                        if made and made["ready"] and part == "hi" and u == 0 and isinstance(t, int) and t == 0:
                                            pe.wait_ge(made["ready"], made["first"] + k + 1)
                                        for xi, x in enumerate((x_hi, x_lo) if part == "hi" else (x_hi,)):
                                            begin = part == "hi" and k == 0 and xi == 0
                                            end = part == "lo" and k == kc - 1
                                            if unit[0] == "F":
                                                for b, (s, m) in enumerate(unit[2]):
                                                    mm = nc.tensor.matmul(out[0:min(P, nt), b, 0:m],
                                                                          w[:, k, unit[1]:unit[1] + min(P, nt)],
                                                                          x[:, k, s:s + m], start=begin, stop=end)
                                            else:
                                                mm = nc.tensor.matmul(out[:, 0, 0:unit[3]], x[:, k, unit[1]],
                                                                      w[:, k, unit[2]:unit[2] + unit[3]],
                                                                      start=begin, stop=end)
                                mm.then_inc(unit_done, 1)

                        over_tiles(pe, n, body, peel=1 if made else 0)

                    @block.vector
                    def _(dve):
                        if made:
                            made["dve"](dve)
                        if evac_dve:
                            over_tiles(dve, n, lambda t, j, last: evac_dve(dve, t, j, counts(t), results(j)))

            ring.tile += n
            ring.split += n
            ring.unit += n * U

        def share_weight_buffers(scope):
            def drop():
                ring.buffers = None

            shared_scopes[0] += 1
            ring.buffers = [sb(scope, f"shared{shared_scopes[0]}_w_{part}", [P, 2, SLOT], F32R) for part in ("hi", "lo")]
            scope.callback(drop)

        shared_scopes = [0]
        ALL = [(0, LAT), (LAT, CTX)]
        ONLY_LAT = [(0, LAT)]

        def feature_units(segs, nt=256):
            return [("F", c, segs) for c in range(0, nt, P)]

        norm_sem = {k: sem("norm_" + k) for k in ("squares", "summed", "root", "rstd", "scaled", "hi", "lo")}
        norms = [0]

        def norm_split(x_of, groups, hi, lo):
            n = norms[0]
            norms[0] += 1
            T = sum(g[1] for g in groups)
            S = norm_sem
            done = {k: norm_done.get(k, 0) for k in S}

            def source(scope):
                squares = sb(scope, f"norm{n}_squares", [P, 2, T])
                rstd = sb(scope, f"norm{n}_rstd", [P, T])
                scaled = squares
                total = psum(scope, f"norm{n}_total", [P, 2, 512])

                def of_act(act):
                    for c in range(DC):
                        if c >= 2:
                            act.wait_ge(S["summed"], done["summed"] + c - 1)
                        for s, m, _, _ in groups:
                            last = nc.scalar.activation(squares[:, c % 2, s:s + m], x_of(c, s, m), ACT.Square)
                        last.then_inc(S["squares"], 1)
                    act.wait_ge(S["summed"], done["summed"] + DC)
                    for b, (s, m, _, _) in enumerate(groups):
                        last = nc.scalar.activation(rstd[:, s:s + m], total[:, b, 0:m], ACT.Sqrt, bias=eps_col,
                                                    scale=1.0 / D)
                    last.then_inc(S["root"], 1)
                    for c in range(DC):
                        act.wait_ge(S["scaled"], done["scaled"] + c + 1)
                        for s, m, _, b in groups:
                            last = nc.scalar.activation(hi[:, c, s:s + m], scaled[:, c % 2, s:s + m],
                                                        ACT.Identity, bias=b(c))
                        last.then_inc(S["hi"], 1)

                def of_pe(pe):
                    for c in range(DC):
                        pe.wait_ge(S["squares"], done["squares"] + c + 1)
                        for b, (s, m, _, _) in enumerate(groups):
                            mm = nc.tensor.matmul(total[:, b, 0:m], ones[:], squares[:, c % 2, s:s + m],
                                                  start=c == 0, stop=c == DC - 1)
                        mm.then_inc(S["summed"], 1)

                def of_dve(dve):
                    dve.wait_ge(S["root"], done["root"] + 1)
                    nc.vector.reciprocal(rstd[:], rstd[:]).then_inc(S["rstd"], 1)
                    dve.wait_ge(S["rstd"], done["rstd"] + 1)

                    def low(c):
                        dve.wait_ge(S["hi"], done["hi"] + c + 1)
                        for s, m, _, b in groups:
                            last = nc.vector.scalar_tensor_tensor(
                                lo[:, c, s:s + m], scaled[:, c % 2, s:s + m], b(c),
                                hi[:, c, s:s + m].bitcast(F32), ALU.add, ALU.subtract)
                        last.then_inc(S["lo"], 1)

                    for c in range(DC):
                        if c >= 2:
                            dve.wait_ge(S["lo"], done["lo"] + c - 1)
                        for s, m, a, _ in groups:
                            last = nc.vector.scalar_tensor_tensor(
                                scaled[:, c % 2, s:s + m], x_of(c, s, m), a(c), rstd[:, s:s + m],
                                ALU.mult, ALU.mult)
                        last.then_inc(S["scaled"], 1)
                        if c >= 1:
                            low(c - 1)
                    low(DC - 1)

                return dict(act=of_act, pe=of_pe, dve=of_dve, ready=S["lo"], first=done["lo"])

            for k, m in (("squares", DC), ("summed", DC), ("root", 1), ("rstd", 1), ("scaled", DC), ("hi", DC),
                         ("lo", DC)):
                norm_done[k] = done[k] + m
            return source

        norm_done = {}

        cut_sem = {"hi": sem("cut_hi"), "lo": sem("cut_lo")}
        cut_done = [0]

        def cut(src, hi, lo, chunks):
            base = cut_done[0]
            cut_done[0] += chunks

            def source(scope):
                def of_act(act):
                    with act.Fori(0, chunks) as c:
                        nc.scalar.copy(hi[:, bass.ds(c, 1), :], src[:, bass.ds(c, 1), :]).then_inc(cut_sem["hi"], 1)

                def of_dve(dve):
                    with dve.Fori(0, chunks) as c:
                        dve.wait_ge(cut_sem["hi"], c + (base + 1))
                        nc.vector.tensor_tensor(lo[:, bass.ds(c, 1), :], src[:, bass.ds(c, 1), :],
                                                hi[:, bass.ds(c, 1), :].bitcast(F32), ALU.subtract)\
                            .then_inc(cut_sem["lo"], 1)

                return dict(act=of_act, pe=None, dve=of_dve, ready=cut_sem["lo"], first=base)

            return source

        ffn_sem = {k: sem("ffn_" + k) for k in ("hi", "lo")}
        ffn_done = [1]

        def feed_forward(layer, x_hi, x_lo, segs, residual, source):
            T = sum(m for _, m in segs)
            weights = ExitStack()
            share_weight_buffers(weights)
            for half in (0, 1):
                base = ffn_done[0]
                ffn_done[0] += HALF
                with ExitStack() as scope:
                    h_hi = sb(scope, f"ffn{layer}{half}_hi", [P, HALF, T], F32R)
                    h_lo = sb(scope, f"ffn{layer}{half}_lo", [P, HALF, T], F32R)
                    with ExitStack() as inner:
                        gate = sb(inner, f"ffn{layer}{half}_gate", [P, T])
                        hidden = sb(inner, f"ffn{layer}{half}_hidden", [P, T])

                        def evac_act(act, t, j, count, res):
                            act.wait_ge(unit_done, count(0))
                            for b, (s, m) in enumerate(segs):
                                last = nc.scalar.activation(gate[:, s:s + m], res[0][:, b, 0:m], ACT.Silu)
                            last.then_inc(unit_free, 1)
                            act.wait_ge(unit_free, count(1))
                            nc.scalar.copy(h_hi[:, bass.ds(t, 1), :], hidden[:].rearrange("p (o n) -> p o n", o=1))\
                                .then_inc(ffn_sem["hi"], 1)

                        def evac_dve(dve, t, j, count, res):
                            dve.wait_ge(unit_done, count(1))
                            dve.wait_ge(unit_free, count(0))
                            wait(dve, ffn_sem["lo"], t + base)
                            for b, (s, m) in enumerate(segs):
                                last = nc.vector.tensor_tensor(hidden[:, s:s + m], res[1][:, b, 0:m],
                                                               gate[:, s:s + m], ALU.mult)
                            last.then_inc(unit_free, 1)
                            dve.wait_ge(ffn_sem["hi"], t + (base + 1))
                            nc.vector.tensor_tensor(h_lo[:, bass.ds(t, 1), :],
                                                    hidden[:].rearrange("p (o n) -> p o n", o=1),
                                                    h_hi[:, bass.ds(t, 1), :].bitcast(F32), ALU.subtract)\
                                .then_inc(ffn_sem["lo"], 1)

                        linear(f"f{layer}i{half}", x_hi, x_lo, feature_units(segs), evac_act, evac_dve,
                               source if half == 0 else None, ahead=True)
                    linear(f"f{layer}o{half}", h_hi, h_lo, [("F", 0, segs)], None, residual, ahead=half == 0)
            weights.close()

        def add_residual(segs, gates, per_tile):
            def evac(dve, t, j, count, res):
                for u in range(per_tile):
                    dve.wait_ge(unit_done, count(u))
                    for b, (s, m) in enumerate(segs):
                        c = t * per_tile + u
                        x = x_lat[:, bass.ds(c, 1), :] if s == 0 else x_ctx[0][:, bass.ds(c, 1), :]
                        x = x.rearrange("p o n -> p (o n)")
                        last = nc.vector.scalar_tensor_tensor(
                            x, res[u][:, b, 0:m], gates[b][:, bass.ds(c, 1)], x, ALU.mult, ALU.add)
                    last.then_inc(unit_free, 1)
            return evac

        x_ctx = [None]

        rope_loaded, rope_turned = sem("ret_rope_loaded"), sem("ret_rope_turned")
        conv_sem, silu_sem = sem("conv_tap"), sem("conv_silu")
        with stage_block() as block:
            @block.sync
            def _(sp):
                sp.dma_start(small[:], io["small"]).then_inc(small_loaded, 16)
                sp.dma_start(ident[:], io["ident"]).then_inc(loaded, 16)

            @block.vector
            def _(dve):
                for s in (unit_done, unit_free):
                    dve.sem_inc(s, ring.unit)
                for s in ffn_sem.values():
                    dve.sem_inc(s, ffn_done[0])
                dve.sem_inc(rope_turned, 1)
                dve.sem_inc(silu_sem, 2)

        QUAD = 4
        quads, quads_main = 60 // QUAD, 48 // QUAD
        SLOTS = 3
        quad_landed = [sem(f"mod_weights_landed_{s}") for s in range(SLOTS)]
        first_landed = sem("mod_first_pair_landed")
        cond_ready, modded = sem("cond_ready"), sem("modulation_ready")
        pair_hi, pair_lo, pair_summed = sem("mod_weights_hi"), sem("mod_weights_lo"), sem("mod_pair_summed")
        rows_copied, cols_turned = sem("mod_rows_copied"), sem("mod_columns_turned")
        with ExitStack() as scope:
            cond = sb(scope, "cond_silu", [P, 24])
            cond_hi = sb(scope, "cond_hi", [P, 24], F32R)
            cond_lo = sb(scope, "cond_lo", [P, 24], F32R)
            mod_w = sb(scope, "mod_weights", [P, SLOTS, QUAD, 2048])
            mod_hi = sb(scope, "mod_weights_hi", [P, 2, 2, 2048], F32R)
            mod_lo = sb(scope, "mod_weights_lo", [P, 2, 2, 2048], F32R)
            rows = sb(scope, "mod_rows", [2, 2, QUAD * 256])
            p_rows = psum(scope, "mod_p_rows", [P, 2, 2, 512])
            mod_sum = psum(scope, "mod_sum", [P, 512])
            with stage_block() as block:
                @block.sync
                def _(sp):
                    for q in range(quads):
                        if q >= SLOTS:
                            sp.wait_ge(pair_lo, 2 * (q - SLOTS) + 2)
                        head = 2 if q == 0 else 0
                        if head:
                            sp.dma_start(mod_w[:, 0, 0:2, :], io["w_mod"][0:2].rearrange("o p n -> p o n"))\
                                .then_inc(first_landed, 16)
                        sp.dma_start(mod_w[:, q % SLOTS, head:, :],
                                     io["w_mod"][q * QUAD + head:(q + 1) * QUAD].rearrange("o p n -> p o n"))\
                            .then_inc(quad_landed[q % SLOTS], 16)
                        if q == SLOTS - 1:
                            for dst, src in ((ones, "ones"), (x_lat, "x")):
                                sp.dma_start(dst[:], io[src]).then_inc(loaded, 16)
                            issue_next(sp, 2)

                @block.scalar
                def _(act):
                    act.wait_ge(small_loaded, 16)
                    a, b = SMALL["cond"][0], SMALL["cond_2"][1]
                    nc.scalar.activation(cond[:], small[:, a:b], ACT.Silu).then_inc(cond_ready, 1)
                    act.wait_ge(cond_ready, 1)
                    nc.scalar.copy(cond_hi[:], cond[:]).then_inc(cond_ready, 1)

                    def round_hi(pair):
                        q, b = divmod(pair, 2)
                        if pair == 0:
                            act.wait_ge(first_landed, 16)
                        else:
                            act.wait_ge(quad_landed[q % SLOTS], 16 * (q // SLOTS + 1))
                        if pair >= 2:
                            act.wait_ge(pair_summed, pair - 1)
                        nc.scalar.copy(mod_hi[:, b, :, :], mod_w[:, q % SLOTS, 2 * b:2 * b + 2, :]).then_inc(pair_hi, 1)

                    def copy_rows(q):
                        m = 2 if q < quads_main else 1
                        act.wait_ge(pair_summed, 2 * q + 2)
                        if q >= 2:
                            act.wait_ge(cols_turned, q - 1)
                        nc.scalar.copy(rows[0:m, q % 2, :].rearrange("p (b n) -> p b n", n=512),
                                       p_rows[0:m, q % 2, :, :]).then_inc(rows_copied, 1)

                    for q in range(quads):
                        round_hi(2 * q)
                        round_hi(2 * q + 1)
                        if q >= 1:
                            copy_rows(q - 1)
                    copy_rows(quads - 1)

                @block.tensor
                def _(pe):
                    pe.wait_ge(cond_ready, 3)

                    def sum_quad(q):
                        if q >= 2:
                            pe.wait_ge(rows_copied, q - 1)
                        m = 2 if q < quads_main else 1
                        for b in range(2):
                            pe.wait_ge(pair_hi, 2 * q + b + 1)
                            for part, (c, w) in enumerate(((cond_hi, mod_hi), (cond_lo, mod_hi), (cond_hi, mod_lo))):
                                if part == 2:
                                    pe.wait_ge(pair_lo, 2 * q + b + 1)
                                for k in range(DC):
                                    who = c[:, k:16:8] if q < quads_main else c[:, 16 + k:17 + k]
                                    mm = nc.tensor.matmul(p_rows[0:m, q % 2, b, :], who,
                                                          w[:, b, :, k * 256:(k + 1) * 256],
                                                          start=part == 0 and k == 0, stop=part == 2 and k == DC - 1)
                            mm.then_inc(pair_summed, 1)

                    def turn_quad(q):
                        m = 2 if q < quads_main else 1
                        at = 16 * q if q < quads_main else 16 * quads_main + 8 * (q - quads_main)
                        if q == 0:
                            pe.wait_ge(loaded, 48)
                        pe.wait_ge(rows_copied, q + 1)
                        for c in range(8):
                            mm = nc.tensor.transpose(mod_sum[:, at + c * m:at + (c + 1) * m],
                                                     rows[0:m, q % 2, c * P:(c + 1) * P], ident[0:m, 0:m])
                        mm.then_inc(cols_turned, 1)

                    for q in range(quads):
                        sum_quad(q)
                        if q >= 1:
                            turn_quad(q - 1)
                    turn_quad(quads - 1)

                @block.vector
                def _(dve):
                    dve.wait_ge(cond_ready, 2)
                    nc.vector.tensor_tensor(cond_lo[:], cond[:], cond_hi[:].bitcast(F32), ALU.subtract)\
                        .then_inc(cond_ready, 1)
                    for pair in range(2 * quads):
                        q, b = divmod(pair, 2)
                        dve.wait_ge(pair_hi, pair + 1)
                        if pair >= 2:
                            dve.wait_ge(pair_summed, pair - 1)
                        nc.vector.tensor_tensor(mod_lo[:, b, :, :], mod_w[:, q % SLOTS, 2 * b:2 * b + 2, :],
                                                mod_hi[:, b, :, :].bitcast(F32), ALU.subtract).then_inc(pair_lo, 1)
                    dve.wait_ge(loaded, 48)
                    dve.wait_ge(cols_turned, quads)
                    a, b = SMALL["mod_b"]
                    bias = small[:, a:b].rearrange("p (m o) -> p m o", o=1).broadcast_to([P, 96, 2])
                    nc.vector.tensor_tensor(mods[:].rearrange("p l m v -> p (l m) v"),
                                            mod_sum[:, 0:192].rearrange("p (m v) -> p m v", v=2), bias, ALU.add)
                    nc.vector.tensor_tensor(ada[:], mod_sum[:, 192:216], cols("ada_b"), ALU.add).then_inc(modded, 1)
                    dve.wait_ge(modded, 1)
                    gain = cols("norm_g").rearrange("p (l w c) -> p l w c", l=2, w=2)
                    for layer in range(2):
                        for which in range(2):
                            for v in range(2):
                                m = 24 * which + 8
                                nc.vector.scalar_tensor_tensor(
                                    scale_of[:, layer, which, v, :], mods[:, layer, m:m + 8, v], 1.0,
                                    gain[:, layer, which, :], ALU.add, ALU.mult)
                    nc.vector.scalar_tensor_tensor(scale_2[:], ada[:, 8:16], 1.0, cols("norm_w"), ALU.add, ALU.mult)

        def group(layer, which, v, first, tokens):
            return (first, tokens, lambda c: scale_of[:, layer, which, v, c:c + 1],
                    lambda c: mods[:, layer, 24 * which + c, v:v + 1])

        def gates_of(layer, which, v):
            m = 24 * which + 16
            return mods[:, layer, m:m + 8, v]

        def copy_units(buf, first, per_tile=2, func=ACT.Identity):
            def evac(act, t, j, count, res):
                for u in range(per_tile):
                    act.wait_ge(unit_done, count(u))
                    width = buf.shape[2]
                    for b, s in enumerate(range(0, width, 512)):
                        m = min(512, width - s)
                        last = nc.scalar.activation(
                            buf[:, bass.ds(t * per_tile + (first + u), 1), s:s + m],
                            res[u][:, b:b + 1, 0:m], func)
                    last.then_inc(unit_free, 1)
            return evac

        mix = ExitStack()

        ctx_scope = ExitStack()
        x_ctx[0] = sb(ctx_scope, "x_ctx", [P, DC, CTX])
        ctx_loaded = sem("context_loaded")
        with stage_block() as block:
            @block.sync
            def _(sp):
                sp.dma_start(x_ctx[0][:], io["ctx"]).then_inc(ctx_loaded, 16)
                sp.wait_ge(ctx_loaded, 16)

        def x_all(c, s, m):
            return x_lat[:, c, s:s + m] if s < LAT else x_ctx[0][:, c, s - LAT:s - LAT + m]

        attend_jobs = ("scores", "scores_read", "maximum", "exp", "turned", "turned_read", "mixed")
        attend_sem = {}
        for k in attend_jobs + ("queries", "reciprocal", "normed", "out", "out_read", "log", "lse"):
            attend_sem[k] = sem("attend_" + k)

        def attend(tag, blocks, heads, q_copies, out_copies, width, kb_max, cols_out, scale, lse=None):
            H = len(heads)
            S = counted_from(attend_sem, {k: H if k in attend_jobs else 1 for k in attend_sem})
            chunks = cols_out // P
            with ExitStack() as scope:
                has_sink = heads[0]["sink"] is not None
                row = sb(scope, f"{tag}_row", [P, 3, width + has_sink])
                minus_max = sb(scope, f"{tag}_minus_max", [P, H])
                total = sb(scope, f"{tag}_total", [P, H])
                inverse = sb(scope, f"{tag}_inverse", [P, H])
                log_total = sb(scope, f"{tag}_log_total", [P, H])
                probs = sb(scope, f"{tag}_probs", [P, 2, kb_max * P])
                mixed = sb(scope, f"{tag}_mixed", [P, cols_out])
                sbanks = (width + 511) // 512
                p_scores = psum(scope, f"{tag}_p_scores", [P, 2, sbanks, 512])
                p_turned = psum(scope, f"{tag}_p_turned", [P, (kb_max + 3) // 4 * 512])
                p_mixed = psum(scope, f"{tag}_p_mixed", [P, (cols_out + 511) // 512 * 512])
                p_out = psum(scope, f"{tag}_p_out", [P, (cols_out + 511) // 512 * 512])

                def slot_of(h):
                    n = heads[h]["column"] // 64
                    return slice(n, n + 1)

                def before(i, h, lag):
                    return i * H + (H + max(h + 1 - lag, 0))

                def key_blocks(i, h):
                    return sum(k[1] for k in heads[h]["keys"](i)) // P

                with stage_block() as block:
                    @block.tensor
                    def _(pe):
                        def scores(i, h):
                            if h == 0:
                                pe.wait_ge(S["queries"], i + 2)
                            pe.wait_ge(S["scores_read"], before(i, h, 2))
                            for b, (_, m, rhs, _) in enumerate(heads[h]["keys"](i)):
                                mm = nc.tensor.matmul(p_scores[:, h % 2, b, 0:m], heads[h]["q"], rhs,
                                                      start=True, stop=True)
                            mm.then_inc(S["scores"], 1)

                        def turn(i, h):
                            pe.wait_ge(S["exp"], i * H + (H + h + 1))
                            pe.wait_ge(S["turned_read"], i * H + (H + h))
                            for b in range(key_blocks(i, h)):
                                mm = nc.tensor.transpose(p_turned[:, b * P:(b + 1) * P],
                                                         row[:, h % 3, b * P:(b + 1) * P], ident[:])
                            mm.then_inc(S["turned"], 1)

                        def mix_values(i, h):
                            pe.wait_ge(S["turned_read"], i * H + (H + h + 1))
                            if h == 0:
                                pe.wait_ge(S["normed"], i + 1)
                            c = heads[h]["column"]
                            n = key_blocks(i, h)
                            for b, v in enumerate(heads[h]["values"](i)):
                                mm = nc.tensor.matmul(p_mixed[:, c:c + 64], probs[:, h % 2, b * P:(b + 1) * P], v,
                                                      start=b == 0, stop=b == n - 1)
                            mm.then_inc(S["mixed"], 1)

                        def turn_back(i):
                            pe.wait_ge(S["normed"], i + 1)
                            pe.wait_ge(S["out_read"], i)
                            for c in range(chunks):
                                mm = nc.tensor.transpose(p_out[:, c * P:(c + 1) * P], mixed[:, c * P:(c + 1) * P],
                                                         ident[:])
                            mm.then_inc(S["out"], 1)

                        def block_of_queries(i, first):
                            scores(i, 0)
                            scores(i, 1)
                            if not first:
                                turn_back(i)
                            for h in range(H):
                                if h + 2 < H:
                                    scores(i, h + 2)
                                turn(i, h)
                                if h >= 1:
                                    mix_values(i, h - 1)
                            mix_values(i, H - 1)

                        block_of_queries(0, True)
                        with pe.Fori(1, blocks) as i:
                            block_of_queries(i, False)
                        turn_back(blocks)

                    @block.vector
                    def _(dve):
                        def read_scores(i, h):
                            head = heads[h]
                            if lse is not None and h == 0:
                                dve.wait_ge(S["lse"], i + 1)
                            dve.wait_ge(S["scores"], i * H + (H + h + 1))
                            dve.wait_ge(S["turned"], before(i, h, 3))
                            if head["sink"] is not None:
                                n = key_blocks(i, h) * P
                                nc.vector.tensor_copy(row[:, h % 3, n:n + 1], head["sink"])
                            for b, (s, m, _, mask) in enumerate(head["keys"](i)):
                                if mask is None:
                                    last = nc.vector.tensor_scalar(row[:, h % 3, s:s + m], p_scores[:, h % 2, b, 0:m],
                                                                   scale, None, ALU.mult)
                                else:
                                    last = nc.vector.scalar_tensor_tensor(
                                        row[:, h % 3, s:s + m], p_scores[:, h % 2, b, 0:m], scale, mask,
                                        ALU.mult, ALU.add)
                            last.then_inc(S["scores_read"], 1)
                            dve.wait_ge(S["scores_read"], i * H + (H + h + 1))
                            n = key_blocks(i, h) * P + has_sink
                            nc.vector.tensor_reduce(minus_max[:, slot_of(h)], row[:, h % 3, 0:n], AX_X, ALU.max,
                                                    negate=True).then_inc(S["maximum"], 1)

                        with dve.Fori(0, blocks) as i:
                            for h in range(H):
                                read_scores(i, h)
                            dve.wait_ge(S["mixed"], i * H + 2 * H)
                            nc.vector.reciprocal(inverse[:], total[:]).then_inc(S["reciprocal"], 1)
                            dve.wait_ge(S["reciprocal"], i + 2)
                            dve.wait_ge(S["out"], i + 1)
                            nc.vector.tensor_tensor(
                                mixed[:].rearrange("p (h n) -> p h n", n=64),
                                p_mixed[:, 0:cols_out].rearrange("p (h n) -> p h n", n=64),
                                inverse[:].rearrange("p (h o) -> p h o", o=1).broadcast_to([P, H, 64]), ALU.mult)\
                                .then_inc(S["normed"], 1)
                            if lse is not None:
                                dve.wait_ge(S["log"], i + 2)
                                nc.vector.tensor_tensor(lse[:, bass.ds(i, 1), :].rearrange("p o h -> p (o h)"),
                                                        log_total[:], minus_max[:], ALU.subtract)\
                                    .then_inc(S["lse"], 1)

                    @block.scalar
                    def _(act):
                        def exponent(i, h):
                            act.wait_ge(S["maximum"], i * H + (H + h + 1))
                            n = key_blocks(i, h) * P + has_sink
                            nc.scalar.activation(row[:, h % 3, 0:n], row[:, h % 3, 0:n], ACT.Exp,
                                                 bias=minus_max[:, slot_of(h)], accum_out=total[:, slot_of(h)])\
                                .then_inc(S["exp"], 1)

                        def copy_turned(i, h):
                            act.wait_ge(S["turned"], i * H + (H + h + 1))
                            act.wait_ge(S["mixed"], before(i, h, 2))
                            n = key_blocks(i, h) * P
                            nc.scalar.copy(probs[:, h % 2, 0:n], p_turned[:, 0:n]).then_inc(S["turned_read"], 1)

                        def copy_out(i):
                            act.wait_ge(S["out"], i + 1)
                            for dst, src in out_copies(i - 1, p_out):
                                last = nc.scalar.copy(dst, src)
                            last.then_inc(S["out_read"], 1)

                        def block_of_queries(i, first):
                            act.wait_ge(S["scores"], i * H + H)
                            for dst, src in q_copies(i):
                                last = nc.scalar.copy(dst, src)
                            last.then_inc(S["queries"], 1)
                            exponent(i, 0)
                            for h in range(H):
                                if h + 1 < H:
                                    exponent(i, h + 1)
                                copy_turned(i, h)
                                if h == 0 and not first:
                                    copy_out(i)
                            if lse is not None:
                                act.wait_ge(S["exp"], i * H + 2 * H)
                                act.wait_ge(S["lse"], i + 1)
                                nc.scalar.activation(log_total[:], total[:], ACT.Ln).then_inc(S["log"], 1)

                        block_of_queries(0, True)
                        with act.Fori(1, blocks) as i:
                            block_of_queries(i, False)
                        copy_out(blocks)

        mixed_0 = sb(mix, "mixed_0", [P, DC, TOK])
        normed_scope = ExitStack()
        n_hi = sb(normed_scope, "norm_a_hi", [P, DC, TOK], F32R)
        n_lo = sb(normed_scope, "norm_a_lo", [P, DC, TOK], F32R)
        norm_a = norm_split(x_all, [group(0, 0, 0, 0, LAT), group(0, 0, 1, LAT, CTX)], n_hi, n_lo)

        attn = ExitStack()
        qk = sb(attn, "qk", [P, 5, TOK])
        k_pad = sb(attn, "k_pad", [P, P + LAT + P + CTX])
        v_pad = sb(attn, "v_pad", [P, 8, P])
        pad_ready = sem("pads_zeroed")

        hn = {k: sem("headnorm_" + k) for k in ("tables", "squares", "summed", "root", "rstd", "normed", "rotated",
                                               "cosine", "sine", "done", "context")}
        window_ready = sem("window_loaded")
        axial = sb(attn, "axial", [P, 2, LAT])
        rotT = sb(attn, "rotT", [P, P])
        ones64 = sb(attn, "ones64", [P, P])
        window = sb(attn, "window", [P, 4, 3 * P])
        linear("aq", n_hi, n_lo, feature_units(ALL), copy_units(qk, 0), source=norm_a)

        def evac_akv(act, t, j, count, res):
            act.wait_ge(unit_done, count(0))
            nc.scalar.copy(qk[:, 4, 0:LAT], res[0][:, 0, :])
            nc.scalar.copy(qk[:, 4, LAT:TOK], res[0][:, 1, 0:CTX]).then_inc(unit_free, 1)
            for b in range(6):
                act.wait_ge(unit_done, count(1 + b))
                nc.scalar.copy(v_pad[:, b + 1 if b < 4 else b + 2, :], res[1 + b][:, 0, 0:P]).then_inc(unit_free, 1)

        linear("akv", n_hi, n_lo, [("F", 0, ALL)] + [("T", slice(b * P, (b + 1) * P), P, P) for b in range(6)],
               evac_akv, loads=[(axial[:], "axial", hn["tables"]), (rotT[:], "rotT", hn["tables"]),
                                (ones64[:], "ones64", hn["tables"]), (window[:], "window", window_ready)])

        with ExitStack() as scope:
            squares = sb(scope, "head_squares", [P, 2, TOK])
            rstd = sb(scope, "head_rstd", [P, 2, TOK])
            unit = sb(scope, "head_unit", [P, 2, TOK])
            turn_c = sb(scope, "head_cosine", [P, 2, LAT])
            turn_s = sb(scope, "head_sine", [P, 2, LAT])
            p_sum = psum(scope, "head_sum", [P, 2, 2, 512])
            p_rot = psum(scope, "head_rot", [P, 2, 512])
            with stage_block() as block:
                @block.gpsimd
                def _(pool):
                    for pad in (k_pad[:, 0:P], k_pad[:, P + LAT:2 * P + LAT], v_pad[:, 0, :], v_pad[:, 5, :]):
                        nc.gpsimd.memset(pad, 0.0).then_inc(pad_ready, 1)
                    pool.wait_ge(hn["tables"], 48)
                    for c in range(5):
                        pool.wait_ge(hn["normed"], c + 1)
                        nc.gpsimd.tensor_tensor(turn_c[:, c % 2, :], unit[:, c % 2, 0:LAT], axial[:, 0, :], ALU.mult)\
                            .then_inc(hn["cosine"], 1)
                        pool.wait_ge(hn["cosine"], c + 1)
                        pool.wait_ge(hn["sine"], c + 1)
                        lat = qk[:, c, 0:LAT] if c < 4 else k_pad[:, P:P + LAT]
                        nc.gpsimd.tensor_tensor(lat, turn_c[:, c % 2, :], turn_s[:, c % 2, :], ALU.add)\
                            .then_inc(hn["done"], 1)
                    pool.wait_ge(pad_ready, 4)
                    pool.wait_ge(hn["done"], 5)

                @block.scalar
                def _(act):
                    def copy_context(c):
                        act.wait_ge(hn["normed"], c + 1)
                        ctx = qk[:, c, LAT:TOK] if c < 4 else k_pad[:, 2 * P + LAT:2 * P + TOK]
                        nc.scalar.copy(ctx, unit[:, c % 2, LAT:TOK]).then_inc(hn["context"], 1)

                    for c in range(5):
                        if c >= 2:
                            act.wait_ge(hn["summed"], c - 1)
                        nc.scalar.activation(squares[:, c % 2, :], qk[:, c, :], ACT.Square).then_inc(hn["squares"], 1)
                        act.wait_ge(hn["summed"], c + 1)
                        if c >= 2:
                            act.wait_ge(hn["normed"], c - 1)
                        nc.scalar.activation(rstd[:, c % 2, 0:LAT], p_sum[:, c % 2, 0, :], ACT.Sqrt, bias=eps_col,
                                             scale=1.0 / 64)
                        nc.scalar.activation(rstd[:, c % 2, LAT:TOK], p_sum[:, c % 2, 1, 0:CTX], ACT.Sqrt, bias=eps_col,
                                             scale=1.0 / 64).then_inc(hn["root"], 1)
                        if c >= 1:
                            copy_context(c - 1)
                    copy_context(4)

                @block.tensor
                def _(pe):
                    pe.wait_ge(hn["tables"], 48)

                    def rotate(c):
                        pe.wait_ge(hn["normed"], c + 1)
                        if c >= 2:
                            pe.wait_ge(hn["sine"], c - 1)
                        nc.tensor.matmul(p_rot[:, c % 2, :], rotT[:], unit[:, c % 2, 0:LAT], start=True, stop=True)\
                            .then_inc(hn["rotated"], 1)

                    for c in range(5):
                        pe.wait_ge(hn["squares"], c + 1)
                        if c >= 2:
                            pe.wait_ge(hn["root"], c - 1)
                        nc.tensor.matmul(p_sum[:, c % 2, 0, :], ones64[:], squares[:, c % 2, 0:LAT], start=True, stop=True)
                        nc.tensor.matmul(p_sum[:, c % 2, 1, 0:CTX], ones64[:], squares[:, c % 2, LAT:TOK],
                                         start=True, stop=True).then_inc(hn["summed"], 1)
                        if c >= 1:
                            rotate(c - 1)
                    rotate(4)

                @block.vector
                def _(dve):
                    dve.wait_ge(hn["tables"], 48)

                    def normed(c):
                        g = cols("qk_g")[:, 0:1] if c < 4 else cols("qk_g")[:, 1:2]
                        dve.wait_ge(hn["root"], c + 1)
                        nc.vector.reciprocal(rstd[:, c % 2, :], rstd[:, c % 2, :]).then_inc(hn["rstd"], 1)
                        dve.wait_ge(hn["rstd"], c + 1)
                        if c >= 2:
                            dve.wait_ge(hn["rotated"], c - 1)
                            dve.wait_ge(hn["cosine"], c - 1)
                            dve.wait_ge(hn["context"], c - 1)
                        nc.vector.scalar_tensor_tensor(unit[:, c % 2, :], qk[:, c, :], g, rstd[:, c % 2, :],
                                                       ALU.mult, ALU.mult).then_inc(hn["normed"], 1)

                    def sine(c):
                        dve.wait_ge(hn["rotated"], c + 1)
                        if c >= 2:
                            dve.wait_ge(hn["done"], c - 1)
                        nc.vector.tensor_tensor(turn_s[:, c % 2, :], p_rot[:, c % 2, :], axial[:, 1, :], ALU.mult)\
                            .then_inc(hn["sine"], 1)

                    for c in range(5):
                        normed(c)
                        if c >= 1:
                            sine(c - 1)
                    sine(4)

        with ExitStack() as scope:
            q_zero = sb(scope, "q_zero", [P, 8, P])
            zeroed = sem("queries_zeroed")
            with stage_block() as block:
                @block.sync
                def _(sp):
                    sp.wait_ge(window_ready, 16)

                @block.vector
                def _(dve):
                    nc.vector.memset(q_zero[:], 0.0).then_inc(zeroed, 1)

            k_ctx = k_pad[:, 2 * P + LAT:2 * P + TOK]

            def head_of(h, with_lat):
                g = h // 4
                half = slice(64 * g, 64 * g + 64)

                def keys(i):
                    ctx = (3 * P if with_lat else 0, CTX, k_ctx, None)
                    if not with_lat:
                        return [ctx]
                    mask = window[:, bass.ds(i, 1), :].rearrange("p o n -> p (o n)")
                    return [(0, 3 * P, k_pad[:, bass.ds(i * P, 3 * P)], mask), ctx]

                def values(i):
                    lat = [v_pad[:, bass.ds(i + b, 1), half].rearrange("p o n -> p (o n)") for b in range(3)]
                    return lat * with_lat + [v_pad[:, 6, half], v_pad[:, 7, half]]

                return dict(q=q_zero[:, h, :], keys=keys, values=values, column=(h % 4) * P + 64 * g,
                            sink=cols("sink")[:, h:h + 1])

            def q_copies_from(first):
                def copies(i):
                    return [(q_zero[64 * g:64 * g + 64, 4 * g:4 * g + 4, :],
                             qk[64 * g:64 * g + 64, 0:4, bass.ds(i * P + first, P)]) for g in range(2)]
                return copies

            def out_copies_to(first):
                def copies(i, p_out):
                    return [(mixed_0[:, 0:4, bass.ds(i * P + first, P)],
                             p_out[:, 0:512].rearrange("p (c n) -> p c n", c=4))]
                return copies

            attend("win", LAT // P, [head_of(h, True) for h in range(8)], q_copies_from(0), out_copies_to(0),
                   3 * P + CTX, 5, 512, 64.0 ** -0.5)
            attend("ctxa", CTX // P, [head_of(h, False) for h in range(8)], q_copies_from(LAT), out_copies_to(LAT),
                   CTX, 2, 512, 64.0 ** -0.5)
        attn.close()

        head_norm_sem = {k: sem("head_norm_" + k) for k in ("squares", "summed", "root", "rstd", "scaled", "gated")}

        def head_norm(tag, heads, per, width, out, gain=None, gate=None, within=False, each=None):
            S = counted_from(head_norm_sem, {})
            segs = [(s, min(512, width - s)) for s in range(0, width, 512)]
            def source(scope):
                squares = sb(scope, f"{tag}_squares", [P, 2, width])
                rstd = sb(scope, f"{tag}_rstd", [P, 2, width])
                total = psum(scope, f"{tag}_sums", [P, 2, len(segs), 512])
                def of_act(act):
                    def root(h):
                        act.wait_ge(S["summed"], (h + 1) * per)
                        if h >= 2:
                            act.wait_ge(S["scaled"], h - 1)
                        for b, (s, m) in enumerate(segs):
                            last = nc.scalar.activation(rstd[:, h % 2, s:s + m], total[:, h % 2, b, 0:m], ACT.Sqrt,
                                                        bias=eps_col, scale=1.0 / (per * P))
                        last.then_inc(S["root"], 1)

                    for h in range(heads):
                        for j in range(per):
                            n = h * per + j
                            if n >= 2:
                                act.wait_ge(S["summed"], n - 1)
                            nc.scalar.activation(squares[:, n % 2, :], out(h, j), ACT.Square)\
                                .then_inc(S["squares"], 1)
                        if h >= 1:
                            root(h - 1)
                    root(heads - 1)

                def of_pe(pe):
                    for h in range(heads):
                        if h >= 2:
                            pe.wait_ge(S["root"], h - 1)
                        for j in range(per):
                            n = h * per + j
                            pe.wait_ge(S["squares"], n + 1)
                            for b, (s, m) in enumerate(segs):
                                mm = nc.tensor.matmul(total[:, h % 2, b, 0:m], ones[:], squares[:, n % 2, s:s + m],
                                                      start=j == 0, stop=j == per - 1)
                            mm.then_inc(S["summed"], 1)

                def of_dve(dve):
                    for h in range(heads):
                        dve.wait_ge(S["root"], h + 1)
                        nc.vector.reciprocal(rstd[:, h % 2, :], rstd[:, h % 2, :]).then_inc(S["rstd"], 1)
                        dve.wait_ge(S["rstd"], h + 1)
                        for j in range(per):
                            g = gain(j) if callable(gain) else gain
                            if g is None:
                                last = nc.vector.tensor_tensor(out(h, j), out(h, j), rstd[:, h % 2, :], ALU.mult)
                            else:
                                last = nc.vector.scalar_tensor_tensor(out(h, j), out(h, j), g, rstd[:, h % 2, :],
                                                                      ALU.mult, ALU.mult)
                            if each is not None and j < per - 1:
                                last.then_inc(each, 1)
                        last.then_inc(S["scaled"], 1)
                        if gate is not None:
                            dve.wait_ge(S["scaled"], h + 1)
                            for j in range(per):
                                last = nc.vector.tensor_tensor(out(h, j), out(h, j), gate(h, j), ALU.mult)
                            last.then_inc(S["gated"], 1)
                    dve.wait_ge(S["scaled" if gate is None else "gated"], heads)

                return dict(act=of_act, pe=of_pe, dve=of_dve, ready=None)

            if within:
                return source
            with ExitStack() as scope:
                made = source(scope)
                with stage_block() as block:
                    @block.scalar
                    def _(act):
                        made["act"](act)

                    @block.tensor
                    def _(pe):
                        made["pe"](pe)

                    @block.vector
                    def _(dve):
                        made["dve"](dve)

        gla = ExitStack()
        q_silu = sb(gla, "hgrn_q", [P, GLA_H, TOK])
        keep = sb(gla, "hgrn_forget", [P, 2 * GLA_H, TOK])
        i_tok = sb(gla, "hgrn_i", [P, TOK // P, 512])
        g_silu = sb(gla, "hgrn_gate", [P, GLA_H, TOK])
        weights = ExitStack()
        share_weight_buffers(weights)
        linear("bq", n_hi, n_lo, feature_units(ALL), copy_units(q_silu, 0, func=ACT.Silu), ahead=True)
        linear("bg", n_hi, n_lo, feature_units(ALL), copy_units(g_silu, 0, func=ACT.Silu), ahead=True)
        linear("bf", n_hi, n_lo, feature_units(ALL), copy_units(keep, 0, func=ACT.Sigmoid), ahead=True)

        def token_units(blocks, nt=256):
            return [("T", slice(b * P, (b + 1) * P), 0, nt) for b in range(blocks)]

        def copy_token_units(buf, blocks, first=0):
            def evac(act, t, j, count, res):
                for b in range(blocks):
                    act.wait_ge(unit_done, count(b))
                    nc.scalar.copy(buf[:, first + b, bass.ds(t * 256, 256)], res[b][:, 0, 0:256]).then_inc(unit_free, 1)
            return evac

        gs = {k: sem("hgrn_" + k) for k in ("tables", "zeroed", "top", "bound_exp", "bound", "f", "ln", "k", "cum", "dist",
                                           "exp", "q_scaled", "k_scaled", "turned", "turned_read", "scores", "masked",
                                           "kv", "link", "exponents_read", "states", "out", "out_read")}
        restart = mixed_0[:, 4 + GLA_H - 1, :]
        linear("bi", n_hi, n_lo, token_units(6), copy_token_units(i_tok, 6))
        weights.close()
        normed_scope.close()

        CH = TOK // 64
        ORDER = ([8, 9, 10, 11, 0, 1, 2, 3, 4, 5, 6, 7], [11, 10, 9, 8, 7, 6, 5, 4, 3, 2, 1, 0])
        REF, LAST = (32, 31), (63, 0)
        JOBS = 2 * GLA_H
        with ExitStack() as scope:
            tri64 = sb(scope, "tri64", [P, 2, 64])
            bound = sb(scope, "hgrn_bound", [P, 6, GLA_H])
            log_f = sb(scope, "hgrn_log_f", [P, TOK])
            q_ref = sb(scope, "hgrn_q_ref", [P, 2, TOK])
            k_ref = sb(scope, "hgrn_k_ref", [P, 2, TOK])
            k_end = sb(scope, "hgrn_k_end", [P, 2, TOK])
            q_cum = sb(scope, "hgrn_q_cum", [P, 4, TOK])
            decay = sb(scope, "hgrn_decay", [P, 4, CH])
            state = sb(scope, "hgrn_state", [P, 4, CH, P])
            scores = sb(scope, "hgrn_scores", [P, 4, CH, 64])
            k_end_tok = sb(scope, "hgrn_k_end_tok", [P, CH, P])
            p_turned = psum(scope, "hgrn_p_turned", [P, 1024])
            p_scores = psum(scope, "hgrn_p_scores", [P, 512])
            p_kv = psum(scope, "hgrn_p_kv", [P, 1536])
            p_out = psum(scope, "hgrn_p_out", [P, 1024])

            def by_chunk(ap):
                return ap.rearrange("p (c n) -> p c n", n=64)

            def at_chunk(ap, place):
                return by_chunk(ap)[:, :, place:place + 1].broadcast_to([P, CH, 64])

            def gate_of(n):
                return keep[:, GLA_H * (n % 2) + n // 2, :]

            with stage_block() as block:
                @block.sync
                def _(sp):
                    sp.dma_start(tri64[:], io["tri64"]).then_inc(gs["tables"], 16)
                    sp.dma_start(restart, io["restart"]).then_inc(gs["tables"], 16)

                @block.vector
                def _(dve):
                    a, b = cols("lb")[:, 0:GLA_H], cols("lb")[:, GLA_H:2 * GLA_H]
                    nc.vector.tensor_tensor(bound[:, 0, :], a, b, ALU.max).then_inc(gs["top"], 1)
                    dve.wait_ge(gs["top"], 1)
                    nc.vector.tensor_tensor(bound[:, 1, :], a, bound[:, 0, :], ALU.subtract)
                    nc.vector.tensor_tensor(bound[:, 2, :], b, bound[:, 0, :], ALU.subtract).then_inc(gs["top"], 1)
                    dve.wait_ge(gs["bound_exp"], 1)
                    nc.vector.tensor_tensor(bound[:, 3, :], bound[:, 1, :], bound[:, 2, :], ALU.add).then_inc(gs["bound"], 1)
                    dve.wait_ge(gs["bound"], 1)
                    nc.vector.reciprocal(bound[:, 3, :], bound[:, 3, :]).then_inc(gs["bound"], 1)
                    dve.wait_ge(gs["bound"], 2)
                    nc.vector.tensor_tensor(bound[:, 4, :], bound[:, 1, :], bound[:, 3, :], ALU.mult)
                    nc.vector.tensor_tensor(bound[:, 5, :], bound[:, 2, :], bound[:, 3, :], ALU.mult).then_inc(gs["bound"], 1)
                    dve.wait_ge(gs["bound"], 3)
                    dve.wait_ge(gs["tables"], 32)

                    def exponents(n):
                        f, d, x, cum = gate_of(n), n % 2, n % 2, q_cum[:, n % 4, :]
                        nc.vector.tensor_scalar(f, f, bound[:, 5, n // 2:n // 2 + 1], bound[:, 4, n // 2:n // 2 + 1],
                                                ALU.mult, ALU.add).then_inc(gs["f"], 1)
                        dve.wait_ge(gs["ln"], n + 1)
                        way = slice(None, None, 1 if d == 0 else -1)
                        wait(dve, gs["out"], n // 2 - 1)
                        nc.vector.tensor_tensor_scan(cum[:, way], restart, log_f[:, way], 0.0, ALU.mult, ALU.add)\
                            .then_inc(gs["cum"], 1)
                        dve.wait_ge(gs["cum"], n + 1)
                        wait(dve, gs["scores"], n - 1)
                        wait(dve, gs["turned"], n - 1)
                        nc.vector.tensor_tensor(by_chunk(q_ref[:, x, :]), by_chunk(cum), at_chunk(cum, REF[d]),
                                                ALU.subtract)
                        nc.vector.tensor_tensor(by_chunk(k_end[:, x, :]), at_chunk(cum, LAST[d]), by_chunk(cum),
                                                ALU.subtract).then_inc(gs["dist"], 1)

                    def scale_queries(n):
                        q = q_silu[:, n // 2, :]
                        dve.wait_ge(gs["exp"], n + 1)
                        nc.vector.tensor_tensor(q_ref[:, n % 2, :], q_ref[:, n % 2, :], q, ALU.mult)
                        nc.vector.tensor_tensor(q_cum[:, n % 4, :], q_cum[:, n % 4, :], q, ALU.mult)\
                            .then_inc(gs["q_scaled"], 1)

                    def mask_scores(n):
                        d = n % 2
                        wait(dve, gs["out"], n // 2 - 1)
                        dve.wait_ge(gs["scores"], n + 1)
                        for odd in range(2):
                            part = slice(64 * odd, 64 * odd + 64)
                            last = nc.vector.copy_predicated(
                                scores[part, n % 4, odd:CH:2, :],
                                tri64[part, d:d + 1, :].bitcast(U32).broadcast_to([64, CH // 2, 64]),
                                p_scores[part, 0:CH * 32].rearrange("p (c n) -> p c n", n=64))
                        last.then_inc(gs["masked"], 1)

                    def chain_states(n):
                        d = n % 2
                        dve.wait_ge(gs["kv"], n + 1)
                        for link, (a, b) in enumerate(zip(ORDER[d], ORDER[d][1:])):
                            nc.vector.scalar_tensor_tensor(
                                state[:, n % 4, b, :], state[:, n % 4, a, :], decay[:, n % 4, a:a + 1],
                                p_kv[:, a * P:(a + 1) * P], ALU.mult, ALU.add).then_inc(gs["link"], 1)
                            dve.wait_ge(gs["link"], n * (CH - 1) + link + 1)
                        nc.vector.engine_nop().then_inc(gs["states"], 1)

                    exponents(0)
                    nc.vector.memset(scores[:], 0.0)
                    nc.vector.memset(p_scores[:], 0.0)
                    nc.vector.memset(k_end_tok[:], 0.0)
                    for n in range(4):
                        last = nc.vector.memset(state[:, n, ORDER[n % 2][0], :], 0.0)
                    last.then_inc(gs["zeroed"], 1)
                    dve.wait_ge(gs["zeroed"], 1)
                    scale_queries(0)
                    for n in range(JOBS):
                        if n + 1 < JOBS:
                            exponents(n + 1)
                        mask_scores(n)
                        chain_states(n)
                        if n + 1 < JOBS:
                            scale_queries(n + 1)

                @block.scalar
                def _(act):
                    def logarithm(n):
                        act.wait_ge(gs["f"], n + 1)
                        nc.scalar.activation(log_f[:], gate_of(n), ACT.Ln).then_inc(gs["ln"], 1)
                        nc.scalar.activation(gate_of(n), gate_of(n), ACT.Identity, scale=-1.0, bias=1.0)\
                            .then_inc(gs["k"], 1)

                    def exponentials(n):
                        d, x = n % 2, n % 2
                        act.wait_ge(gs["dist"], n + 1)
                        wait(act, gs["states"], n - 3)
                        nc.scalar.activation(decay[:, n % 4, :], by_chunk(q_cum[:, n % 4, :])[:, :, LAST[d]], ACT.Exp)\
                            .then_inc(gs["exponents_read"], 1)
                        nc.scalar.activation(k_ref[:, x, :], q_ref[:, x, :], ACT.Exp, scale=-1.0)\
                            .then_inc(gs["exponents_read"], 1)
                        nc.scalar.activation(k_end[:, x, :], k_end[:, x, :], ACT.Exp)
                        act.wait_ge(gs["exponents_read"], 2 * n + 2)
                        nc.scalar.activation(q_ref[:, x, :], q_ref[:, x, :], ACT.Exp)
                        nc.scalar.activation(q_cum[:, n % 4, :], q_cum[:, n % 4, :], ACT.Exp).then_inc(gs["exp"], 1)

                    def copy_turned(n):
                        act.wait_ge(gs["turned"], n + 1)
                        wait(act, gs["kv"], n)
                        for odd in range(2):
                            part = slice(64 * odd, 64 * odd + 64)
                            last = nc.scalar.copy(k_end_tok[part, odd:CH:2, :],
                                                  p_turned[part, 0:TOK].rearrange("p (c n) -> p c n", n=P))
                        last.then_inc(gs["turned_read"], 1)

                    def copy_out(h):
                        act.wait_ge(gs["out"], h + 1)
                        nc.scalar.copy(mixed_0[:, 4 + h, :], p_out[:, 0:TOK]).then_inc(gs["out_read"], 1)

                    act.wait_ge(gs["top"], 2)
                    nc.scalar.activation(bound[:, 1:3, :], bound[:, 1:3, :], ACT.Exp).then_inc(gs["bound_exp"], 1)
                    logarithm(0)
                    exponentials(0)
                    act.wait_ge(gs["zeroed"], 1)
                    for n in range(JOBS):
                        if n + 1 < JOBS:
                            logarithm(n + 1)
                        copy_turned(n)
                        if n + 1 < JOBS:
                            exponentials(n + 1)
                        if n % 2 == 1 and n >= 3:
                            copy_out(n // 2 - 1)
                    copy_out(GLA_H - 1)

                @block.gpsimd
                def _(pool):
                    for n in range(JOBS):
                        pool.wait_ge(gs["k"], n + 1)
                        pool.wait_ge(gs["exp"], n + 1)
                        for scaled in (k_end, k_ref):
                            nc.gpsimd.tensor_tensor(scaled[:, n % 2, :], scaled[:, n % 2, :], gate_of(n), ALU.mult)\
                                .then_inc(gs["k_scaled"], 1)

                @block.tensor
                def _(pe):
                    def turn_keys(n):
                        pe.wait_ge(gs["k_scaled"], 2 * n + 2)
                        wait(pe, gs["turned_read"], n)
                        for b in range(TOK // P):
                            mm = nc.tensor.transpose(p_turned[:, b * P:(b + 1) * P], k_end[:, n % 2, b * P:(b + 1) * P],
                                                     ident[:])
                        mm.then_inc(gs["turned"], 1)

                    def score(n):
                        d, x = n % 2, n % 2
                        pe.wait_ge(gs["q_scaled"], n + 1)
                        wait(pe, gs["masked"], n)
                        for c in range(CH):
                            for half in range(2):
                                key = c * 64 + 32 * half
                                first, width = (0, 64) if half == d else (32 * half, 32)
                                part, col = slice(key % P, key % P + 32), (c // 2) * 64 + first
                                mm = nc.tensor.matmul(p_scores[part, col:col + width], k_ref[:, x, key:key + 32],
                                                      q_ref[:, x, c * 64 + first:c * 64 + first + width],
                                                      start=True, stop=True, tile_position=(0, key % P))
                        mm.then_inc(gs["scores"], 1)

                    def write_states(n):
                        h = n // 2
                        pe.wait_ge(gs["turned_read"], n + 1)
                        wait(pe, gs["states"], n)
                        for c in range(CH):
                            mm = nc.tensor.matmul(p_kv[:, c * P:(c + 1) * P], k_end_tok[:, c, :],
                                                  i_tok[:, c // 2, h * P:(h + 1) * P], start=True, stop=True)
                        mm.then_inc(gs["kv"], 1)

                    def sum_out(h, half):
                        if half == 0:
                            pe.wait_ge(gs["masked"], 2 * h + 2)
                            pe.wait_ge(gs["states"], 2 * h + 2)
                            wait(pe, gs["out_read"], h)
                        for b in range(3 * half, 3 * half + 3):
                            def add_scores(e):
                                return nc.tensor.matmul(p_out[:, b * P:(b + 1) * P], i_tok[:, b, h * P:(h + 1) * P],
                                                        scores[:, (2 * h + e) % 4, 2 * b:2 * b + 2, :], start=e == 0, stop=e == 1)

                            add_scores(0)
                            for c in (2 * b, 2 * b + 1):
                                tok = slice(c * 64, c * 64 + 64)
                                for e in range(2):
                                    nc.tensor.matmul(p_out[:, tok], state[:, (2 * h + e) % 4, c, :], q_cum[:, (2 * h + e) % 4, tok],
                                                     start=False, stop=False)
                            mm = add_scores(1)
                        if half == 1:
                            mm.then_inc(gs["out"], 1)

                    pe.wait_ge(gs["zeroed"], 1)
                    turn_keys(0)
                    score(0)
                    for n in range(JOBS):
                        write_states(n)
                        if n + 1 < JOBS:
                            turn_keys(n + 1)
                            score(n + 1)
                        if n:
                            sum_out((n - 1) // 2, (n - 1) % 2)
                    sum_out(GLA_H - 1, 1)

        head_norm("hgrn_norm", GLA_H, 1, TOK, lambda h, j: mixed_0[:, 4 + h, :], cols("hgrn_g"),
                  lambda h, j: g_silu[:, h, :])
        gla.close()

        with ExitStack() as scope:
            m_hi = sb(scope, "mixed_0_hi", [P, DC, TOK], F32R)
            m_lo = sb(scope, "mixed_0_lo", [P, DC, TOK], F32R)
            mixed_cut = cut(mixed_0, m_hi, m_lo, DC)
            linear("eo", m_hi, m_lo, feature_units(ALL), None,
                   add_residual(ALL, [gates_of(0, 0, 0), gates_of(0, 0, 1)], 2), mixed_cut)
        mix.close()

        with ExitStack() as scope:
            f_hi = sb(scope, "norm_b_hi", [P, DC, TOK], F32R)
            f_lo = sb(scope, "norm_b_lo", [P, DC, TOK], F32R)
            norm_b = norm_split(x_all, [group(0, 1, 0, 0, LAT), group(0, 1, 1, LAT, CTX)], f_hi, f_lo)
            feed_forward(0, f_hi, f_lo, ALL, add_residual(ALL, [gates_of(0, 1, 0), gates_of(0, 1, 1)], 1), norm_b)

        ret = ExitStack()
        ret_keys = ExitStack()
        k_ctx1 = sb(ret_keys, "ret_k_ctx", [P, DC, CTX])
        v_tok = sb(ret_keys, "ret_v", [P, TOK // P, 2048])
        with ExitStack() as scope:
            c_hi = sb(scope, "norm_c_hi", [P, DC, CTX], F32R)
            c_lo = sb(scope, "norm_c_lo", [P, DC, CTX], F32R)
            norm_c = norm_split(lambda c, s, m: x_ctx[0][:, c, s:s + m], [group(1, 0, 1, 0, CTX)], c_hi, c_lo)
            share_weight_buffers(scope)
            linear("ckv0", c_hi, c_lo, feature_units([(0, CTX)]), copy_units(k_ctx1, 0), source=norm_c, ahead=True)
            linear("ckv1", c_hi, c_lo, token_units(2), copy_token_units(v_tok, 2, LAT // P))
        ctx_scope.close()

        normed_1 = ExitStack()
        n1_hi = sb(normed_1, "norm_d_hi", [P, DC, LAT], F32R)
        n1_lo = sb(normed_1, "norm_d_lo", [P, DC, LAT], F32R)

        def x_only(c, s, m):
            return x_lat[:, c, s:s + m]

        norm_d = norm_split(x_only, [group(1, 0, 0, 0, LAT)], n1_hi, n1_lo)
        qk_ret = sb(ret, "ret_qk", [P, 2 * DC, LAT])
        weights = ExitStack()
        share_weight_buffers(weights)
        with ExitStack() as scope:
            rope = sb(scope, "ret_rope", [P, 2, LAT])
            part = sb(scope, "ret_rope_parts", [P, 4, LAT])
            with stage_block() as block:
                @block.sync
                def _(sp):
                    sp.dma_start(rope[:], io["retrope"]).then_inc(rope_loaded, 16)
                    sp.wait_ge(rope_loaded, 16)

            def evac_rope(dve, t, j, count, res):
                dve.wait_ge(rope_turned, t + 1)
                for u in range(2):
                    dve.wait_ge(unit_done, count(u))
                    nc.vector.tensor_tensor(part[:, 2 * u, :], res[u][:, 0, :], rope[:, 0, :], ALU.mult)
                    nc.vector.tensor_tensor(part[:, 2 * u + 1, :], res[u][:, 0, :], rope[:, 1, :], ALU.mult)\
                        .then_inc(unit_free, 1)
                dve.wait_ge(unit_free, count(1))
                nc.vector.tensor_tensor(qk_ret[:, bass.ds(2 * t, 1), :].rearrange("p o n -> p (o n)"),
                                        part[:, 0, :], part[:, 3, :], ALU.subtract)
                nc.vector.tensor_tensor(qk_ret[:, bass.ds(2 * t + 1, 1), :].rearrange("p o n -> p (o n)"),
                                        part[:, 2, :], part[:, 1, :], ALU.add).then_inc(rope_turned, 1)

            linear("rqk", n1_hi, n1_lo, feature_units(ONLY_LAT), None, evac_rope, norm_d, ahead=True)
        linear("rv", n1_hi, n1_lo, token_units(4), copy_token_units(v_tok, 4))
        weights.close()

        KB = TOK // P

        def ret_out(h, j):
            return qk_ret[:, 2 * h + j if j < 2 else 8 + 2 * h + j - 2, :]

        rs = {k: sem("ret_" + k) for k in ("table_0", "table_1", "scores", "decayed", "mixed", "mixed_read")}
        with ExitStack() as scope:
            table = sb(scope, "ret_decay", [P, 2, 12 * P])
            decayed = sb(scope, "ret_decayed", [P, 3, LAT])
            p_scores = psum(scope, "ret_p_scores", [P, 2, 512])
            p_mixed = psum(scope, "ret_p_mixed", [P, 4, 512])
            with stage_block() as block:
                @block.sync
                def _(sp):
                    for h in range(RET_H):
                        if h >= 2:
                            sp.wait_ge(rs["decayed"], (h - 1) * KB)
                        sp.dma_start(table[:, h % 2, :], io["decay"][h]).then_inc(rs[f"table_{h % 2}"], 16)

                @block.tensor
                def _(pe):
                    def scores(n):
                        h, b = divmod(n, KB)
                        if n >= 2:
                            pe.wait_ge(rs["decayed"], n - 1)
                        for j in range(2):
                            k = qk_ret[:, 8 + 2 * h + j, b * P:(b + 1) * P] if b < 4 else \
                                k_ctx1[:, 2 * h + j, (b - 4) * P:(b - 3) * P]
                            mm = nc.tensor.matmul(p_scores[:, n % 2, :], k, qk_ret[:, 2 * h + j, :],
                                                  start=j == 0, stop=j == 1)
                        mm.then_inc(rs["scores"], 1)

                    scores(0)
                    for n in range(RET_H * KB):
                        h, b = divmod(n, KB)
                        if n + 1 < RET_H * KB:
                            scores(n + 1)
                        pe.wait_ge(rs["decayed"], n + 1)
                        if b == 0 and h >= 1:
                            pe.wait_ge(rs["mixed_read"], h)
                        for e in range(4):
                            mm = nc.tensor.matmul(p_mixed[:, e, :], v_tok[:, b, h * 512 + e * P:h * 512 + (e + 1) * P],
                                                  decayed[:, n % 3, :], start=b == 0, stop=b == KB - 1)
                        mm.then_inc(rs["mixed"], 1)

                @block.vector
                def _(dve):
                    for n in range(RET_H * KB):
                        h, b = divmod(n, KB)
                        if b == 0:
                            dve.wait_ge(rs[f"table_{h % 2}"], 16 * (h // 2 + 1))
                        dve.wait_ge(rs["scores"], n + 1)
                        if n >= 3:
                            dve.wait_ge(rs["mixed"], n - 2)
                        at = (3 - b) * P if b < 4 else 7 * P + (5 - b) * P
                        nc.vector.tensor_tensor(decayed[:, n % 3, :], p_scores[:, n % 2, :],
                                                table[:, h % 2, at:at + LAT], ALU.mult).then_inc(rs["decayed"], 1)

                @block.scalar
                def _(act):
                    for h in range(RET_H):
                        act.wait_ge(rs["mixed"], (h + 1) * KB)
                        for e in range(4):
                            last = nc.scalar.copy(ret_out(h, e), p_mixed[:, e, :])
                        last.then_inc(rs["mixed_read"], 1)

        ret_keys.close()
        ret_norm = head_norm("ret_norm", RET_H, 4, LAT, ret_out, within=True)

        gate_sem = sem("gate_ready")
        gates_done = [0]

        def gate_linear(name, x_hi, x_lo, buf, func, other=None, ahead=False, source=None):
            n = shapes[name][0]
            base = gates_done[0]
            gates_done[0] += 2 * n
            with ExitStack() as scope:
                gate = sb(scope, f"{name}_gate", [P, 2, LAT])
                gated = sem(f"{name}_gated") if other is not None else None

                def evac_act(act, t, j, count, res):
                    for u in range(2):
                        act.wait_ge(unit_done, count(u))
                        act.wait_ge(unit_free, count(0) - 1)
                        nc.scalar.activation(gate[:, u, :], res[u][:, 0, :], func).then_inc(gate_sem, 1)

                def evac_dve(dve, t, j, count, res):
                    for u in range(2):
                        b = buf[:, bass.ds(2 * t + u, 1), :].rearrange("p o n -> p (o n)")
                        dve.wait_ge(gate_sem, 2 * t + (base + u + 1))
                        if other is None:
                            nc.vector.tensor_tensor(b, b, gate[:, u, :], ALU.mult).then_inc(unit_free, 1)
                        else:
                            o = other[:, bass.ds(2 * t + u, 1), :].rearrange("p o n -> p (o n)")
                            nc.vector.tensor_tensor(b, b, gate[:, u, :], ALU.mult).then_inc(gated, 1)
                            dve.wait_ge(gated, 2 * t + (u + 1))
                            nc.vector.tensor_tensor(o, o, b, ALU.add).then_inc(unit_free, 1)

                linear(name, x_hi, x_lo, feature_units(ONLY_LAT), evac_act, evac_dve, source, ahead)

        weights = ExitStack()
        share_weight_buffers(weights)
        gate_linear("rg", n1_hi, n1_lo, qk_ret, ACT.Silu, ahead=True, source=ret_norm)
        normed_1.close()
        with ExitStack() as scope:
            m_hi = sb(scope, "mixed_1_hi", [P, 2 * DC, LAT], F32R)
            m_lo = sb(scope, "mixed_1_lo", [P, 2 * DC, LAT], F32R)
            mixed_cut = cut(qk_ret, m_hi, m_lo, 2 * DC)
            linear("ro", m_hi, m_lo, [("F", 0, ONLY_LAT)], None, add_residual(ONLY_LAT, [gates_of(1, 0, 0)], 1),
                   mixed_cut)
        weights.close()
        ret.close()
        with ExitStack() as scope:
            f_hi = sb(scope, "norm_e_hi", [P, DC, LAT], F32R)
            f_lo = sb(scope, "norm_e_lo", [P, DC, LAT], F32R)
            norm_e = norm_split(x_only, [group(1, 1, 0, 0, LAT)], f_hi, f_lo)
            feed_forward(1, f_hi, f_lo, ONLY_LAT, add_residual(ONLY_LAT, [gates_of(1, 1, 0)], 1), norm_e)

        two = ExitStack()
        t_hi = sb(two, "norm_f_hi", [P, DC, LAT], F32R)
        t_lo = sb(two, "norm_f_lo", [P, DC, LAT], F32R)
        norm_f = norm_split(x_only, [(0, LAT, lambda c: scale_2[:, c:c + 1], lambda c: ada[:, c:c + 1])], t_hi, t_lo)

        NB = LAT // P
        y_a = sb(two, "y_a", [P, DC, LAT])
        dn = ExitStack()
        qkv = sb(dn, "dn_qkv", [P, 3 * DN_H, LAT])
        ba = sb(dn, "dn_beta_a", [P, NB, 16])
        weights = ExitStack()
        share_weight_buffers(weights)
        with ExitStack() as scope:
            conv = sb(scope, "conv_sum", [P, 2, LAT])

            def evac_conv(dve, t, j, count, res):
                for u in range(2):
                    def tap(k):
                        c, _ = SMALL["conv"]
                        return small[:, bass.ds(8 * t + (c + 4 * u + k), 1)]

                    dve.wait_ge(unit_done, count(u))
                    dve.wait_ge(silu_sem, 2 * t + 2)
                    nc.vector.tensor_scalar(conv[:, u, :], res[u][:, 0, :], tap(3), None, ALU.mult).then_inc(conv_sem, 1)
                    for k in (2, 1, 0):
                        dve.wait_ge(conv_sem, 8 * t + (4 * u + 3 - k))
                        lag = 3 - k
                        last = nc.vector.scalar_tensor_tensor(conv[:, u, lag:], res[u][:, 0, 0:LAT - lag], tap(k),
                                                              conv[:, u, lag:], ALU.mult, ALU.add)
                        last.then_inc(conv_sem, 1)
                    dve.wait_ge(conv_sem, 8 * t + (4 * u + 4))
                    dve.sem_inc(unit_free, 1)

            def evac_silu(act, t, j, count, res):
                for u in range(2):
                    act.wait_ge(conv_sem, 8 * t + (4 * u + 4))
                    nc.scalar.activation(qkv[:, bass.ds(2 * t + u, 1), :].rearrange("p o n -> p (o n)"), conv[:, u, :],
                                         ACT.Silu).then_inc(silu_sem, 1)

            linear("dqkv", t_hi, t_lo, feature_units(ONLY_LAT), evac_silu, evac_conv, norm_f, ahead=True)

        ba_rows = sb(dn, "dn_beta_a_rows", [2 * DN_H, LAT])

        def evac_ba(act, t, j, count, res):
            act.wait_ge(unit_done, count(0))
            nc.scalar.copy(ba_rows[:], res[0][0:2 * DN_H, 0, :]).then_inc(unit_free, 1)

        dc = {k: sem("dn_" + k) for k in ("turned", "columns", "tables", "a", "abs", "exp", "log", "g", "cum", "ready")}
        upper = sb(dn, "upper", [P, P])
        levels = sb(dn, "levels", [P, 7, P])
        linear("dba", t_hi, t_lo, [("F", 0, ONLY_LAT)], evac_ba,
               loads=[(upper[:], "upper", dc["tables"]), (levels[:], "levels", dc["tables"])])
        weights.close()

        beta = sb(dn, "dn_beta", [P, NB, DN_H])
        g_tok = sb(dn, "dn_g", [P, NB, DN_H])
        g_cum = sb(dn, "dn_g_cum", [P, NB, DN_H])
        with ExitStack() as scope:
            a_in = sb(scope, "dn_a_in", [P, NB, DN_H])
            a_abs = sb(scope, "dn_a_abs", [P, NB, DN_H])
            rate = sb(scope, "dn_rate", [P, DN_H])
            p_cum = psum(scope, "dn_p_cum", [P, NB * DN_H])
            p_cols = psum(scope, "dn_p_cols", [P, NB, 2 * DN_H])

            def per_head(ap):
                return ap.rearrange("p (o h) -> p o h", o=1).broadcast_to([P, NB, DN_H])

            with stage_block() as block:
                @block.sync
                def _(sp):
                    sp.wait_ge(dc["tables"], 32)

                @block.scalar
                def _(act):
                    act.wait_ge(dc["columns"], 1)
                    nc.scalar.activation(beta[:], ba[:, :, 0:DN_H], ACT.Sigmoid)
                    nc.scalar.activation(rate[:], cols("a_log"), ACT.Exp)
                    act.wait_ge(dc["a"], 1)
                    nc.scalar.activation(a_abs[:], a_in[:], ACT.Abs).then_inc(dc["abs"], 1)
                    act.wait_ge(dc["abs"], 1)
                    nc.scalar.activation(a_abs[:], a_abs[:], ACT.Exp, scale=-1.0).then_inc(dc["exp"], 1)
                    act.wait_ge(dc["exp"], 1)
                    nc.scalar.activation(a_abs[:], a_abs[:], ACT.Ln, bias=1.0).then_inc(dc["log"], 1)

                @block.vector
                def _(dve):
                    dve.wait_ge(dc["turned"], 1)
                    nc.vector.tensor_copy(ba[:], p_cols[:]).then_inc(dc["columns"], 1)
                    dve.wait_ge(dc["columns"], 1)
                    nc.vector.tensor_tensor(a_in[:], ba[:, :, DN_H:2 * DN_H], per_head(cols("dt_bias")), ALU.add)\
                        .then_inc(dc["a"], 1)
                    dve.wait_ge(dc["log"], 1)
                    nc.vector.scalar_tensor_tensor(a_in[:], a_in[:], 0.0, a_abs[:], ALU.max, ALU.add).then_inc(dc["g"], 1)
                    dve.wait_ge(dc["g"], 1)
                    nc.vector.scalar_tensor_tensor(g_tok[:], a_in[:], -1.0, per_head(rate[:]), ALU.mult, ALU.mult)\
                        .then_inc(dc["g"], 1)
                    dve.wait_ge(dc["cum"], 1)
                    nc.vector.tensor_copy(g_cum[:].rearrange("p c h -> p (c h)"), p_cum[:]).then_inc(dc["ready"], 1)

                @block.tensor
                def _(pe):
                    for b in range(NB):
                        mm = nc.tensor.transpose(p_cols[:, b, :], ba_rows[:, b * P:(b + 1) * P],
                                                 ident[0:2 * DN_H, 0:2 * DN_H])
                    mm.then_inc(dc["turned"], 1)
                    pe.wait_ge(dc["tables"], 32)
                    pe.wait_ge(dc["g"], 2)
                    nc.tensor.matmul(p_cum[:], upper[:], g_tok[:].rearrange("p c h -> p (c h)"), start=True, stop=True)\
                        .then_inc(dc["cum"], 1)

        d = {k: sem("delta_" + k) for k in (
            "columns", "squares", "sums", "roots", "rstd", "unit", "spread", "distances", "exps", "small", "products",
            "turned", "tokens", "grams", "masked", "lower", "eye", "join", "half", "half_read", "step", "next",
            "solved", "solved_read", "norms", "seen", "written", "fresh", "stored", "out", "out_read", "gram_read")}
        pair_scope = ExitStack()

        def two_of(name, shape, count=2):
            return [sb(pair_scope, f"delta_{name}_{a}", shape) for a in range(count)]

        g_col, c_col, b_col = (two_of(n, [P, NB]) for n in ("g_col", "c_col", "b_col"))
        last_col, end_col, bg_col = (two_of(n, [P, NB]) for n in ("last_col", "end_col", "bg_col"))
        squares = two_of("squares", [P, 2, LAT])
        roots = sb(pair_scope, "delta_roots", [P, LAT])
        (q_unit, k_unit, v_copy, grow, low, high, k_beta, k_end_t, v_beta, join, inv, inv_t, half_t, fresh) = (
            two_of(n, [P, LAT]) for n in ("q_unit", "k_unit", "v_copy", "grow", "low", "high", "k_beta", "k_end",
                                         "v_beta", "join", "inv", "inv_t", "half_t", "fresh"))
        state2 = two_of("state", [P, P])
        banks = [[psum(pair_scope, f"delta_p{a}{b}", [P, LAT]) for b in range(4)] for a in range(2)]

        def ch(ap, c):
            return ap[:, c * P:(c + 1) * P]

        def chunks(ap):
            return ap.rearrange("p (c n) -> p c n", n=P)

        def over_cols(ap):
            return ap.rearrange("p (c o) -> p c o", o=1).broadcast_to([P, NB, P])

        def over_chunks(ap):
            return ap.rearrange("p (o n) -> p o n", o=1).broadcast_to([P, NB, P])

        with nc.Fori(0, DN_H // 2) as pair:
            with stage_block() as block:
                @block.vector
                def _(dve):
                    for s in d.values():
                        dve.sem_clear(s)

            def head(a, part):
                return qkv[:, bass.ds(2 * pair + (8 * part + a), 1), :].rearrange("p o n -> p (o n)")

            with stage_block() as block:
                @block.scalar
                def _(act):
                    for a in range(2):
                        nc.scalar.activation(squares[a][:, 0, :], head(a, 0), ACT.Square)
                        nc.scalar.activation(squares[a][:, 1, :], head(a, 1), ACT.Square).then_inc(d["squares"], 1)
                    act.wait_ge(d["sums"], 1)
                    nc.scalar.activation(roots[:], banks[0][0][:], ACT.Sqrt, bias=eps_col).then_inc(d["roots"], 1)
                    for a in range(2):
                        act.wait_ge(d["distances"], a + 1)
                        nc.scalar.activation(grow[a][:], banks[a][2][:], ACT.Exp)
                        nc.scalar.activation(low[a][:], low[a][:], ACT.Exp, scale=-1.0)
                        nc.scalar.activation(high[a][:], high[a][:], ACT.Exp)
                        nc.scalar.activation(end_col[a][:], end_col[a][:], ACT.Exp)
                        nc.scalar.activation(bg_col[a][:], c_col[a][:], ACT.Exp)
                        nc.scalar.activation(last_col[a][:], last_col[a][:], ACT.Exp).then_inc(d["exps"], 1)
                    for m in range(1, 7):
                        for a in range(2):
                            act.wait_ge(d["half"], 2 * m + a + 1)
                            nc.scalar.copy(half_t[a][:], banks[a][0][:]).then_inc(d["half_read"], 1)
                    for a in range(2):
                        act.wait_ge(d["solved"], a + 1)
                        nc.scalar.copy(half_t[a][:], banks[a][0][:])
                        nc.scalar.copy(join[a][:], banks[a][1][:]).then_inc(d["solved_read"], 1)
                    for a in range(2):
                        act.wait_ge(d["out"], a + 1)
                        nc.scalar.copy(y_a[:, bass.ds(2 * pair + a, 1), :].rearrange("p o n -> p (o n)"), banks[a][3][:])\
                            .then_inc(d["out_read"], 1)

                @block.vector
                def _(dve):
                    for a in range(2):
                        for dst, src in ((g_col, g_tok), (c_col, g_cum), (b_col, beta)):
                            last = nc.vector.tensor_copy(dst[a][:].rearrange("p (c o) -> p c o", o=1),
                                                         src[:, :, bass.ds(2 * pair + a, 1)])
                        last.then_inc(d["columns"], 1)
                        nc.vector.tensor_copy(v_copy[a][:], head(a, 2)).then_inc(d["small"], 1)
                    dve.wait_ge(d["roots"], 1)
                    nc.vector.reciprocal(roots[:], roots[:]).then_inc(d["rstd"], 1)
                    for a in range(2):
                        dve.wait_ge(d["norms"], a + 1)
                        nc.vector.scalar_tensor_tensor(q_unit[a][:], head(a, 0), P ** -0.5, banks[a][0][:],
                                                       ALU.mult, ALU.mult)
                        nc.vector.tensor_tensor(k_unit[a][:], head(a, 1), banks[a][1][:], ALU.mult)\
                            .then_inc(d["unit"], 1)
                    for a in range(2):
                        dve.wait_ge(d["spread"], a + 1)
                        spread = banks[a][2]
                        dve.wait_ge(d["columns"], a + 1)
                        nc.vector.tensor_copy(last_col[a][:], spread[:, P - 1:LAT:P]).then_inc(d["small"], 1)
                        for c in range(NB):
                            nc.vector.tensor_scalar(ch(low[a], c), ch(spread, c), c_col[a][:, c:c + 1], 0.0,
                                                    ALU.subtract, ALU.max)
                            nc.vector.tensor_scalar(ch(high[a], c), ch(spread, c), c_col[a][:, c:c + 1], 0.0,
                                                    ALU.subtract, ALU.min)
                        dve.wait_ge(d["small"], 2 + a + 1)
                        nc.vector.tensor_tensor(end_col[a][:], last_col[a][:], c_col[a][:], ALU.subtract)\
                            .then_inc(d["distances"], 1)
                    for a in range(2):
                        dve.wait_ge(d["exps"], a + 1)
                        nc.vector.tensor_tensor(bg_col[a][:], bg_col[a][:], b_col[a][:], ALU.mult).then_inc(d["small"], 1)
                        nc.vector.tensor_tensor(grow[a][:], grow[a][:], q_unit[a][:], ALU.mult)
                        dve.wait_ge(d["turned"], a + 1)
                        dve.wait_ge(d["small"], 4 + a + 1)
                        keys, values = banks[a][0], banks[a][1]
                        nc.vector.tensor_tensor(chunks(k_beta[a][:]), chunks(keys[:]), over_cols(bg_col[a][:]), ALU.mult)
                        nc.vector.tensor_tensor(chunks(k_end_t[a][:]), chunks(keys[:]), over_cols(end_col[a][:]), ALU.mult)
                        nc.vector.tensor_tensor(chunks(v_beta[a][:]), chunks(values[:]), over_cols(b_col[a][:]), ALU.mult)\
                            .then_inc(d["tokens"], 1)
                    for a in range(2):
                        dve.wait_ge(d["grams"], a + 1)
                        dve.wait_ge(d["masked"], 2 * a + 2)
                        nc.vector.tensor_tensor(high[a][:], banks[a][3][:], high[a][:], ALU.mult)
                        nc.vector.tensor_tensor(low[a][:], banks[a][2][:], low[a][:], ALU.mult).then_inc(d["lower"], 1)
                    for m in range(7):
                        for a in range(2):
                            if m == 0:
                                dve.wait_ge(d["half"], a + 1)
                            else:
                                dve.wait_ge(d["step"], 2 * (m - 1) + a + 1)
                            if m < 6:
                                nc.vector.tensor_tensor(inv[a][:], inv[a][:], banks[a][1][:] if m else join[a][:],
                                                        ALU.subtract)
                            nc.vector.tensor_tensor(inv_t[a][:], inv_t[a][:], banks[a][3 if m else 0][:], ALU.subtract)\
                                .then_inc(d["next"], 1)
                    for c in range(NB):
                        for a in range(2):
                            if c:
                                dve.wait_ge(d["seen"], 2 * (c - 1) + a + 1)
                                nc.vector.tensor_tensor(ch(fresh[a], c), ch(half_t[a], c), banks[a][0][:, 0:P], ALU.subtract)\
                                    .then_inc(d["fresh"], 1)
                            else:
                                dve.wait_ge(d["solved_read"], a + 1)
                                nc.vector.tensor_copy(ch(fresh[a], c), ch(half_t[a], c)).then_inc(d["fresh"], 1)
                        for a in range(2):
                            if c < NB - 1:
                                dve.wait_ge(d["written"], 2 * c + a + 1)
                                if c:
                                    nc.vector.scalar_tensor_tensor(state2[a][:], state2[a][:], last_col[a][:, c:c + 1],
                                                                   banks[a][1][:, 0:P], ALU.mult, ALU.add)\
                                        .then_inc(d["stored"], 1)
                                else:
                                    nc.vector.tensor_copy(state2[a][:], banks[a][1][:, 0:P]).then_inc(d["stored"], 1)

                @block.gpsimd
                def _(pool):
                    for a in range(2):
                        for m in (inv, inv_t):
                            nc.gpsimd.tensor_copy(chunks(m[a][:]), over_chunks(ident[:])).then_inc(d["eye"], 1)
                    for a in range(2):
                        pool.wait_ge(d["exps"], a + 1)
                        nc.gpsimd.tensor_tensor(chunks(high[a][:]), chunks(high[a][:]), over_chunks(upper[:]), ALU.mult)\
                            .then_inc(d["masked"], 1)
                        pool.wait_ge(d["columns"], a + 1)
                        nc.gpsimd.tensor_tensor(chunks(low[a][:]), chunks(low[a][:]), over_cols(b_col[a][:]), ALU.mult)\
                            .then_inc(d["masked"], 1)
                    for m in range(7):
                        for a in range(2):
                            n = 2 * m + a
                            pool.wait_ge(d["lower"], a + 1)
                            if m:
                                pool.wait_ge(d["half"], n - 1)
                            if m == 1:
                                pool.wait_ge(d["next"], a + 1)
                            nc.gpsimd.tensor_tensor(chunks(join[a][:]), chunks(low[a][:]), over_chunks(levels[:, m, :]),
                                                    ALU.mult).then_inc(d["join"], 1)

                @block.tensor
                def _(pe):
                    for a in range(2):
                        pe.wait_ge(d["squares"], a + 1)
                        for r in range(2):
                            g = 32 * (2 * a + r)
                            mm = nc.tensor.matmul(banks[0][0][g:g + 32, :], ones[:, 0:32], squares[a][:, r, :],
                                                  start=True, stop=True, tile_position=(0, g))
                    mm.then_inc(d["sums"], 1)
                    for a in range(2):
                        pe.wait_ge(d["columns"], a + 1)
                        for c in range(NB):
                            mm = nc.tensor.matmul(ch(banks[a][2], c), g_col[a][:, c:c + 1].broadcast_to([P, P]), upper[:],
                                                  start=True, stop=True)
                        mm.then_inc(d["spread"], 1)
                    pe.wait_ge(d["rstd"], 1)
                    for a in range(2):
                        for r in range(2):
                            g = 32 * (2 * a + r)
                            mm = nc.tensor.matmul(banks[a][r][:], ident[:, g:g + 1].broadcast_to([P, P]), roots[:],
                                                  start=True, stop=True)
                        mm.then_inc(d["norms"], 1)
                    for a in range(2):
                        pe.wait_ge(d["unit"], a + 1)
                        pe.wait_ge(d["small"], a + 1)
                        for c in range(NB):
                            nc.tensor.transpose(ch(banks[a][0], c), ch(k_unit[a], c), ident[:])
                        for c in range(NB):
                            mm = nc.tensor.transpose(ch(banks[a][1], c), ch(v_copy[a], c), ident[:])
                        mm.then_inc(d["turned"], 1)
                    for a in range(2):
                        pe.wait_ge(d["exps"], a + 1)
                        for c in range(NB):
                            nc.tensor.matmul(ch(banks[a][2], c), ch(k_unit[a], c), ch(k_unit[a], c), start=True, stop=True)
                        for c in range(NB):
                            mm = nc.tensor.matmul(ch(banks[a][3], c), ch(k_unit[a], c), ch(q_unit[a], c), start=True, stop=True)
                        mm.then_inc(d["grams"], 1)
                    pe.wait_ge(d["eye"], 4)
                    for a in range(2):
                        pe.wait_ge(d["tokens"], a + 1)
                    def half_step(m, a):
                        n = 2 * m + a
                        pe.wait_ge(d["join"], n + 1)
                        if m:
                            pe.wait_ge(d["next"], n - 1)
                        for c in range(NB):
                            mm = nc.tensor.matmul(ch(banks[a][0], c), ch(join[a], c), ch(inv_t[a], c), start=True, stop=True)
                        mm.then_inc(d["half"], 1)

                    def full_step(m, a):
                        pe.wait_ge(d["half_read"], 2 * (m - 1) + a + 1)
                        for c in range(NB):
                            if m < 6:
                                nc.tensor.matmul(ch(banks[a][1], c), ch(half_t[a], c), ch(inv[a], c), start=True, stop=True)
                        for c in range(NB):
                            mm = nc.tensor.matmul(ch(banks[a][3], c), ch(inv[a], c), ch(half_t[a], c), start=True, stop=True)
                        mm.then_inc(d["step"], 1)

                    for m in range(7):
                        half_step(m, 0)
                        half_step(m, 1)
                        if m:
                            full_step(m, 0)
                            full_step(m, 1)
                    for a in range(2):
                        pe.wait_ge(d["next"], 12 + a + 1)
                        for c in range(NB):
                            nc.tensor.matmul(ch(banks[a][0], c), ch(inv_t[a], c), ch(v_beta[a], c), start=True, stop=True)
                        for c in range(NB):
                            mm = nc.tensor.matmul(ch(banks[a][1], c), ch(k_beta[a], c), ch(inv_t[a], c), start=True, stop=True)
                        mm.then_inc(d["solved"], 1)
                    for c in range(NB):
                        for a in range(2):
                            pe.wait_ge(d["solved_read"], a + 1)
                            if c:
                                pe.wait_ge(d["stored"], 2 * (c - 1) + a + 1)
                                nc.tensor.matmul(banks[a][0][:, 0:P], ch(join[a], c), state2[a][:], start=True, stop=True)\
                                    .then_inc(d["seen"], 1)
                        for a in range(2):
                            pe.wait_ge(d["fresh"], 2 * c + a + 1)
                            if c:
                                nc.tensor.matmul(ch(banks[a][3], c), state2[a][:], ch(grow[a], c), start=True, stop=False)
                            if c < NB - 1:
                                nc.tensor.matmul(banks[a][1][:, 0:P], ch(k_end_t[a], c), ch(fresh[a], c), start=True, stop=True)\
                                    .then_inc(d["written"], 1)
                            mm = nc.tensor.matmul(ch(banks[a][3], c), ch(fresh[a], c), ch(high[a], c), start=c == 0, stop=True)
                            if c == NB - 1:
                                mm.then_inc(d["out"], 1)
        pair_scope.close()
        dn.close()

        dn_norm = head_norm("dn_norm", DN_H, 1, LAT, lambda h, j: y_a[:, h, :], cols("dn_w"), within=True)
        weights = ExitStack()
        share_weight_buffers(weights)
        gate_linear("dz", t_hi, t_lo, y_a, ACT.Silu, ahead=True, source=dn_norm)

        with ExitStack() as scope:
            m_hi = sb(scope, "delta_hi", [P, DC, LAT], F32R)
            m_lo = sb(scope, "delta_lo", [P, DC, LAT], F32R)
            delta_cut = cut(y_a, m_hi, m_lo, DC)
            linear("pa", m_hi, m_lo, feature_units(ONLY_LAT), copy_units(y_a, 0), source=delta_cut, ahead=True)
        gate_linear("ga", t_hi, t_lo, y_a, ACT.Sigmoid)
        weights.close()

        WC = 6
        y_b = sb(two, "y_b", [P, WC, LAT])
        lse = sb(two, "dil_lse", [P, 4, 2 * WC])
        dil_scope = ExitStack()
        qk_t = sb(dil_scope, "dil_qk", [P, 2 * WC, P + LAT])
        v_t = sb(dil_scope, "dil_v", [P, 5, 2 * WC * 64])
        q_zero_t = sb(dil_scope, "dil_q_zero", [P, 2 * WC, P])
        near = sb(dil_scope, "dil_near", [P, 4, 2 * P])
        dil = sb(dil_scope, "dil_masks", [P, 2, P])
        dil_tables, dil_zeroed = sem("dil_tables"), sem("dil_zeroed")
        with stage_block() as block:
            @block.sync
            def _(sp):
                sp.dma_start(near[:], io["near"]).then_inc(dil_tables, 16)
                sp.dma_start(dil[:], io["dil"]).then_inc(dil_tables, 16)
                sp.wait_ge(dil_tables, 32)

            @block.vector
            def _(dve):
                nc.vector.memset(qk_t[:, :, 0:P], 0.0)
                nc.vector.memset(v_t[:, 0, :], 0.0)
                nc.vector.memset(q_zero_t[:], 0.0).then_inc(dil_zeroed, 1)

        def evac_tqk(act, t, j, count, res):
            for u in range(2):
                act.wait_ge(unit_done, count(u))
                nc.scalar.copy(qk_t[:, bass.ds(2 * t + u, 1), P:P + LAT], res[u][:, 0:1, :]).then_inc(unit_free, 1)

        def value_units(t):
            return [("T", slice(b * P, (b + 1) * P) if t == 0 else slice(b, LAT, 4), 0, 256) for b in range(4)]

        weights = ExitStack()
        share_weight_buffers(weights)
        linear("tqk", t_hi, t_lo, feature_units(ONLY_LAT), evac_tqk, ahead=True)
        linear("tv", t_hi, t_lo, value_units, copy_token_units(v_t, 4, 1))
        weights.close()

        def strided(first):
            return bass.ds(first, P, 4)

        def dilated_head(h):
            g, c = h // 4, h // 2
            cols64 = slice(64 * h, 64 * h + 64)

            def keys(i):
                if g == 0:
                    return [(0, 2 * P, qk_t[:, WC + c, bass.ds(i * P, 2 * P)],
                             near[:, bass.ds(i, 1), :].rearrange("p o n -> p (o n)"))]
                return [(0, P, qk_t[:, WC + c, strided(i + P)], dil[:, g - 1, :])]

            def values(i):
                return [v_t[:, bass.ds(i + b, 1), cols64].rearrange("p o n -> p (o n)")
                        for b in ((0, 1) if g == 0 else (1,))]

            return dict(q=q_zero_t[:, h, :], keys=keys, values=values, column=64 * h, sink=None)

        def dilated_queries(i):
            copies = []
            for half in range(2):
                part = slice(64 * half, 64 * half + 64)
                copies += [(q_zero_t[part, half:4:2, :], qk_t[part, 0:2, bass.ds(i * P + P, P)]),
                           (q_zero_t[part, 4 + half:12:2, :], qk_t[part, 2:WC, strided(i + P)])]
            return copies

        def dilated_results(i, p_out):
            out = p_out[:, 0:WC * P].rearrange("p (c n) -> p c n", n=P)
            return [(y_b[:, 0:2, bass.ds(i * P, P)], out[:, 0:2, :]), (y_b[:, 2:WC, strided(i)], out[:, 2:WC, :])]

        attend("dil", 4, [dilated_head(h) for h in range(2 * WC)], dilated_queries, dilated_results,
               2 * P, 2, WC * P, 64.0 ** -0.5, lse)
        dil_scope.close()

        gw = {k: sem("groups_" + k) for k in ("pair", "turned", "logs", "max", "shifted", "exp", "sum", "weights",
                                             "spread")}
        with ExitStack() as scope:
            pair_of = sb(scope, "groups_pair", [P, 2, P])
            logs = sb(scope, "groups_logs", [4, 3, LAT])
            top_log = sb(scope, "groups_top", [4, LAT])
            p_logs = psum(scope, "groups_p_logs", [P, 3, 512])
            p_spread = psum(scope, "groups_p_spread", [P, 5, 512])

            def over_groups(ap):
                return ap.rearrange("p (o n) -> p o n", o=1).broadcast_to([4, 3, LAT])

            with stage_block() as block:
                @block.sync
                def _(sp):
                    sp.dma_start(pair_of[:], io["pair"]).then_inc(gw["pair"], 16)

                @block.tensor
                def _(pe):
                    for g in range(3):
                        for i in range(4):
                            mm = nc.tensor.transpose(p_logs[0:4, g, i * P:(i + 1) * P], lse[:, i, 4 * g:4 * g + 4],
                                                     ident[:])
                    mm.then_inc(gw["turned"], 1)
                    pe.wait_ge(gw["pair"], 16)
                    pe.wait_ge(gw["weights"], 1)
                    for c in range(WC):
                        if c == 5:
                            pe.wait_ge(gw["spread"], 1)
                        nc.tensor.matmul(p_spread[:, c % 5, :], pair_of[0:4, c % 2, :], logs[:, c // 2, :],
                                         start=True, stop=True).then_inc(gw["turned"], 1)

                @block.scalar
                def _(act):
                    act.wait_ge(gw["shifted"], 1)
                    nc.scalar.activation(logs[:], logs[:], ACT.Exp).then_inc(gw["exp"], 1)

                @block.vector
                def _(dve):
                    dve.wait_ge(gw["turned"], 1)
                    nc.vector.tensor_copy(logs[:, 0, :], p_logs[0:4, 0, :])
                    nc.vector.tensor_copy(logs[:, 1:3, :].rearrange("p g (n r) -> p g r n", r=4),
                                          p_logs[0:4, 1:3, :].rearrange("p g (r n) -> p g r n", r=4))\
                        .then_inc(gw["logs"], 1)
                    dve.wait_ge(gw["logs"], 1)
                    nc.vector.tensor_tensor(top_log[:], logs[:, 0, :], logs[:, 1, :], ALU.max).then_inc(gw["max"], 1)
                    dve.wait_ge(gw["max"], 1)
                    nc.vector.tensor_tensor(top_log[:], top_log[:], logs[:, 2, :], ALU.max).then_inc(gw["max"], 1)
                    dve.wait_ge(gw["max"], 2)
                    nc.vector.tensor_tensor(logs[:], logs[:], over_groups(top_log[:]), ALU.subtract)\
                        .then_inc(gw["shifted"], 1)
                    dve.wait_ge(gw["exp"], 1)
                    nc.vector.tensor_tensor(top_log[:], logs[:, 0, :], logs[:, 1, :], ALU.add).then_inc(gw["sum"], 1)
                    dve.wait_ge(gw["sum"], 1)
                    nc.vector.tensor_tensor(top_log[:], top_log[:], logs[:, 2, :], ALU.add).then_inc(gw["sum"], 1)
                    dve.wait_ge(gw["sum"], 2)
                    nc.vector.reciprocal(top_log[:], top_log[:]).then_inc(gw["sum"], 1)
                    dve.wait_ge(gw["sum"], 3)
                    nc.vector.tensor_tensor(logs[:], logs[:], over_groups(top_log[:]), ALU.mult)\
                        .then_inc(gw["weights"], 1)
                    for c in range(WC):
                        dve.wait_ge(gw["turned"], c + 2)
                        nc.vector.tensor_tensor(y_b[:, c, :], y_b[:, c, :], p_spread[:, c % 5, :], ALU.mult)\
                            .then_inc(gw["spread"], 1)

        weights = ExitStack()
        share_weight_buffers(weights)
        gate_linear("tz", t_hi, t_lo, y_b, ACT.Silu, ahead=True)

        merge = ExitStack()
        y_proj = sb(merge, "y_b_projected", [P, DC, LAT])
        with ExitStack() as scope:
            m_hi = sb(scope, "dilated_hi", [P, WC, LAT], F32R)
            m_lo = sb(scope, "dilated_lo", [P, WC, LAT], F32R)
            dilated_cut = cut(y_b, m_hi, m_lo, WC)
            linear("pb", m_hi, m_lo, feature_units(ONLY_LAT), copy_units(y_proj, 0), source=dilated_cut, ahead=True)
        gate_linear("gb", t_hi, t_lo, y_proj, ACT.Sigmoid, y_a, ahead=True)
        merge.close()
        with ExitStack() as scope:
            m_hi = sb(scope, "merged_hi", [P, DC, LAT], F32R)
            m_lo = sb(scope, "merged_lo", [P, DC, LAT], F32R)
            merged_cut = cut(y_a, m_hi, m_lo, DC)
            linear("wo", m_hi, m_lo, feature_units(ONLY_LAT), None, add_residual(ONLY_LAT, [ada[:, 16:24]], 2),
                   merged_cut)
        weights.close()
        two.close()
        chunk_ready = sem("final_chunk_ready")
        final = head_norm("final", 1, DC, LAT, lambda h, j: x_lat[:, j, :], lambda j: cols("final_w")[:, j:j + 1],
                          within=True, each=chunk_ready)
        with ExitStack() as scope:
            made = final(scope)
            with stage_block() as block:
                @block.sync
                def _(sp):
                    for c in range(0, DC, 2):
                        if c < DC - 2:
                            sp.wait_ge(chunk_ready, c + 2)
                        else:
                            sp.wait_ge(head_norm_sem["scaled"], 1)
                        sp.dma_start(io["y"][:, c:c + 2, :], x_lat[:, c:c + 2, :]).then_inc(stored, 16)
                    sp.wait_ge(stored, 16 * DC // 2)

                @block.scalar
                def _(act):
                    made["act"](act)

                @block.tensor
                def _(pe):
                    made["pe"](pe)

                @block.vector
                def _(dve):
                    made["dve"](dve)


def layout(inp):
    f = {k: np.asarray(v) for k, v in inp.items()}

    def fm(a):
        return np.ascontiguousarray(a.reshape(a.shape[0] // P, P, -1).transpose(1, 0, 2))

    def col(a):
        return a.reshape(-1, P).T

    def rows(a):
        return np.broadcast_to(a.reshape(1, -1), (P, a.size))

    def tiles(w, nt=256):
        k, n = w.shape
        w = w.reshape(k // P, P, n // nt, nt).transpose(2, 1, 0, 3)
        return np.ascontiguousarray(w).reshape(n // nt, P, -1)

    out = dict(constants())
    out["x"] = fm(f["x"][0].T)
    out["ctx"] = fm(f["ctx"][0].T)
    parts = dict(
        mod_b=col(f["mod_b"].reshape(-1)), ada_b=col(f["ada_b_2"][0]), norm_g=col(f["norm_g"].reshape(-1)),
        norm_w=col(f["norm_w_2"][0]), final_w=col(f["final_norm_w_2"]),
        qk_g=np.tile(f["attn_qk_norm_g"][0].T, (2, 1)), sink=rows(f["attn_sink"][0]),
        lb=col(f["hgrn_lb"].reshape(-1)), hgrn_g=f["hgrn_out_norm_g"][0].reshape(P, 1),
        conv=f["conv_w_2"][0].reshape(4, 24, P).transpose(2, 1, 0).reshape(P, 96),
        a_log=rows(f["a_log_2"][0]), dt_bias=rows(f["dt_bias_2"][0]), dn_w=f["dn_norm_w_2"][0].reshape(P, 1),
        cond=np.concatenate([col(f["c"][0]), col(f["c_ctx"])], 1), cond_2=col(f["c_2"][0]),
        eps=np.full((P, 1), EPS, np.float32))
    out["small"] = np.concatenate([parts[k] for k in SMALL], axis=1)

    out["w_mod"] = np.concatenate([tiles(f["mod_w"][0]), tiles(f["mod_w"][1]), tiles(f["ada_w_2"][0])])
    w = f["even_w_in"][0]
    wq = w[:, 0:512].reshape(D, 2, 4, 64).transpose(0, 2, 1, 3).reshape(D, 512)
    out["w_aq"], out["w_akv"] = tiles(wq), tiles(w[:, 512:768])
    out["w_bq"], out["w_bf"] = tiles(w[:, 768:1280]), tiles(w[:, 1280:2304])
    out["w_bi"], out["w_bg"] = tiles(w[:, 2304:2816]), tiles(w[:, 2816:3328])
    w = f["even_w_out"][0]
    wa = w[0:512].reshape(2, 4, 64, D).transpose(1, 0, 2, 3).reshape(512, D)
    out["w_eo"] = tiles(np.concatenate([wa, w[512:]], axis=0))
    for layer in (0, 1):
        w = f["ffn_w_in"][layer].reshape(DC, P, 2, FFN // P, P).transpose(3, 1, 0, 2, 4)
        w = np.ascontiguousarray(w).reshape(FFN // P, P, -1)
        wo = f["ffn_w_out"][layer].reshape(2, HALF * P, D)
        for half in (0, 1):
            out[f"w_f{layer}i{half}"] = w[half * HALF:(half + 1) * HALF]
            out[f"w_f{layer}o{half}"] = tiles(wo[half], P)
    w = f["odd_w_in"][0]
    out["w_rqk"], out["w_rv"] = tiles(w[:, 0:2048]), tiles(w[:, 2048:4096])
    wg = w[:, 4096:].reshape(D, RET_H, 2, 256).transpose(0, 2, 1, 3).reshape(D, 2048)
    out["w_rg"] = tiles(wg)
    wo = f["odd_w_out"][0].reshape(RET_H, 2, 256, D).transpose(1, 0, 2, 3).reshape(2048, D)
    out["w_ro"] = tiles(wo, P)
    w = f["w_in_2"][0]
    out["w_dqkv"], out["w_dz"], out["w_dba"] = tiles(w[:, 0:3072]), tiles(w[:, 3072:4096]), tiles(w[:, 4096:4112], 16)
    out["w_tqk"], out["w_tv"], out["w_tz"] = tiles(w[:, 4112:5648]), tiles(w[:, 5648:6416]), tiles(w[:, 6416:7184])
    out["w_ga"], out["w_gb"] = tiles(w[:, 7184:8208]), tiles(w[:, 8208:9232])
    out["w_pa"], out["w_pb"], out["w_wo"] = tiles(f["w_proj_a_2"][0]), tiles(f["w_proj_b_2"][0]), tiles(f["w_out_2"][0])
    return out


def kernel(**inputs):
    import concourse.bacc as bacc
    from concourse.bass_utils import run_bass_kernel_spmd

    nc = bacc.Bacc("TRN2", target_bir_lowering=False, num_devices=1)
    arrays = {"in_" + k: np.ascontiguousarray(a) for k, a in layout(inputs).items()}
    io = {k[3:]: nc.dram_tensor(k, a.shape, mybir.dt.from_np(a.dtype), kind="ExternalInput").ap()
          for k, a in arrays.items()}
    io["y"] = nc.dram_tensor("y", (P, DC, LAT), F32, kind="ExternalOutput").ap()
    program(nc, io)
    got = run_bass_kernel_spmd(nc, [arrays], core_ids=[0]).results[0]["y"]
    return np.ascontiguousarray(got.transpose(2, 1, 0).reshape(1, LAT, D))
```
